# Optimizing a Trainium2 kernel written in Bass

```python
import math
import jax
import jax.numpy as jnp
from jax import lax
import numpy as np

D_MODEL = 2048
BATCH = 1
SEQ = 256
DEPTH = 1
DEC_BATCH = 8
DEC_SEQ = 8
PAST_LEN = 256
PAGE_SIZE = 128

GLA_HEADS = 4
GLA_DK = 128
GLA_DV = 256
GLA_GATE_RANK = 16
GLA_TAU = 16.0
GLA_CHUNK = 64
GLA_WIDTH = GLA_HEADS * GLA_DV
NSA_HEADS = 16
NSA_KV = 4
NSA_GROUP = NSA_HEADS // NSA_KV
NSA_HD = 64
NSA_WIDTH = NSA_HEADS * NSA_HD
CMP_LEN = 32
CMP_STRIDE = 16
CMP_HIDDEN = 2 * NSA_HD
SEL_LEN = 64
SEL_TOPN = 16
WINDOW = 512
Q_BLOCK = 128
ROPE_THETA = 10000.0
MIX_WIDTH = GLA_WIDTH + NSA_WIDTH
D_FF = 5632
LN_EPS = 1e-5
ALPHA = (2.0 * DEPTH) ** 0.25
BETA = (8.0 * DEPTH) ** -0.25
NEG = -1e30

SPLIT_SIZES = (GLA_HEADS * GLA_DK, GLA_HEADS * GLA_DK, GLA_WIDTH, GLA_GATE_RANK, GLA_WIDTH,
               NSA_WIDTH, NSA_KV * NSA_HD, NSA_KV * NSA_HD, NSA_KV * NSA_HD, NSA_KV * NSA_HD,
               NSA_KV * NSA_HD, NSA_KV * NSA_HD, NSA_HEADS * 3)
SPLIT_IS_VALUE = (False, False, True, False, False, False, False, True, False, True, False, True, False)
IN_WIDTH = sum(SPLIT_SIZES)
SPLIT_POINTS = tuple(int(p) for p in np.cumsum(SPLIT_SIZES)[:-1])

kernel_name = 'gla_nsa_hybrid_decode_step'

def layer_norm(x, g, b):
    xf = x.astype(jnp.float32)
    mu = jnp.mean(xf, -1, keepdims=True)
    var = jnp.mean(jnp.square(xf - mu), -1, keepdims=True)
    return ((xf - mu) * lax.rsqrt(var + LN_EPS) * g + b).astype(x.dtype)

def head_rms_norm(o, g):
    of = o.astype(jnp.float32)
    return of * lax.rsqrt(jnp.mean(of * of, -1, keepdims=True) + LN_EPS) * g

def swiglu(x, w_in, w_out):
    gate, up = jnp.split(x @ w_in, 2, axis=-1)
    return (jax.nn.silu(gate) * up) @ w_out

def rope(x, pos):
    half = x.shape[-1] // 2
    freq = ROPE_THETA ** (-jnp.arange(half, dtype=jnp.float32) / half)
    ang = pos.astype(jnp.float32)[:, None] * freq[None, :]
    cos = jnp.cos(ang)[None, :, None, :]
    sin = jnp.sin(ang)[None, :, None, :]
    x1 = x[..., :half].astype(jnp.float32)
    x2 = x[..., half:].astype(jnp.float32)
    return jnp.concatenate([x1 * cos - x2 * sin, x2 * cos + x1 * sin], -1).astype(x.dtype)

def gla_chunked(q, k, v, log_a, s0):
    B, T, H, DK = q.shape
    DV = v.shape[-1]
    C = math.gcd(T, GLA_CHUNK)
    n = T // C
    f32 = jnp.float32

    def to_chunks(a):
        return a.astype(f32).reshape(B, n, C, H, a.shape[-1]).transpose(1, 0, 3, 2, 4)

    xs = (to_chunks(q * (DK ** -0.5)), to_chunks(k), to_chunks(v), to_chunks(log_a))
    causal = jnp.tril(jnp.ones((C, C), bool))[None, None, :, :, None]

    def step(S, inp):
        qi, ki, vi, ai = inp
        b = jnp.cumsum(ai, axis=2)
        diff = b[:, :, :, None, :] - b[:, :, None, :, :]
        decay = jnp.exp(jnp.where(causal, diff, -jnp.inf))
        attn = jnp.einsum('bhik,bhijk,bhjk->bhij', qi, decay, ki)
        o = jnp.einsum('bhij,bhjv->bhiv', attn, vi) + jnp.einsum('bhik,bhkv->bhiv', qi * jnp.exp(b), S)
        b_last = b[:, :, -1:, :]
        S_new = jnp.exp(b_last[:, :, 0, :])[..., None] * S + jnp.einsum('bhjk,bhjv->bhkv', ki * jnp.exp(b_last - b), vi)
        return S_new, o

    S_fin, o = lax.scan(step, s0.astype(f32), xs)
    o = o.transpose(1, 0, 3, 2, 4).reshape(B, T, H, DV)
    return o, S_fin.astype(s0.dtype)

def compress(rows, pos_emb, w1, w2):
    B, L, KV, HD = rows.shape
    n_cmp = (L - CMP_LEN) // CMP_STRIDE + 1
    idx = np.arange(n_cmp)[:, None] * CMP_STRIDE + np.arange(CMP_LEN)[None, :]
    blocks = rows[:, idx] + pos_emb[:, None, :].astype(rows.dtype)
    flat = blocks.transpose(0, 1, 3, 2, 4).reshape(B, n_cmp, KV, CMP_LEN * HD)
    return jax.nn.gelu(flat @ w1) @ w2

def cmp_attention(q, kc, vc, qpos):
    N = kc.shape[1]
    s = jnp.einsum('btkgd,bnkd->btkgn', q, kc).astype(jnp.float32) * (NSA_HD ** -0.5)
    end = jnp.asarray(np.arange(N) * CMP_STRIDE + CMP_LEN - 1)
    valid = (end[None, :] <= qpos[:, None])[None, :, None, None, :]
    p = jax.nn.softmax(jnp.where(valid, s, NEG), axis=-1) * valid
    o = jnp.einsum('btkgn,bnkd->btkgd', p.astype(vc.dtype), vc)
    return o, p

def select_blocks(p_cmp, qpos, n_sel):
    N = p_cmp.shape[-1]
    cs = np.arange(N) * CMP_STRIDE
    ss = np.arange(n_sel) * SEL_LEN
    overlap = ((cs[:, None] < ss[None, :] + SEL_LEN) & (cs[:, None] + CMP_LEN > ss[None, :])).astype(np.float32)
    imp = jnp.einsum('btkgn,ns->btks', p_cmp, jnp.asarray(overlap))
    ssj = jnp.asarray(ss)[None, :]
    cur = (qpos[:, None] // SEL_LEN) * SEL_LEN
    start_ok = ssj <= qpos[:, None]
    forced = (ssj == 0) | (ssj == cur) | (ssj == cur - SEL_LEN)
    score = jnp.where(start_ok[None, :, None, :], jnp.where(forced[None, :, None, :], 1e9, imp), -1e9)
    val, idx = lax.top_k(score, min(SEL_TOPN, n_sel))
    return idx, val > -1e8

def sel_attention_item(q, qpos, idx, ok, kblk, vblk):
    Tq = q.shape[0]
    kv_ar = jnp.arange(NSA_KV)[None, :, None]
    kg = kblk[kv_ar, idx]
    vg = vblk[kv_ar, idx]
    s = jnp.einsum('tkgd,tkjsd->tkgjs', q, kg).astype(jnp.float32) * (NSA_HD ** -0.5)
    kpos = idx[..., None] * SEL_LEN + jnp.arange(SEL_LEN)
    valid = (ok[..., None] & (kpos <= qpos[:, None, None, None]))[:, :, None]
    s = jnp.where(valid, s, NEG)
    p = jax.nn.softmax(s.reshape(Tq, NSA_KV, NSA_GROUP, -1), axis=-1).reshape(s.shape)
    return jnp.einsum('tkgjs,tkjsd->tkgd', p.astype(vg.dtype), vg)

def sel_attention(q, qpos, idx, ok, k_rows, v_rows, n_sel):
    B, T = q.shape[:2]
    L = k_rows.shape[1]
    pad = n_sel * SEL_LEN - L

    def blocks(r):
        r = jnp.pad(r, ((0, 0), (0, pad), (0, 0), (0, 0)))
        return r.reshape(B, n_sel, SEL_LEN, NSA_KV, NSA_HD).transpose(0, 3, 1, 2, 4)

    kb, vb = blocks(k_rows), blocks(v_rows)
    qb = math.gcd(T, Q_BLOCK)
    nb = T // qb

    def items(a):
        return a.reshape(B * nb, qb, *a.shape[2:])

    b_id = jnp.repeat(jnp.arange(B), nb)
    qpos_items = jnp.tile(qpos.reshape(nb, qb), (B, 1))

    def fn(args):
        qi, pi, ii, oi, bi = args
        return sel_attention_item(qi, pi, ii, oi, kb[bi], vb[bi])

    o = lax.map(fn, (items(q), qpos_items, items(idx), items(ok), b_id))
    return o.reshape(B, T, NSA_KV, NSA_GROUP, NSA_HD)

def window_attention(q, qpos, k_full, v_full, kpos_full):
    B, T = q.shape[:2]
    qb = math.gcd(T, Q_BLOCK)
    nb = T // qb
    band = np.arange(nb)[:, None] * qb + np.arange(WINDOW + qb)[None, :]
    kb, vb, kp = k_full[:, band], v_full[:, band], kpos_full[band]
    qq = q.reshape(B, nb, qb, NSA_KV, NSA_GROUP, NSA_HD)
    qp = qpos.reshape(nb, qb)
    s = jnp.einsum('bnqkgd,bnskd->bnqkgs', qq, kb).astype(jnp.float32) * (NSA_HD ** -0.5)
    dist = qp[:, :, None] - kp[:, None, :]
    valid = ((kp[:, None, :] >= 0) & (dist >= 0) & (dist < WINDOW))[None, :, :, None, None, :]
    p = jax.nn.softmax(jnp.where(valid, s, NEG), axis=-1)
    o = jnp.einsum('bnqkgs,bnskd->bnqkgd', p.astype(vb.dtype), vb)
    return o.reshape(B, T, NSA_KV, NSA_GROUP, NSA_HD)

def token_mixing(h, qpos, past_cmp, past_slc, win_prefix, win_prefix_pos, gla_s0, w_buf,
                 w_in, w_gla_gate2, b_gla_gate2, gla_norm_g, cmp_pos, cmp_w1, cmp_w2, w_out):
    B, T, _ = h.shape
    f32 = jnp.float32
    (gq, gk, gv, ga, gr, nq, kc, vc, ks, vs, kw, vw, ng) = jnp.split(h @ w_in, SPLIT_POINTS, axis=-1)

    def heads(a, n):
        return a.reshape(B, T, n, -1)

    log_a = jax.nn.log_sigmoid((ga @ w_gla_gate2 + b_gla_gate2).astype(f32)) / GLA_TAU
    o_g, gla_s = gla_chunked(heads(gq, GLA_HEADS), heads(gk, GLA_HEADS), heads(gv, GLA_HEADS),
                             heads(log_a, GLA_HEADS), gla_s0)
    o_g = head_rms_norm(o_g, gla_norm_g) * jax.nn.silu(heads(gr, GLA_HEADS).astype(f32))

    q = rope(heads(nq, NSA_HEADS), qpos).reshape(B, T, NSA_KV, NSA_GROUP, NSA_HD)
    cmp_rows = jnp.stack([rope(heads(kc, NSA_KV), qpos), heads(vc, NSA_KV)], axis=2)
    slc_rows = jnp.stack([rope(heads(ks, NSA_KV), qpos), heads(vs, NSA_KV)], axis=2)
    win_rows = jnp.stack([rope(heads(kw, NSA_KV), qpos), heads(vw, NSA_KV)], axis=2)
    cmp_all = cmp_rows if past_cmp is None else jnp.concatenate([past_cmp, cmp_rows], axis=1)
    slc_all = slc_rows if past_slc is None else jnp.concatenate([past_slc, slc_rows], axis=1)

    k_cmp = compress(cmp_all[:, :, 0], cmp_pos[0], cmp_w1[0], cmp_w2[0])
    v_cmp = compress(cmp_all[:, :, 1], cmp_pos[1], cmp_w1[1], cmp_w2[1])
    o_c, p_c = cmp_attention(q, k_cmp, v_cmp, qpos)

    n_sel = -(-slc_all.shape[1] // SEL_LEN)
    idx, ok = select_blocks(p_c, qpos, n_sel)
    o_s = sel_attention(q, qpos, idx, ok, slc_all[:, :, 0], slc_all[:, :, 1], n_sel)

    win_all = jnp.concatenate([win_prefix.astype(win_rows.dtype), win_rows], axis=1)
    win_pos = jnp.concatenate([win_prefix_pos, qpos])
    o_w = window_attention(q, qpos, win_all[:, :, 0], win_all[:, :, 1], win_pos)

    g = jax.nn.sigmoid(ng.reshape(B, T, NSA_KV, NSA_GROUP, 3).astype(f32))
    o_n = g[..., 0:1] * o_c + g[..., 1:2] * o_s + g[..., 2:3] * o_w

    mix = jnp.concatenate([o_g.reshape(B, T, GLA_WIDTH), o_n.reshape(B, T, NSA_WIDTH)], axis=-1).astype(h.dtype)
    return mix @ w_out, cmp_rows, slc_rows, win_all[:, -w_buf:], gla_s

def decoder_layer(x, qpos, past_cmp, past_slc, win_prefix, win_prefix_pos, gla_s0, w_buf,
                  w_ffn1_in, w_ffn1_out, w_in, w_gla_gate2, b_gla_gate2, gla_norm_g,
                  cmp_pos, cmp_w1, cmp_w2, w_out, w_ffn2_in, w_ffn2_out, ln_g, ln_b):
    x = layer_norm(ALPHA * x + 0.5 * swiglu(x, w_ffn1_in, w_ffn1_out), ln_g[0], ln_b[0])
    m, cmp_rows, slc_rows, win_buf, gla_s = token_mixing(
        x, qpos, past_cmp, past_slc, win_prefix, win_prefix_pos, gla_s0, w_buf,
        w_in, w_gla_gate2, b_gla_gate2, gla_norm_g, cmp_pos, cmp_w1, cmp_w2, w_out)
    x = layer_norm(ALPHA * x + m, ln_g[1], ln_b[1])
    x = layer_norm(ALPHA * x + 0.5 * swiglu(x, w_ffn2_in, w_ffn2_out), ln_g[2], ln_b[2])
    return x, cmp_rows, slc_rows, win_buf, gla_s

def gather_pages(pool, page_table):
    db, n_pages = page_table.shape
    return pool[page_table].reshape(db, n_pages * PAGE_SIZE, *pool.shape[2:])

def setup_inputs(seed: int = 0) -> dict:
    key = jax.random.key(seed)
    k = jax.random.split(key, 24)
    f32 = jnp.float32
    n_pages = PAST_LEN // PAGE_SIZE
    n_pool = (DEC_BATCH * n_pages * 5) // 4
    w_buf = min(WINDOW, PAST_LEN)

    def nrm(kk, shape, scale):
        return jax.random.normal(kk, shape, f32) * scale

    col_scale = jnp.asarray(np.concatenate(
        [np.full((n,), BETA if is_v else 1.0, np.float32) for n, is_v in zip(SPLIT_SIZES, SPLIT_IS_VALUE)]))
    page_table = jax.random.permutation(k[6], n_pool)[: DEC_BATCH * n_pages].reshape(DEC_BATCH, n_pages).astype(jnp.int32)
    return {
        'x_prompt': nrm(k[0], (BATCH, SEQ, D_MODEL), 1.0),
        'x_sample': nrm(k[1], (DEC_BATCH, DEC_SEQ, D_MODEL), 1.0),
        'cache_cmp_kv': nrm(k[2], (DEPTH, n_pool, PAGE_SIZE, 2, NSA_KV, NSA_HD), 1.0),
        'cache_slc_kv': nrm(k[3], (DEPTH, n_pool, PAGE_SIZE, 2, NSA_KV, NSA_HD), 1.0),
        'cache_win_kv': nrm(k[4], (DEPTH, DEC_BATCH, w_buf, 2, NSA_KV, NSA_HD), 1.0),
        'state_gla': nrm(k[5], (DEPTH, DEC_BATCH, GLA_HEADS, GLA_DK, GLA_DV), 0.5),
        'page_table': page_table,
        'w_ffn1_in': nrm(k[7], (DEPTH, D_MODEL, 2 * D_FF), BETA * D_MODEL ** -0.5),
        'w_ffn1_out': nrm(k[8], (DEPTH, D_FF, D_MODEL), BETA * D_FF ** -0.5),
        'w_in': nrm(k[9], (DEPTH, D_MODEL, IN_WIDTH), D_MODEL ** -0.5) * col_scale,
        'w_gla_gate2': nrm(k[10], (DEPTH, GLA_GATE_RANK, GLA_HEADS * GLA_DK), GLA_GATE_RANK ** -0.5),
        'b_gla_gate2': nrm(k[11], (DEPTH, GLA_HEADS * GLA_DK), 0.1),
        'gla_norm_g': 1.0 + nrm(k[12], (DEPTH, GLA_DV), 0.01),
        'cmp_pos': nrm(k[13], (DEPTH, 2, CMP_LEN, NSA_HD), 0.02),
        'cmp_w1': nrm(k[14], (DEPTH, 2, CMP_LEN * NSA_HD, CMP_HIDDEN), (CMP_LEN * NSA_HD) ** -0.5),
        'cmp_w2': nrm(k[15], (DEPTH, 2, CMP_HIDDEN, NSA_HD), CMP_HIDDEN ** -0.5),
        'w_out': nrm(k[16], (DEPTH, MIX_WIDTH, D_MODEL), BETA * MIX_WIDTH ** -0.5),
        'w_ffn2_in': nrm(k[17], (DEPTH, D_MODEL, 2 * D_FF), BETA * D_MODEL ** -0.5),
        'w_ffn2_out': nrm(k[18], (DEPTH, D_FF, D_MODEL), BETA * D_FF ** -0.5),
        'ln_g': 1.0 + nrm(k[19], (DEPTH, 3, D_MODEL), 0.01),
        'ln_b': nrm(k[20], (DEPTH, 3, D_MODEL), 0.01),
    }

def reference(x_prompt, x_sample, cache_cmp_kv, cache_slc_kv, cache_win_kv, state_gla, page_table,
              w_ffn1_in, w_ffn1_out, w_in, w_gla_gate2, b_gla_gate2, gla_norm_g,
              cmp_pos, cmp_w1, cmp_w2, w_out, w_ffn2_in, w_ffn2_out, ln_g, ln_b):
    B, T = x_prompt.shape[:2]
    DB, TS = x_sample.shape[:2]
    past_len = page_table.shape[1] * PAGE_SIZE
    w_buf = cache_win_kv.shape[2]
    qpos_p = jnp.arange(T, dtype=jnp.int32)
    qpos_s = past_len + jnp.arange(TS, dtype=jnp.int32)
    pref_pos_p = jnp.arange(-WINDOW, 0, dtype=jnp.int32)
    pref_pos_s = jnp.concatenate([jnp.full((WINDOW - w_buf,), -1, jnp.int32),
                                  past_len - w_buf + jnp.arange(w_buf, dtype=jnp.int32)])
    win_pref_p = jnp.zeros((B, WINDOW, 2, NSA_KV, NSA_HD), x_prompt.dtype)
    gla_zero = jnp.zeros((B, GLA_HEADS, GLA_DK, GLA_DV), x_prompt.dtype)

    hp, hs = x_prompt, x_sample
    cmp_p, slc_p, win_p, gla_p = [], [], [], []
    cmp_s, slc_s, win_s, gla_s = [], [], [], []
    for l in range(DEPTH):
        weights = (w_ffn1_in[l], w_ffn1_out[l], w_in[l], w_gla_gate2[l], b_gla_gate2[l], gla_norm_g[l],
                   cmp_pos[l], cmp_w1[l], cmp_w2[l], w_out[l], w_ffn2_in[l], w_ffn2_out[l], ln_g[l], ln_b[l])
        hp, c_r, s_r, w_b, g_s = decoder_layer(hp, qpos_p, None, None, win_pref_p, pref_pos_p, gla_zero, w_buf, *weights)
        cmp_p.append(c_r); slc_p.append(s_r); win_p.append(w_b); gla_p.append(g_s)
        past_cmp = gather_pages(cache_cmp_kv[l], page_table)
        past_slc = gather_pages(cache_slc_kv[l], page_table)
        win_pref_s = jnp.pad(cache_win_kv[l], ((0, 0), (WINDOW - w_buf, 0), (0, 0), (0, 0), (0, 0)))
        hs, c_r, s_r, w_b, g_s = decoder_layer(hs, qpos_s, past_cmp, past_slc, win_pref_s, pref_pos_s, state_gla[l], w_buf, *weights)
        cmp_s.append(c_r); slc_s.append(s_r); win_s.append(w_b); gla_s.append(g_s)

    return (hp, hs,
            jnp.stack(cmp_p), jnp.stack(slc_p), jnp.stack(win_p), jnp.stack(gla_p),
            jnp.stack(cmp_s), jnp.stack(slc_s), jnp.stack(win_s), jnp.stack(gla_s))


_drawn_inputs = setup_inputs


def setup_inputs(seed=0):
    import zlib

    import numpy as np

    out = dict(_drawn_inputs(seed))
    spreads = {}
    factors = {'cache_slc_kv': 12.586,
     'gla_norm_g': 200.0,
     'cmp_pos': 200.0,
     'ln_g': 3.201,
     'ln_b': 3.111,
     'cache_cmp_kv': 19.801,
     'cmp_w1': 3.488,
     'cmp_w2': 2.896}
    for name, (base, spread) in spreads.items():
        noise = np.random.default_rng([zlib.crc32(name.encode()), seed]).standard_normal(out[name].shape)
        drawn = base * np.exp(spread * noise) if base else spread * noise
        out[name] = jnp.asarray(drawn.astype(out[name].dtype))
    for name, factor in factors.items():
        out[name] = (out[name] * factor).astype(out[name].dtype)
    return out
```

```python
from contextlib import ExitStack

import numpy as np
import concourse.bass as bass
from concourse import mybir
from concourse.alu_op_type import AluOpType as ALU

ACT = mybir.ActivationFunctionType
F32 = mybir.dt.float32
F32R = mybir.dt.float32r
U8 = mybir.dt.uint8
I32 = mybir.dt.int32
AX = mybir.AxisListType

P = 128
D = 2048
KD = D // P
TP, NB, TS = 256, 8, 8
T = TP + NB * TS
PAST, PAGE = 256, 128
NPG = PAST // PAGE
D_FF = 5632
FT = D_FF // P
FC = 11
CH = FT // FC
GH, DV = 4, 256
NH, KV, G, HD = 16, 4, 4, 64
CL, CS = 32, 16
NC = (TP - CL) // CS + 1
assert NC == (PAST + TS - CL) // CS + 1 and (NC - 1) * CS + CL <= PAST
SEL_LEN, SEL_TOPN, WINDOW = 64, 16, 512
assert -(-(PAST + TS) // SEL_LEN) <= SEL_TOPN and TP // SEL_LEN <= SEL_TOPN
assert PAST + TS <= WINDOW
ALPHA = 2.0 ** 0.25
EPS = 1e-5
NEG = -1e30
FLOOR = -5e29
LEVELS = 8
GW = PAST + 16
C_GA, C_GR, C_NQ, C_KV, C_NG = 2048, 2064, 3088, 4112, 5648
T_GQ, T_GK, T_GV, T_GR, T_NQ, T_KV, NT = 0, 4, 8, 16, 24, 32, 44
T_OG = 0
K_ID, K_MEAN, K_RMS, K_ROT, K_COS, K_SIN = 0, 128, 256, 384, 512, 832
K_RESET, K_CAUSAL, K_CMP, K_NEW, K_SEQ = 1152, 1472, 1984, 2016, 2064
K_ALL = 2072


def constants():
    c = np.zeros((P, K_ALL), np.float32)
    c[:, K_ID:K_ID + P] = np.eye(P)
    c[:, K_MEAN:K_MEAN + P] = 1.0 / D
    c[:, K_RMS:K_RMS + P] = 1.0 / DV
    half = HD // 2
    for m in range(P):
        if m % HD < half:
            c[m + half, K_ROT + m] = -1.0
        else:
            c[m - half, K_ROT + m] = 1.0
    pos = np.concatenate([np.arange(TP), np.tile(PAST + np.arange(TS), NB)]).astype(np.float32)
    freq = np.float32(10000.0) ** (-np.arange(half, dtype=np.float32) / np.float32(half))
    ang = (freq.astype(np.float32)[np.arange(P) % half][:, None] * pos[None, :]).astype(np.float32)
    c[:, K_COS:K_COS + T] = np.cos(ang)
    c[:, K_SIN:K_SIN + T] = np.sin(ang)
    c[:, K_RESET:K_RESET + T] = 1.0
    c[:, K_RESET] = 0.0
    c[:, K_RESET + TP:K_RESET + T:TS] = 0.0
    i = np.arange(P)[:, None]
    for qt in range(2):
        j = np.arange(TP)[None, :]
        c[:, K_CAUSAL + qt * TP:K_CAUSAL + (qt + 1) * TP] = np.where(j <= i + qt * P, 0.0, NEG)
        n = np.arange(16)[None, :]
        c[:, K_CMP + qt * 16:K_CMP + qt * 16 + 16] = np.where(
            (n < NC) & (n * CS + CL - 1 <= i + qt * P), 0.0, NEG)
    n = np.arange(16)[None, :]
    own = np.where((n >= 8) & (n - 8 <= i % TS), 0.0, NEG)
    c[:, K_NEW:K_NEW + 16] = own
    c[:, K_NEW + 16:K_NEW + 32] = own
    c[:, K_NEW + 32:K_NEW + 48] = np.where(n < NC, 0.0, NEG)
    for b in range(NB):
        c[b * TS:(b + 1) * TS, K_SEQ + b] = 1.0
    return c


def level_masks():
    m = np.zeros((P, LEVELS, T), np.int32)
    for lv in range(LEVELS):
        for i in range(T):
            r = i % P
            for j in range(P if i < TP else T - TP):
                if i >= TP and lv > 3:
                    continue
                s = 1 << lv
                if lv == 0:
                    m[j, 0, i] = j == r
                elif j // s == r // s and j % s < s // 2 <= r % s:
                    m[j, lv, i] = 1
    return m


class Layer:
    pass



def build(nc, A, O):
    ctx = ExitStack()
    with ctx:
        L = Layer()
        L.nc, L.A, L.O, L.ctx = nc, A, O, ctx
        L.scope = ctx

        def sem(name):
            return ctx.enter_context(nc.semaphore(name))

        def sb(name, shape, dt=F32, scope=None):
            return (scope or ctx).enter_context(nc.sbuf_tensor(name, shape, dt))

        L.sem, L.sb = sem, sb
        L.bank = [ctx.enter_context(nc.psum_tensor(f"bank{i}", [P, 512], F32)) for i in range(8)]
        L.cst = sb("cst", [P, K_ALL])
        L.lvl = sb("lvl", [P, LEVELS, T], U8)
        L.ln_g = sb("ln_g", [P, 3, KD])
        L.ln_b = sb("ln_b", [P, 3, KD])
        L.xT = sb("xT", [P, KD, T])
        L.raw = [sb(f"raw{a}", [P, KD * P]) for a in range(2)]
        L.proj = sb("proj", [P, NT, T])
        L.gate = sb("gate", [P, T])
        L.loaded = [sem(f"loaded{a}") for a in range(2)]
        L.mixw_loaded = [sem(f"mixw_loaded{a}") for a in range(2)]
        L.hi = [sem(f"hi{a}") for a in range(2)]
        L.split = [sem(f"split{a}") for a in range(2)]
        L.multiplied = [sem(f"multiplied{a}") for a in range(2)]
        L.taken = [sem(f"taken{a}") for a in range(2)]
        L.added = [sem(f"added{a}") for a in range(2)]
        L.hidden_made = sem("hidden_made")
        L.cst_loaded = sem("cst_loaded")
        L.stored = sem("stored")
        L.n_stored = 0
        L.q = 0
        L.q_own = 0
        L.y = 0
        L.h = 0

        open_operands(L, "before")
        load_inputs(L)
        ffn(L, "ffn1", "w_ffn1_in", "w_ffn1_out")
        layer_norm(L, 0)
        projection(L)
        L.operands.close()
        with ExitStack() as mixing:
            L.kv_tok = sb("kv_tok", [P, 3, 12 * P], scope=mixing)
            L.gate_tok = sb("gate_tok", [P, 3, 48], scope=mixing)
            with ExitStack() as s:
                L.v_gla = sb("v_gla", [P, 3, GH * DV], scope=s)
                turn_projection(L)
                gla(L, s)
            with ExitStack() as s:
                L.k_cmp = sb("k_cmp", [P, NB + 1, 2, 16], scope=s)
                L.v_small = sb("v_small", [16, 3, NB + 1, 256], scope=s)
                L.gate_rows = sb("gate_rows", [P, NB, 3], scope=s)
                with ExitStack() as s2:
                    compress(L, s2)
                with ExitStack() as s2:
                    attention(L, s2)
        open_operands(L, "after")
        mix_projection(L)
        layer_norm(L, 1)
        ffn(L, "ffn2", "w_ffn2_in", "w_ffn2_out")
        L.operands.close()
        layer_norm(L, 2)
        write_outputs(L)


def open_operands(L, when):
    L.operands = ExitStack()
    L.xh = L.sb("xh_" + when, [P, KD, T], F32R, L.operands)
    L.xl = L.sb("xl_" + when, [P, KD, T], F32R, L.operands)
    L.wh = [L.sb(f"wh{a}_{when}", [P, KD * P], F32R, L.operands) for a in range(2)]
    L.wl = [L.sb(f"wl{a}_{when}", [P, KD * P], F32R, L.operands) for a in range(2)]


def load_inputs(L):
    nc, A, bank = L.nc, L.A, L.bank
    scope = ExitStack()
    with scope:
        x_tok = L.proj[:].rearrange("p k t -> p (k t)")[:, 0:3 * D].rearrange("p (t d) -> p t d", t=3)
        x_loaded, turned, hi_made, bank_free = (
            L.sem("x_loaded"), L.sem("x_turned"), L.sem("x_hi_made"), L.sem("x_bank_free"))
        levels = L.proj[:, 24:32].bitcast(I32)
        levels_loaded = L.sem("levels_loaded")
        ident = L.cst[:, K_ID:K_ID + P]
        with nc.Block() as block:
            @block.sync
            def _(sp):
                sp.dma_start(L.cst[:], A["consts"]).then_inc(L.cst_loaded, 16)
                sp.dma_start(x_tok[:, 0:2, :], A["x_prompt"][0].rearrange("(t p) d -> p t d", p=P)
                             ).then_inc(x_loaded, 16)
                sp.dma_start(x_tok[0:T - TP, 2, :], A["x_sample"].rearrange("b t d -> (b t) d")
                             ).then_inc(x_loaded, 16)
                sp.dma_start(levels, A["levels"]).then_inc(levels_loaded, 16)
                with nc.allow_non_contiguous_dma(reason="small vectors, feature-major"):
                    for n in range(3):
                        sp.dma_start(L.ln_g[:, n, :], A["ln_g"][0, n].rearrange("(k p) -> p k", p=P)
                                     ).then_inc(L.cst_loaded, 16)
                        sp.dma_start(L.ln_b[:, n, :], A["ln_b"][0, n].rearrange("(k p) -> p k", p=P)
                                     ).then_inc(L.cst_loaded, 16)
                sp.wait_ge(L.cst_loaded, 7 * 16)

            @block.gpsimd
            def _(pool):
                pool.wait_ge(levels_loaded, 16)
                pool.tensor_copy(L.lvl[:], levels)

            @block.tensor
            def _(pe):
                pe.wait_ge(L.cst_loaded, 7 * 16)
                pe.wait_ge(x_loaded, 32)
                for k in range(KD):
                    if k >= 4:
                        pe.wait_ge(bank_free, k - 3)
                    for t in range(3):
                        n = P if t < 2 else T - TP
                        last = pe.transpose(bank[k % 4][:, t * P:t * P + n],
                                            x_tok[0:n, t, k * P:(k + 1) * P], ident[0:n, 0:n])
                    last.then_inc(turned, 1)

            @block.scalar
            def _(act):
                for k in range(KD):
                    act.wait_ge(turned, k + 1)
                    act.activation(L.xT[:, k], bank[k % 4][:, 0:T], ACT.Copy, scale=ALPHA)
                    act.activation(L.xh[:, k], bank[k % 4][:, 0:T], ACT.Copy).then_inc(hi_made, 1)

            @block.vector
            def _(dve):
                for a in range(2):
                    for s in (L.split[a], L.multiplied[a], L.taken[a], L.added[a]):
                        dve.sem_inc(s, 1)
                dve.sem_inc(L.hidden_made, 1)
                for k in range(KD):
                    dve.wait_ge(hi_made, k + 1)
                    dve.tensor_tensor(L.xl[:, k], bank[k % 4][:, 0:T], L.xh[:, k].bitcast(F32),
                                      ALU.subtract).then_inc(bank_free, 1)


def multiply_unit(L, pe, q, a, nk, moving, first_wait=None):
    out = L.bank[a][:, 0:T]
    pe.wait_ge(L.split[a], q + 2)
    pe.wait_ge(L.taken[a], q + 1)
    hi, lo = moving
    for k in range(nk):
        if first_wait is not None:
            first_wait(k)
        w = slice(k * P, (k + 1) * P)
        pe.matmul(out, L.wh[a][:, w], hi[:, k], start=(k == 0), stop=False)
        pe.matmul(out, L.wh[a][:, w], lo[:, k], start=False, stop=False)
        last = pe.matmul(out, L.wl[a][:, w], hi[:, k], start=False, stop=(k == nk - 1))
    last.then_inc(L.multiplied[a], 1)


def split_pair(L, dve, q, landed, per, own_q, nk):
    n = nk * P
    for a in range(2):
        dve.wait_ge(landed[a], own_q * per + per)
        dve.wait_ge(L.multiplied[a], q + 1)
        dve.tensor_copy(L.wh[a][:, 0:n], L.raw[a][:, 0:n]).then_inc(L.hi[a], 1)
        dve.wait_ge(L.hi[a], q + 1)
        dve.tensor_tensor(L.wl[a][:, 0:n], L.raw[a][:, 0:n], L.wh[a][:, 0:n].bitcast(F32),
                          ALU.subtract).then_inc(L.split[a], 1)


def load_unit(L, sp, q, a, src, nk):
    sp.wait_ge(L.split[a], q + 1)
    sp.dma_start(L.raw[a][:, 0:nk * P].rearrange("p (k n) -> p k n", n=P), src
                 ).then_inc(L.loaded[a], 16)


def ffn(L, name, w_in, w_out):
    nc = L.nc
    wi = L.A[w_in][0].rearrange("(k p) n -> p k n", p=P)
    wo = L.A[w_out][0].rearrange("(c k p) n -> p (c k) n", p=P, k=FC)
    q0, own0, y0, h0 = L.q, L.q_own, L.y, L.h
    per = FC + KD // 2
    scope = ExitStack()
    with scope:
        hh = L.sb(name + "_hh", [P, FC, T], F32R, scope)
        hl = L.sb(name + "_hl", [P, FC, T], F32R, scope)
        gate, up, hid = (L.proj[:, i] for i in range(3))
        part = [L.proj[:, 3 + a] for a in range(2)]
        product, hi_done = L.sem(name + "_product"), L.sem(name + "_hidden_hi")
        with nc.Block() as block:
            @block.sync
            def _(sp):
                with sp.Fori(0, CH) as c:
                    with sp.Fori(0, FC) as f:
                        for a in range(2):
                            load_unit(L, sp, c * per + f + q0, a,
                                      wi[:, :, bass.ds(c * (FC * P) + f * P + a * D_FF, P)], KD)
                    with sp.Fori(0, KD // 2) as n:
                        for a in range(2):
                            load_unit(L, sp, c * per + n + (FC + q0), a,
                                      wo[:, bass.ds(c * FC, FC), bass.ds(n * (2 * P) + a * P, P)], FC)

            @block.vector
            def _(dve):
                with dve.Fori(0, CH) as c:
                    with dve.Fori(0, FC) as f:
                        split_pair(L, dve, c * per + f + q0, L.loaded, 16, c * per + f + own0, KD)
                    with dve.Fori(0, KD // 2) as n:
                        split_pair(L, dve, c * per + n + (FC + q0), L.loaded, 16,
                                   c * per + n + (FC + own0), FC)

            @block.tensor
            def _(pe):
                with pe.Fori(0, CH) as c:
                    with pe.Fori(0, FC) as f:
                        for a in range(2):
                            multiply_unit(L, pe, c * per + f + q0, a, KD, (L.xh, L.xl))

                    def hidden_there(k):
                        if k == 0:
                            pe.wait_ge(L.hidden_made, c * FC + (FC + h0))
                        if k == FC - 1:
                            pe.wait_ge(L.hidden_made, c * FC + (FC + h0 + 1))

                    with pe.Fori(0, KD // 2) as n:
                        for a in range(2):
                            multiply_unit(L, pe, c * per + n + (FC + q0), a, FC, (hh, hl),
                                          hidden_there if a == 0 else None)

            @block.scalar
            def _(act):
                with act.Fori(0, CH) as c:
                    with act.Fori(0, FC) as f:
                        act.wait_ge(L.multiplied[0], c * per + f + (q0 + 2))
                        act.wait_ge(L.hidden_made, c * FC + f + (h0 + 1))
                        act.activation(gate, L.bank[0][:, 0:T], ACT.Silu).then_inc(L.taken[0], 1)
                        act.wait_ge(L.multiplied[1], c * per + f + (q0 + 2))
                        act.activation(up, L.bank[1][:, 0:T], ACT.Copy).then_inc(L.taken[1], 1)
                    with act.Fori(0, KD // 2) as n:
                        take_parts(L, act, part, c * per + n + (FC + q0), c * (KD // 2) + n + y0, 0.5)

            @block.gpsimd
            def _(pool):
                with pool.Fori(0, CH) as c:
                    with pool.Fori(0, FC) as f:
                        pool.wait_ge(L.taken[0], c * per + f + (q0 + 2))
                        pool.wait_ge(L.taken[1], c * per + f + (q0 + 2))
                        pool.tensor_tensor(hid, gate, up, ALU.mult).then_inc(product, 1)
                        pool.wait_ge(product, c * FC + f + 1)
                        pool.tensor_copy(hh[:, bass.ds(f, 1), :], hid.rearrange("p (o t) -> p o t", o=1)
                                         ).then_inc(hi_done, 1)
                        pool.wait_ge(hi_done, c * FC + f + 1)
                        pool.tensor_tensor(hl[:, bass.ds(f, 1), :], hid.rearrange("p (o t) -> p o t", o=1),
                                           hh[:, bass.ds(f, 1), :].bitcast(F32), ALU.subtract
                                           ).then_inc(L.hidden_made, 1)
                    with pool.Fori(0, KD // 2) as n:
                        add_parts(L, pool, part, c * per + n + (FC + q0), n)
    L.q += CH * per
    L.q_own += CH * per
    L.y += CH * KD // 2
    L.h += FT


def take_parts(L, act, part, q, y, scale):
    for a in range(2):
        act.wait_ge(L.multiplied[a], q + 2)
        act.wait_ge(L.added[a], y + 1)
        act.activation(part[a], L.bank[a][:, 0:T], ACT.Copy, scale=scale).then_inc(L.taken[a], 1)


def add_parts(L, pool, part, q, n):
    for a in range(2):
        pool.wait_ge(L.taken[a], q + 2)
        x = L.xT[:, bass.ds(n * 2 + a, 1), :]
        pool.tensor_tensor(x, x, part[a].rearrange("p (o t) -> p o t", o=1), ALU.add
                           ).then_inc(L.added[a], 1)


def rsqrt_steps(L, act, dve, var, work, done, n0, part):
    v, r, t = work[:, 0], work[:, 1], work[:, 2]
    if part == 0:
        dve.tensor_scalar(v, var, EPS, None, ALU.add).then_inc(done, 1)
    if part == 1:
        act.wait_ge(done, n0 + 1)
        act.activation(t, v, ACT.Sqrt).then_inc(done, 1)
    if part == 2:
        steps = [
            lambda: dve.reciprocal(r, t),
            lambda: dve.tensor_tensor(t, v, r, ALU.mult),
            lambda: dve.tensor_tensor(t, t, r, ALU.mult),
            lambda: dve.tensor_scalar(t, t, -0.5, 1.5, ALU.mult, ALU.add),
            lambda: dve.tensor_tensor(r, r, t, ALU.mult),
        ]
        for i, s in enumerate(steps):
            dve.wait_ge(done, n0 + 2 + i)
            s().then_inc(done, 1)
        dve.wait_ge(done, n0 + 7)


def layer_norm(L, n):
    nc, bank, xT = L.nc, L.bank, L.xT
    last = n == 2
    mean_ready, centred, squared, summed, root, scaled, shifted, hi_made, lo_made, kept, warm = (
        L.sem(f"ln{n}_{s}") for s in ("mean", "centred", "squared", "summed", "root", "scaled",
                                     "shifted", "hi", "lo", "kept", "warm"))
    ones = L.cst[:, K_MEAN:K_MEAN + P]
    scope = ExitStack()
    with scope:
        sq, z, work = L.proj[:, 0:4], L.proj[:, 4:8], L.proj[:, 8:11]
        with nc.Block() as block:
            @block.tensor
            def _(pe):
                for k in range(KD):
                    mm = pe.matmul(bank[2][:, 0:T], ones, xT[:, k], start=(k == 0), stop=(k == KD - 1))
                mm.then_inc(mean_ready, 1)
                for k in range(KD):
                    pe.wait_ge(squared, k + 1)
                    pe.matmul(bank[3][:, 0:T], ones, sq[:, k % 4], start=(k == 0),
                              stop=(k == KD - 1)).then_inc(summed, 1)

            @block.scalar
            def _(act):
                for k in range(KD):
                    act.wait_ge(centred, k + 1)
                    if k >= 4:
                        act.wait_ge(summed, k - 3)
                    act.activation(sq[:, k % 4], xT[:, k], ACT.Square).then_inc(squared, 1)
                rsqrt_steps(L, act, None, None, work, root, 0, 1)
                for k in range(KD):
                    act.wait_ge(scaled, k + 1)
                    if not last and k >= 4:
                        act.wait_ge(lo_made, k - 3)
                        act.wait_ge(kept, k - 3)
                    out = xT[:, k] if last else z[:, k % 4]
                    act.activation(out, xT[:, k], ACT.Identity, scale=L.ln_g[:, n, k:k + 1],
                                   bias=L.ln_b[:, n, k:k + 1]).then_inc(shifted, 1)
                    if not last:
                        act.wait_ge(shifted, k + 1)
                        act.activation(L.xh[:, k], z[:, k % 4], ACT.Copy).then_inc(hi_made, 1)

            @block.vector
            def _(dve):
                dve.wait_ge(mean_ready, 1)
                for k in range(KD):
                    dve.tensor_tensor(xT[:, k], xT[:, k], bank[2][:, 0:T], ALU.subtract
                                      ).then_inc(centred, 1)
                dve.wait_ge(summed, KD)
                rsqrt_steps(L, None, dve, bank[3][:, 0:T], work, root, 0, 0)
                rsqrt_steps(L, None, dve, None, work, root, 0, 2)

                def lo(k):
                    dve.wait_ge(hi_made, k + 1)
                    dve.tensor_tensor(L.xl[:, k], z[:, k % 4], L.xh[:, k].bitcast(F32), ALU.subtract
                                      ).then_inc(lo_made, 1)

                for k in range(KD):
                    dve.tensor_tensor(xT[:, k], xT[:, k], work[:, 1], ALU.mult).then_inc(scaled, 1)
                    if not last and k >= 2:
                        lo(k - 2)
                if not last:
                    lo(KD - 2)
                    lo(KD - 1)

            @block.gpsimd
            def _(pool):
                if not last:
                    for k in range(KD):
                        pool.wait_ge(shifted, k + 1)
                        pool.tensor_scalar(xT[:, k], z[:, k % 4], ALPHA, None, ALU.mult
                                           ).then_inc(kept, 1)


def projection(L):
    nc = L.nc
    w = L.A["w_in"][0]
    seg_a = w[:, 0:C_GA].rearrange("(k p) n -> p k n", p=P)
    seg_r = w[:, C_GR:C_NQ].rearrange("(k p) n -> p k n", p=P)
    seg_q = [w[:, C_NQ + u * G * HD:C_KV].rearrange("(k p) n -> p k n", p=P) for u in range(2)]
    seg_kv = w[:, C_KV:C_NG].rearrange("(k p) n -> p k n", p=P)
    w_rows = w.rearrange("(k p) n -> p k n", p=P)
    q0, own0 = L.q, L.q_own
    NP = NT // 2
    q_loaded = [L.sem(f"q_loaded{a}") for a in range(2)]
    small_loaded, small_mult = L.sem("gates_w_loaded"), L.sem("gates_mult")
    small_taken = L.sem("gates_taken")
    scope = ExitStack()
    with scope:
        w_small = L.sb("w_small", [P, KD, 80], scope=scope)
        cleared = L.sem("w_small_cleared")
        with nc.Block() as block:
            @block.sync
            def _(sp):
                sp.wait_ge(cleared, 1)
                sp.dma_start(w_small[:, :, 0:48], w_rows[:, :, C_NG:C_NG + 48]).then_inc(small_loaded, 16)
                sp.dma_start(w_small[:, :, 64:80], w_rows[:, :, C_GA:C_GA + 16]).then_inc(small_loaded, 16)

                def segment(src, pairs, at):
                    with sp.Fori(0, pairs) as i:
                        for a in range(2):
                            load_unit(L, sp, i + (q0 + at), a, src[:, :, bass.ds(i * (2 * P) + a * P, P)], KD)

                segment(seg_a, 8, 0)
                segment(seg_r, 4, 8)
                with sp.Fori(0, 2) as h:
                    with sp.Fori(0, 2) as gg:
                        for a in range(2):
                            sp.wait_ge(L.split[a], h * 2 + gg + (q0 + 12 + 1))
                            to = L.raw[a][:].rearrange("p (k u d) -> p k u d", u=2, d=HD)
                            for u in range(2):
                                sp.dma_start(to[:, :, u], seg_q[u][:, :, bass.ds(h * (8 * HD) + gg * (2 * HD) + a * HD, HD)]
                                             ).then_inc(q_loaded[a], 16)
                segment(seg_kv, 6, 16)

            @block.vector
            def _(dve):
                dve.memset(w_small[:], 0.0).then_inc(cleared, 1)
                with dve.Fori(0, 12) as i:
                    split_pair(L, dve, i + q0, L.loaded, 16, i + own0, KD)
                with dve.Fori(0, 4) as i:
                    split_pair(L, dve, i + (q0 + 12), q_loaded, 32, i, KD)
                with dve.Fori(0, 6) as i:
                    split_pair(L, dve, i + (q0 + 16), L.loaded, 16, i + (own0 + 12), KD)

            @block.tensor
            def _(pe):
                with pe.Fori(0, NP) as i:
                    for a in range(2):
                        multiply_unit(L, pe, i + q0, a, KD, (L.xh, L.xl))
                pe.wait_ge(small_loaded, 32)
                for k in range(KD):
                    mm = pe.matmul(L.bank[2][0:80, 0:T], w_small[:, k], L.xT[:, k],
                                   start=(k == 0), stop=(k == KD - 1))
                mm.then_inc(small_mult, 1)

            @block.scalar
            def _(act):
                with act.Fori(0, NP) as i:
                    for a in range(2):
                        act.wait_ge(L.multiplied[a], i + (q0 + 2))
                        act.activation(L.proj[:, bass.ds(i * 2 + a, 1), :],
                                       L.bank[a][:, 0:T].rearrange("p (o t) -> p o t", o=1),
                                       ACT.Copy).then_inc(L.taken[a], 1)
                act.wait_ge(small_mult, 1)
                act.activation(L.gate[64:80], L.bank[2][64:80, 0:T], ACT.Copy, scale=1.0 / ALPHA)
                act.activation(L.gate[0:48], L.bank[2][0:48, 0:T], ACT.Sigmoid, scale=1.0 / ALPHA
                               ).then_inc(small_taken, 1)
    L.q += NP
    L.q_own += NP - 4


def turn_projection(L):
    nc, A, O, bank, proj = L.nc, L.A, L.O, L.bank, L.proj
    roped = [T_NQ + i for i in range(8)] + [T_KV + i for i in (0, 1, 4, 5, 8, 9)]
    NR = len(roped)
    ident = L.cst[:, K_ID:K_ID + P]
    rotated, by_cos, by_sin, rope_done = (L.sem("rope_" + s) for s in ("rotated", "cos", "sin", "done"))
    turned, turned_out = L.sem("turned"), L.sem("turned_out")
    L.kv_stored = L.sem("kv_stored")
    jobs = [("v", t, n) for t in range(3) for n in range(2)] + \
           [("kv", t, n) for t in range(3) for n in range(3)] + [("g", t, 0) for t in range(3)]
    with ExitStack() as scope:
        xc = L.sb("rope_xc", [P, 2, T], scope=scope)
        xs = L.sb("rope_xs", [P, 2, T], scope=scope)
        with nc.Block() as block:
            @block.tensor
            def _(pe):
                for i, t in enumerate(roped):
                    if i >= 2:
                        pe.wait_ge(by_sin, i - 1)
                    pe.matmul(bank[i % 2][:, 0:T], L.cst[:, K_ROT:K_ROT + P], proj[:, t],
                              start=True, stop=True).then_inc(rotated, 1)
                for i, (what, t, n) in enumerate(jobs):
                    if i >= 4:
                        pe.wait_ge(turned_out, i - 3)
                    if i == 6:
                        pe.wait_ge(rope_done, NR)
                    rows = P if t < 2 else T - TP
                    b = bank[2 + i % 4]
                    if what == "g":
                        mm = pe.transpose(b[0:rows, 0:48], L.gate[0:48, t * P:t * P + rows],
                                          ident[0:48, 0:48])
                    else:
                        base = (T_GV if what == "v" else T_KV) + 4 * n
                        for j in range(4):
                            mm = pe.transpose(b[0:rows, j * P:(j + 1) * P],
                                              proj[:, base + j, t * P:t * P + rows], ident)
                    mm.then_inc(turned, 1)

            @block.scalar
            def _(act):
                for i, (what, t, n) in enumerate(jobs):
                    act.wait_ge(turned, i + 1)
                    rows = P if t < 2 else T - TP
                    b = bank[2 + i % 4]
                    if what == "g":
                        act.activation(L.gate_tok[0:rows, t], b[0:rows, 0:48], ACT.Copy).then_inc(turned_out, 1)
                    else:
                        to = L.v_gla if what == "v" else L.kv_tok
                        act.activation(to[0:rows, t, n * 512:(n + 1) * 512], b[0:rows, :], ACT.Copy
                                       ).then_inc(turned_out, 1)

            @block.gpsimd
            def _(pool):
                for i, t in enumerate(roped):
                    if i >= 2:
                        pool.wait_ge(rope_done, i - 1)
                    pool.tensor_tensor(xc[:, i % 2], proj[:, t], L.cst[:, K_COS:K_COS + T], ALU.mult
                                       ).then_inc(by_cos, 1)

            @block.vector
            def _(dve):
                for i, t in enumerate(roped):
                    dve.wait_ge(rotated, i + 1)
                    dve.tensor_tensor(xs[:, i % 2], bank[i % 2][:, 0:T], L.cst[:, K_SIN:K_SIN + T],
                                      ALU.mult).then_inc(by_sin, 1)
                    dve.wait_ge(by_sin, i + 1)
                    dve.wait_ge(by_cos, i + 1)
                    dve.tensor_tensor(proj[:, t], xc[:, i % 2], xs[:, i % 2], ALU.add
                                      ).then_inc(rope_done, 1)

            @block.sync
            def _(sp):
                sp.dma_start(O["win_s"][0, :, 0:PAST - TS].rearrange("b r s k d -> b r (s k d)"),
                             A["cache_win_kv"][0, :, TS:PAST].rearrange("b r s k d -> b r (s k d)")
                             ).then_inc(L.stored, 16)
                L.n_stored += 1
                for t in range(3):
                    for n, what in enumerate(("cmp", "slc", "win")):
                        sp.wait_ge(turned_out, 6 + 3 * t + n + 1)
                        if t < 2:
                            dst = O[what + "_p"][0, 0, t * P:(t + 1) * P].rearrange("r s k d -> r (s k d)")
                            src = L.kv_tok[:, t, n * 512:(n + 1) * 512]
                            sp.dma_start(dst, src).then_inc(L.kv_stored, 16)
                        elif what != "win":
                            dst = O[what + "_s"][0].rearrange("b t s k d -> (b t) (s k d)")
                            sp.dma_start(dst, L.kv_tok[0:64, 2, n * 512:(n + 1) * 512]
                                         ).then_inc(L.kv_stored, 16)
                        else:
                            for b in range(NB):
                                dst = O["win_s"][0, b, PAST - TS:PAST].rearrange("t s k d -> t (s k d)")
                                sp.dma_start(dst, L.kv_tok[b * TS:(b + 1) * TS, 2, 1024:1536]
                                             ).then_inc(L.kv_stored, 16)
                sp.wait_ge(L.kv_stored, 16 * (6 + 2 + NB))


class Chain:

    def __init__(self, eng, sem):
        self.eng, self.sem, self.n = eng, sem, 0

    def __call__(self, ins):
        self.n += 1
        ins.then_inc(self.sem, 1)

    def settle(self):
        self.eng.wait_ge(self.sem, self.n)


def gla(L, s):
    nc, A, O, bank, proj = L.nc, L.A, L.O, L.bank, L.proj
    TT = GH * T
    NS = NB * TS
    gw2 = L.sb("gw2", [P, GH * P], scope=s)
    gb2 = L.sb("gb2", [P, GH], scope=s)
    norm_g = L.sb("norm_g", [P, 2], scope=s)
    B = L.sb("decay", [P, GH, T], scope=s)
    EE = L.sb("decay_e", [P, 2, GH, T], scope=s)
    E, E2 = EE[:, 0], EE[:, 1]
    three = L.sb("gla_three", [P, 3, GH, T], scope=s)
    QL, KL, att = three[:, 0], three[:, 1], three[:, 2]
    attx = L.sb("gla_attx", [P, GH, P], scope=s)
    k_tok = L.sb("k_tok", [P, 3, GH * P], scope=s)
    q = proj[:, T_GQ:T_GQ + GH]
    k = proj[:, T_GK:T_GK + GH]
    ident = L.cst[:, K_ID:K_ID + P]
    w_loaded = L.sem("gla_w_loaded")
    logit, biased, dve_s, act_s, pool_s = (L.sem("gla_" + x) for x in
                                           ("logit", "biased", "dve", "act", "pool"))
    with nc.Block() as block:
        @block.sync
        def _(sp):
            sp.dma_start(gw2[64:80], A["w_gla_gate2"][0]).then_inc(w_loaded, 16)
            with nc.allow_non_contiguous_dma(reason="small vectors, feature-major"):
                sp.dma_start(gb2[:], A["b_gla_gate2"][0].rearrange("(h p) -> p h", p=P)).then_inc(w_loaded, 16)
                sp.dma_start(norm_g[:], A["gla_norm_g"][0].rearrange("(h p) -> p h", p=P)).then_inc(w_loaded, 16)

        @block.tensor
        def _(pe):
            pe.wait_ge(w_loaded, 48)
            for h in range(GH):
                pe.matmul(bank[h][:, 0:T], gw2[64:80, h * P:(h + 1) * P], L.gate[64:80, :],
                          start=True, stop=True).then_inc(logit, 1)

        @block.scalar
        def _(act):
            act.wait_ge(w_loaded, 48)
            for h in range(GH):
                act.wait_ge(logit, h + 1)
                act.activation(B[:, h], bank[h][:, 0:T], ACT.Identity, bias=gb2[:, h:h + 1]).then_inc(biased, 1)
            act.wait_ge(biased, GH)
            act.activation(E, B[:], ACT.Abs).then_inc(act_s, 1)
            act.wait_ge(act_s, 1)
            act.activation(E, E, ACT.Exp, scale=-1.0).then_inc(act_s, 1)
            act.wait_ge(act_s, 2)
            act.activation(E, E, ACT.Ln, bias=1.0).then_inc(act_s, 1)

        @block.vector
        def _(dve):
            dve.wait_ge(biased, GH)
            dve.wait_ge(act_s, 1)
            dve.tensor_scalar(B[:], B[:], 0.0, None, ALU.min).then_inc(dve_s, 1)
            dve.wait_ge(act_s, 3)
            dve.wait_ge(dve_s, 1)
            dve.tensor_tensor(B[:], B[:], E, ALU.subtract).then_inc(dve_s, 1)
            dve.wait_ge(dve_s, 2)
            dve.tensor_scalar(E, B[:], 1.0 / 16.0, None, ALU.mult).then_inc(dve_s, 1)
            dve.wait_ge(dve_s, 3)
            for h in range(GH):
                dve.tensor_tensor_scan(B[:, h], L.cst[:, K_RESET:K_RESET + T], E[:, h], 0.0,
                                       ALU.mult, ALU.add).then_inc(dve_s, 1)
            dve.tensor_scalar(proj[:, T_GQ:T_GQ + GH], proj[:, T_GQ:T_GQ + GH], P ** -0.5, None, ALU.mult
                              ).then_inc(dve_s, 1)

    diff, made_e, made_q, made_k, scored, merged = (L.sem("gla_lv_" + x) for x in
                                                    ("diff", "e", "q", "k", "scored", "merged"))
    made_abs = L.sem("gla_lv_abs")
    with nc.Block() as block:
        @block.vector
        def _(dve):
            dve.memset(att, 0.0).then_inc(merged, 1)
            for lv in range(LEVELS + 1):
                if lv > 0:
                    S = 1 << lv
                    if lv >= 2:
                        dve.wait_ge(made_e, lv - 1)
                    if lv <= 6:
                        v = B[:].rearrange("p h (n s) -> p (h n) s", s=S)
                        e = E.rearrange("p h (n s) -> p (h n) s", s=S)
                        r = v[:, :, S // 2 - 1:S // 2].to_broadcast([P, GH * T // S, S])
                        ins = dve.tensor_tensor(e, v, r, ALU.subtract)
                    else:
                        for h in range(GH):
                            v = B[:, h, 0:TP].rearrange("p (n s) -> p n s", s=S)
                            e = E[:, h, 0:TP].rearrange("p (n s) -> p n s", s=S)
                            r = v[:, :, S // 2 - 1:S // 2].to_broadcast([P, TP // S, S])
                            ins = dve.tensor_tensor(e, v, r, ALU.subtract)
                    ins.then_inc(diff, 1)
                    dve.wait_ge(made_e, lv)
                    if lv >= 1:
                        dve.wait_ge(scored, GH * lv)
                    dve.tensor_tensor(QL, q, E2, ALU.mult).then_inc(made_q, 1)
                for h in range(GH):
                    dve.wait_ge(scored, GH * lv + h + 1)
                    b = bank[(GH * lv + h) % 8]
                    dve.wait_ge(merged, 1 + (GH * lv + h))
                    if lv == LEVELS:
                        dve.tensor_copy(attx[:, h], b[:, 0:P]).then_inc(merged, 1)
                    elif lv <= 3:
                        dve.copy_predicated(att[:, h, 0:TP], L.lvl[:, lv, 0:TP], b[:, 0:TP])
                        dve.copy_predicated(att[0:NS, h, TP:T], L.lvl[0:NS, lv, TP:T], b[0:NS, TP:T]
                                            ).then_inc(merged, 1)
                    else:
                        dve.copy_predicated(att[:, h, 0:TP], L.lvl[:, lv, 0:TP], b[:, 0:TP]
                                            ).then_inc(merged, 1)

        @block.scalar
        def _(act):
            for lv in range(1, LEVELS + 1):
                act.wait_ge(diff, lv)
                if lv >= 2:
                    act.wait_ge(made_q, lv - 1)
                    act.wait_ge(made_k, lv - 1)
                act.activation(E, E, ACT.Abs).then_inc(made_abs, 1)
                act.wait_ge(made_abs, lv)
                act.activation(E2, E, ACT.Exp, scale=-1.0).then_inc(made_e, 1)

        @block.gpsimd
        def _(pool):
            for lv in range(1, LEVELS + 1):
                pool.wait_ge(made_e, lv)
                pool.wait_ge(scored, GH * lv)
                pool.tensor_tensor(KL, k, E2, ALU.mult).then_inc(made_k, 1)

        @block.tensor
        def _(pe):
            for lv in range(LEVELS + 1):
                ql, kl = (QL, KL) if lv else (q, k)
                if lv:
                    pe.wait_ge(made_q, lv)
                    pe.wait_ge(made_k, lv)
                for h in range(GH):
                    n = GH * lv + h
                    b = bank[n % 8]
                    if n >= 8:
                        pe.wait_ge(merged, 1 + n - 7)
                    if lv == LEVELS:
                        mm = pe.matmul(b[:, 0:P], kl[:, h, 0:P], ql[:, h, P:TP], start=True, stop=True)
                    else:
                        for t in range(3 if lv <= 3 else 2):
                            rows = P if t < 2 else NS
                            c = slice(t * P, t * P + rows)
                            mm = pe.matmul(b[0:rows, c], kl[:, h, c], ql[:, h, c], start=True, stop=True)
                    mm.then_inc(scored, 1)

    decayed, eb_made, q_in, k_out, turned, k_tok_made, o_ready, o_taken = (
        L.sem("gla_o_" + x) for x in ("decayed", "eb", "q_in", "k_out", "turned", "k_tok", "ready", "taken"))
    v_made, st_mult, st_made, sp_ready, sp_taken, joined, squared, ms_ready = (
        L.sem("gla_s_" + x) for x in ("v", "mult", "made", "p_ready", "p_taken", "joined", "squared", "ms"))
    st_in = [L.sem(f"state_in{i}") for i in range(2)]
    st_out = [L.sem(f"state_out{i}") for i in range(2)]
    s0 = [L.raw[0][:, i * 1024:(i + 1) * 1024].rearrange("p (h v) -> p h v", h=GH) for i in range(2)]
    s_new = [L.raw[1][:, i * 1024:(i + 1) * 1024].rearrange("p (h v) -> p h v", h=GH) for i in range(2)]
    v_one = [L.sb(f"v_one{i}", [64, GH * DV], scope=s) for i in range(2)]
    s_prompt = L.sb("s_prompt", [P, GH, DV], scope=s)
    last_e = L.sb("last_e", [P, GH, NB], scope=s)
    og = proj[:, T_GV:T_GV + 2 * GH]
    sq = L.sb("gla_sq", [P, 2 * GH, T], scope=s)
    inter = bank[4]
    ms_bank = [bank[i] for i in (2, 3, 6, 7)]
    with nc.Block() as block:
        @block.vector
        def _(dve):
            for h in range(GH):
                dve.tensor_tensor(E[:, h, 0:TP], B[:, h, TP - 1:TP].to_broadcast([P, TP]),
                                  B[:, h, 0:TP], ALU.subtract).then_inc(decayed, 1)
                v = B[:, h, TP:T].rearrange("p (n s) -> p n s", s=TS)
                dve.tensor_tensor(E[:, h, TP:T].rearrange("p (n s) -> p n s", s=TS),
                                  v[:, :, TS - 1:TS].to_broadcast([P, NB, TS]), v, ALU.subtract
                                  ).then_inc(decayed, 1)
            dve.wait_ge(eb_made, 1)
            dve.tensor_tensor(KL, k, E2, ALU.mult).then_inc(k_out, 1)
            dve.wait_ge(eb_made, 2)
            dve.tensor_tensor(QL[:, :, TP:T], q[:, :, TP:T], E[:, :, TP:T], ALU.mult).then_inc(q_in, 1)
            dve.tensor_copy(last_e[:], E[:, :, TP + TS - 1:T:TS]).then_inc(q_in, 1)
            dve.wait_ge(q_in, 2)
            for b in range(NB):
                if b >= 2:
                    dve.wait_ge(st_mult, GH * (b - 1))
                dve.tensor_scalar(v_one[b % 2][:], L.v_gla[0:64, 2], L.cst[0:64, K_SEQ + b:K_SEQ + b + 1],
                                  None, ALU.mult).then_inc(v_made, 1)
                if b >= 2:
                    dve.wait_ge(st_out[b % 2], 16 * (b // 2))
                dve.wait_ge(st_in[b % 2], 16 * (b // 2 + 1))
                for h in range(GH):
                    dve.wait_ge(st_mult, GH * b + h + 1)
                    dve.scalar_tensor_tensor(out=s_new[b % 2][:, h], in0=s0[b % 2][:, h],
                                             scalar=last_e[:, h, b:b + 1],
                                             in1=bank[5 + h % 2][:, 0:DV], op0=ALU.mult, op1=ALU.add
                                             ).then_inc(st_made, 1)
            dve.wait_ge(o_taken, 2 * GH)
            for n in range(2 * GH):
                o = og[:, n, TP:T].rearrange("p (b t) -> p b t", t=TS)
                dve.tensor_tensor(o, o, inter[:].rearrange("p (b n t) -> p n b t", n=2 * GH, t=TS)[:, n],
                                  ALU.add).then_inc(joined, 1)

        @block.scalar
        def _(act):
            act.wait_ge(decayed, 2 * GH)
            act.activation(E2, E, ACT.Exp).then_inc(eb_made, 1)
            act.wait_ge(eb_made, 1)
            act.activation(E[:, :, TP:T], B[:, :, TP:T], ACT.Exp).then_inc(eb_made, 1)
            for t in range(3):
                rows = P if t < 2 else NS
                act.wait_ge(turned, t + 1)
                act.activation(k_tok[0:rows, t], bank[t][0:rows, :], ACT.Copy).then_inc(k_tok_made, 1)
            for n in range(2 * GH):
                act.wait_ge(o_ready, n + 1)
                act.activation(og[:, n], bank[n % 4][:, 0:T], ACT.Copy).then_inc(o_taken, 1)
            for i in range(2):
                act.wait_ge(sp_ready, i + 1)
                act.activation(s_prompt[:, 2 * i:2 * i + 2], bank[i][:].rearrange("p (h v) -> p h v", h=2),
                               ACT.Copy).then_inc(sp_taken, 1)
            act.wait_ge(joined, 2 * GH)
            act.activation(sq[:], og, ACT.Square).then_inc(squared, 1)

        @block.sync
        def _(sp):
            for b in range(NB):
                if b >= 2:
                    sp.wait_ge(st_made, GH * (b - 1))
                sp.dma_start(s0[b % 2], A["state_gla"][0, b].rearrange("h k v -> k h v")
                             ).then_inc(st_in[b % 2], 16)
                if b >= 1:
                    sp.wait_ge(st_made, GH * b)
                    sp.dma_start(O["gla_s"][0, b - 1].rearrange("h k v -> k h v"), s_new[(b - 1) % 2]
                                 ).then_inc(st_out[(b - 1) % 2], 16)
            sp.wait_ge(st_made, GH * NB)
            sp.dma_start(O["gla_s"][0, NB - 1].rearrange("h k v -> k h v"), s_new[(NB - 1) % 2]
                         ).then_inc(st_out[(NB - 1) % 2], 16)
            sp.wait_ge(sp_taken, 2)
            sp.dma_start(O["gla_p"][0, 0].rearrange("h k v -> k h v"), s_prompt[:]).then_inc(L.stored, 16)
            L.n_stored += 1
            for i in range(2):
                sp.wait_ge(st_out[i], 16 * NB // 2)
            sp.wait_ge(L.stored, 16 * L.n_stored)

        @block.tensor
        def _(pe):
            pe.wait_ge(k_out, 1)
            for t in range(3):
                rows = P if t < 2 else NS
                for h in range(GH):
                    mm = pe.transpose(bank[t][0:rows, h * P:(h + 1) * P], KL[:, h, t * P:t * P + rows], ident)
                mm.then_inc(turned, 1)
            pe.wait_ge(k_tok_made, 3)
            for n in range(2 * GH):
                h, c = n // 2, n % 2
                b = bank[n % 4]
                vc = slice(h * DV + c * P, h * DV + (c + 1) * P)
                if n >= 4:
                    pe.wait_ge(o_taken, n - 3)
                pe.matmul(b[:, 0:P], L.v_gla[:, 0, vc], att[:, h, 0:P], start=True, stop=False,
                          skip_group_check=True)
                pe.matmul(b[:, P:TP], L.v_gla[:, 0, vc], attx[:, h], start=False, stop=False,
                          skip_group_check=True)
                pe.matmul(b[:, P:TP], L.v_gla[:, 1, vc], att[:, h, P:TP], start=False, stop=False,
                          skip_group_check=True)
                pe.matmul(b[:, TP:T], L.v_gla[0:NS, 2, vc], att[0:NS, h, TP:T], start=False, stop=True,
                          skip_group_check=True).then_inc(o_ready, 1)
            pe.wait_ge(q_in, 2)
            for b in range(NB):
                pe.wait_ge(st_in[b % 2], 16 * (b // 2 + 1))
                for n in range(2 * GH):
                    h, c = n // 2, n % 2
                    at = (b * 2 * GH + n) * TS
                    pe.matmul(inter[:, at:at + TS], s0[b % 2][:, h, c * P:(c + 1) * P],
                              QL[:, h, TP + b * TS:TP + (b + 1) * TS], start=True, stop=True)
                pe.wait_ge(v_made, b + 1)
                for h in range(GH):
                    if b * GH + h >= 2:
                        pe.wait_ge(st_made, b * GH + h - 1)
                    pe.matmul(bank[5 + h % 2][:, 0:DV], k_tok[0:NS, 2, h * P:(h + 1) * P],
                              v_one[b % 2][:, h * DV:(h + 1) * DV], start=True, stop=True
                              ).then_inc(st_mult, 1)
            pe.wait_ge(o_taken, 2 * GH)
            for h in range(GH):
                for t in range(2):
                    mm = pe.matmul(bank[h // 2][:, (h % 2) * DV:(h % 2 + 1) * DV],
                                   k_tok[:, t, h * P:(h + 1) * P], L.v_gla[:, t, h * DV:(h + 1) * DV],
                                   start=(t == 0), stop=(t == 1))
                if h % 2:
                    mm.then_inc(sp_ready, 1)
            pe.wait_ge(squared, 1)
            pe.wait_ge(st_made, GH * NB)
            for h in range(GH):
                for c in range(2):
                    mm = pe.matmul(ms_bank[h][:, 0:T], L.cst[:, K_RMS:K_RMS + P], sq[:, 2 * h + c],
                                   start=(c == 0), stop=(c == 1))
            mm.then_inc(ms_ready, 1)

    v, r, t = QL, KL, att
    nd, na, silu = L.sem("gla_n_dve"), L.sem("gla_n_root"), L.sem("gla_n_silu")
    with nc.Block() as block:
        @block.scalar
        def _(act):
            act.wait_ge(nd, GH)
            act.activation(t, v, ACT.Sqrt).then_inc(na, 1)
            act.activation(sq[:], proj[:, T_GR:T_GR + 2 * GH], ACT.Silu).then_inc(silu, 1)

        @block.vector
        def _(dve):
            ch = Chain(dve, nd)
            for h in range(GH):
                ch(dve.tensor_scalar(v[:, h], ms_bank[h][:, 0:T], EPS, None, ALU.add))
            dve.wait_ge(na, 1)
            for step in (lambda: dve.reciprocal(r, t),
                         lambda: dve.tensor_tensor(t, v, r, ALU.mult),
                         lambda: dve.tensor_tensor(t, t, r, ALU.mult),
                         lambda: dve.tensor_scalar(t, t, -0.5, 1.5, ALU.mult, ALU.add),
                         lambda: dve.tensor_tensor(r, r, t, ALU.mult)):
                ch.settle()
                ch(step())
            ch.settle()
            for n in range(2 * GH):
                ch(dve.tensor_tensor(og[:, n], og[:, n], r[:, n // 2], ALU.mult))
            ch.settle()
            dve.wait_ge(silu, 1)
            for n in range(2 * GH):
                ch(dve.scalar_tensor_tensor(out=proj[:, T_OG + n], in0=og[:, n], scalar=norm_g[:, n % 2:n % 2 + 1],
                                            in1=sq[:, n], op0=ALU.mult, op1=ALU.mult))
            ch.settle()


def compress(L, s):
    nc, A, O, bank = L.nc, L.A, L.O, L.bank
    NQ = NB + 1
    LT = CL // 2
    ident = L.cst[:, K_ID:K_ID + P]
    rows = [L.sb(f"cmp_rows{i}", [P, 2, KV, 2, HD], scope=s) for i in range(2)]
    R = [L.sb(f"cmp_turned{n}", [P, NQ, KV, P], scope=s) for n in range(2)]
    w1 = [L.raw[n][:].rearrange("p (l m) -> p l m", m=P) for n in range(2)]
    w2 = L.sb("cmp_w2", [P, 2, HD], scope=s)
    pos = L.sb("cmp_pos_rows", [32, P], scope=s)
    posT = L.sb("cmp_pos_cols", [P, 32], scope=s)
    bias = L.sb("cmp_bias", [P, 2], scope=s)
    hid = [L.sb(f"cmp_hid{n}", [P, NQ, KV, NC], scope=s) for n in range(2)]
    table = L.sb("table", [1, NB * NPG], I32, scope=s)
    scratch = nc.dram_tensor("gate_scratch", [NB * TS, 48], F32, kind="Internal").ap()
    w_in, table_in, gate_out, small_in = (L.sem("cmp_" + x) for x in ("w", "table", "gate", "small"))
    rows_in = [L.sem(f"cmp_rows_in{i}") for i in range(2)]
    taken = [L.sem(f"cmp_taken{n}") for n in range(2)]
    turned, cleared, pos_turned, pos_taken, biased, bias_taken, hidden, acted, k_ready, v_ready, done = (
        L.sem("cmp_" + x) for x in ("turned", "cleared", "pos_turned", "pos_taken", "biased",
                                    "bias_taken", "hidden", "acted", "k", "v", "done"))
    with nc.Block() as block:
        @block.sync
        def _(sp):
            sp.dma_start(table[:], A["page_table"].rearrange("b p -> (b p)").unsqueeze(0)).then_inc(table_in, 16)
            sp.dma_start(pos[:], A["cmp_pos"][0].rearrange("s (l a) d -> (s l) (a d)", a=2)).then_inc(w_in, 16)
            for n in range(2):
                sp.dma_start(w1[n], A["cmp_w1"][0, n].rearrange("(l p) m -> p l m", p=P)).then_inc(w_in, 16)
                sp.dma_start(w2[:, n], A["cmp_w2"][0, n]).then_inc(w_in, 16)
            sp.dma_start(scratch, L.gate_tok[0:64, 2]).then_inc(gate_out, 16)
            sp.wait_ge(table_in, 16)
            for b in range(NQ):
                if b >= 2:
                    sp.wait_ge(turned, 2 * (b - 1))
                for g in range(NPG):
                    dst = rows[b % 2][g * 64:(g + 1) * 64].rearrange("m s k a d -> m (s k) a d")
                    if b < NB:
                        page = sp.value_load(table[0:1, b * NPG + g:b * NPG + g + 1], min_val=0,
                                             max_val=A["cache_cmp_kv"].shape[1] - 1)
                        src = A["cache_cmp_kv"][0, bass.ds(page, 1)].rearrange(
                            "o (m a) s k d -> (o m) a (s k) d", a=2)
                    else:
                        src = O["cmp_p"][0, 0, g * PAGE:(g + 1) * PAGE].rearrange("(m a) s k d -> m a (s k) d", a=2)
                    for r in range(2):
                        sp.dma_start(dst[:, :, r], src[:, r]).then_inc(rows_in[b % 2], 16)
            sp.wait_ge(cleared, 2)
            sp.wait_ge(gate_out, 16)
            for b in range(NB):
                for g, what in ((0, "slc_s"), (1, "win_s")):
                    src = O[what][0, b, (PAST - TS if g else 0):(PAST if g else TS), 1]
                    sp.dma_start(L.v_small[8:16, g, b], src.rearrange("t k d -> t (k d)")
                                 ).then_inc(small_in, 16)
            with nc.allow_non_contiguous_dma(reason="gates by (head, token)"):
                for h in range(NH):
                    sp.dma_start(L.gate_rows[h * TS:(h + 1) * TS],
                                 scratch[:, 3 * h:3 * h + 3].rearrange("(b t) r -> t b r", t=TS)
                                 ).then_inc(small_in, 16)
            sp.wait_ge(small_in, 16 * (2 * NB + NH))

        @block.tensor
        def _(pe):
            pe.wait_ge(w_in, 16 * 5)
            pe.transpose(bank[6][:, 0:32], pos[:], ident[0:32, 0:32]).then_inc(pos_turned, 1)
            pe.wait_ge(pos_taken, 1)
            for n in range(2):
                for l in range(LT):
                    mm = pe.matmul(bank[7][:, n:n + 1], w1[n][:, l], posT[:, n * LT + l:n * LT + l + 1],
                                   start=(l == 0), stop=(l == LT - 1))
            mm.then_inc(biased, 1)
            for b in range(NQ):
                pe.wait_ge(rows_in[b % 2], 32 * NPG * (b // 2 + 1))
                for n in range(2):
                    if b >= 1:
                        pe.wait_ge(taken[n], b)
                    for kv in range(KV):
                        mm = pe.transpose(bank[n][:, kv * P:(kv + 1) * P], rows[b % 2][:, n, kv].rearrange("p a d -> p (a d)"), ident)
                    mm.then_inc(turned, 1)
            for n in range(2):
                pe.wait_ge(taken[n], NQ)
            for n in range(2):
                for l in range(LT):
                    pe.matmul(bank[2 + n][:, 0:NB * KV * NC], w1[n][:, l],
                              R[n][:, 0:NB, :, l:l + 8 * (NC - 1) + 1:8].rearrange("p b k n -> p (b k) n"),
                              start=(l == 0), stop=(l == LT - 1))
                for l in range(LT):
                    mm = pe.matmul(bank[4 + n][:, 0:KV * NC], w1[n][:, l],
                                   R[n][:, NB, :, l:l + 8 * (NC - 1) + 1:8], start=(l == 0), stop=(l == LT - 1))
                mm.then_inc(hidden, 1)
            pe.wait_ge(acted, 2)
            for a in range(2):
                mm = pe.matmul(bank[0][a * HD:(a + 1) * HD, 0:NQ * 2 * NC], w2[:, 0],
                               hid[0][:, :, a:KV:2, :].rearrange("p b k n -> p b k n"), start=True, stop=True)
            mm.then_inc(k_ready, 1)
            pe.wait_ge(acted, 4)
            for b in range(NQ):
                if b >= 2:
                    pe.wait_ge(done, b)
                for kv in range(KV):
                    mm = pe.matmul(bank[6 + b % 2][0:NC, kv * HD:(kv + 1) * HD], hid[1][:, b, kv],
                                   w2[:, 1], start=True, stop=True)
                mm.then_inc(v_ready, 1)

        @block.scalar
        def _(act):
            act.wait_ge(pos_turned, 1)
            act.activation(posT[:], bank[6][:, 0:32], ACT.Copy).then_inc(pos_taken, 1)
            for i in range(0, 2 * NQ, 2):
                act.wait_ge(turned, i + 1)
                act.activation(R[0][:, i // 2].rearrange("p k m -> p (k m)"), bank[0][:], ACT.Copy
                               ).then_inc(taken[0], 1)
            act.wait_ge(bias_taken, 1)
            for n in range(2):
                act.wait_ge(hidden, n + 1)
                act.activation(hid[n][:, 0:NB].rearrange("p b k n -> p (b k n)"), bank[2 + n][:, 0:NB * KV * NC],
                               ACT.Gelu_apprx_tanh, bias=bias[:, n:n + 1]).then_inc(acted, 1)
                act.activation(hid[n][:, NB].rearrange("p k n -> p (k n)"), bank[4 + n][:, 0:KV * NC],
                               ACT.Gelu_apprx_tanh, bias=bias[:, n:n + 1]).then_inc(acted, 1)

        @block.vector
        def _(dve):
            dve.memset(L.k_cmp[:], 0.0).then_inc(cleared, 1)
            dve.memset(L.v_small[:], 0.0).then_inc(cleared, 1)
            dve.wait_ge(biased, 1)
            dve.tensor_copy(bias[:], bank[7][:, 0:2]).then_inc(bias_taken, 1)
            for i in range(1, 2 * NQ, 2):
                dve.wait_ge(turned, i + 1)
                dve.tensor_copy(R[1][:, i // 2].rearrange("p k m -> p (k m)"), bank[1][:]).then_inc(taken[1], 1)
            dve.wait_ge(k_ready, 1)
            dve.wait_ge(cleared, 2)
            dve.tensor_copy(L.k_cmp[:, :, :, 0:NC],
                            bank[0][:, 0:NQ * 2 * NC].rearrange("p (b k n) -> p b k n", b=NQ, k=2)
                            ).then_inc(done, 1)
            for b in range(NQ):
                dve.wait_ge(v_ready, b + 1)
                dve.tensor_copy(L.v_small[0:NC, 2, b], bank[6 + b % 2][0:NC, 0:256]).then_inc(done, 1)


def attention(L, s):
    nc, A, O, bank, proj = L.nc, L.A, L.O, L.bank, L.proj
    mix = proj[:, T_NQ:T_NQ + 8]
    ident = L.cst[:, K_ID:K_ID + P]
    S = [L.sb(f"scores{i}", [P, 3, GW], scope=s) for i in range(2)]
    PR = [L.sb(f"probs{i}", [P, 3, GW], scope=s) for i in range(2)]
    PT = [L.sb(f"probs_turned{i}", [P, 7, P], scope=s) for i in range(2)]
    stat = [L.sb(f"stat{i}", [P, 5, 3], scope=s) for i in range(2)]
    past = [L.sb(f"past{i}", [P, 2, NPG, 512], scope=s) for i in range(2)]
    KT = [L.sb(f"past_k{i}", [P, 2, 2, PAST], scope=s) for i in range(2)]
    table = L.sb("table2", [1, NB * NPG], I32, scope=s)
    q_s = L.sb("q_sample", [P, 2, NB, G * TS], scope=s)
    items = [(p, a, g, qt) for p in range(2) for g in range(G) for qt in range(2) for a in range(2)]
    NP_, NI = len(items), len(items) + NB
    table_in = L.sem("att_table")
    past_in = [L.sem(f"past_in{i}") for i in range(2)]
    k_turned, k_taken, scored, masked, maxed, exped, summed, weighed, turned, taken, out_ready, out_taken, filled = (
        L.sem("att_" + x) for x in ("k_turned", "k_taken", "scored", "masked", "maxed", "exped", "summed",
                                    "weighed", "turned", "taken", "out_ready", "out_taken", "filled"))
    with nc.Block() as block:
        @block.sync
        def _(sp):
            sp.dma_start(table[:], A["page_table"].rearrange("b p -> (b p)").unsqueeze(0)).then_inc(table_in, 16)
            sp.wait_ge(table_in, 16)
            for b in range(NB):
                if b >= 2:
                    sp.wait_ge(out_ready, NP_ + b - 1)
                for g in range(NPG):
                    page = sp.value_load(table[0:1, b * NPG + g:b * NPG + g + 1], min_val=0,
                                         max_val=A["cache_slc_kv"].shape[1] - 1)
                    sp.dma_start(past[b % 2][:, 0, g],
                                 A["cache_slc_kv"][0, bass.ds(page, 1)].rearrange("o r s k d -> (o r) (s k d)")
                                 ).then_inc(past_in[b % 2], 16)
                    sp.dma_start(past[b % 2][:, 1, g],
                                 A["cache_win_kv"][0, b, g * P:(g + 1) * P].rearrange("r s k d -> r (s k d)")
                                 ).then_inc(past_in[b % 2], 16)

        @block.tensor
        def _(pe):
            def scores(i):
                if i >= 1:
                    pe.wait_ge(masked, 2 * i)
                if i < NP_:
                    p, a, g, qt = items[i]
                    r = slice(a * HD, (a + 1) * HD)
                    qT = proj[r, T_NQ + 4 * p + g, qt * P:(qt + 1) * P]
                    for n in range(2):
                        pe.matmul(bank[0][:, n * 256:(n + 1) * 256], qT, proj[r, T_KV + 4 + 4 * n + p, 0:TP],
                                  start=True, stop=True)
                    pe.matmul(bank[1][:, 32:48], qT, L.k_cmp[r, NB, p], start=True, stop=True).then_inc(scored, 1)
                    return
                b = i - NP_
                pe.wait_ge(k_taken, 2 * b + 2)
                pe.wait_ge(filled, 4)
                c = TP + b * TS
                for kv in range(KV):
                    p, a = kv // 2, kv % 2
                    r = slice(a * HD, (a + 1) * HD)
                    o = slice(32 * kv, 32 * kv + 32)
                    qT = q_s[r, p, b]
                    for n in range(2):
                        pe.matmul(bank[0][o, n * 256:(n + 1) * 256], qT, KT[b % 2][r, n, p], start=True, stop=True)
                        pe.matmul(bank[1][o, 16 * n:16 * n + 16], qT, proj[r, T_KV + 4 + 4 * n + p, c - TS:c + TS],
                                  start=True, stop=True)
                    mm = pe.matmul(bank[1][o, 32:48], qT, L.k_cmp[r, b, p], start=True, stop=True)
                mm.then_inc(scored, 1)

            def turn_keys(b):
                for n in range(2):
                    if 2 * b + n >= 2:
                        pe.wait_ge(k_taken, 2 * b + n - 1)
                    if n == 0:
                        pe.wait_ge(past_in[b % 2], 64 * (b // 2 + 1))
                    for p in range(2):
                        for g in range(NPG):
                            mm = pe.transpose(bank[6 + n][:, p * PAST + g * P:p * PAST + (g + 1) * P],
                                              past[b % 2][:, n, g, p * P:(p + 1) * P], ident)
                    mm.then_inc(k_turned, 1)

            def turn_probs(i):
                pe.wait_ge(weighed, i + 1)
                if i >= 1:
                    pe.wait_ge(taken, 2 * i)
                w = PR[i % 2]
                for n in range(2):
                    for g in range(2):
                        pe.transpose(bank[2][:, (2 * n + g) * P:(2 * n + g + 1) * P],
                                     w[:, n, g * P:(g + 1) * P], ident)
                for n in range(3) if i >= NP_ else [2]:
                    mm = pe.transpose(bank[3][0:16, n * P:(n + 1) * P], w[:, n, PAST:GW], ident)
                mm.then_inc(turned, 1)

            def outputs(i):
                pe.wait_ge(taken, 2 * i + 2)
                if i >= 2:
                    pe.wait_ge(out_taken, i - 1)
                pt = PT[i % 2]
                b = i - NP_
                o_bank = bank[4 + i % 2]
                for kv in range(KV) if b >= 0 else [2 * items[i][0] + items[i][1]]:
                    p, a = kv // 2, kv % 2
                    r = slice(a * HD, (a + 1) * HD)
                    if b < 0:
                        o, cols = o_bank[r, 0:P], slice(0, P)
                        v = [L.kv_tok[:, g, (3 + 2 * n) * 256 + kv * HD:(3 + 2 * n) * 256 + (kv + 1) * HD]
                             for n in range(2) for g in range(2)]
                    else:
                        o, cols = o_bank[r, p * 32:p * 32 + 32], slice(32 * kv, 32 * kv + 32)
                        v = [past[b % 2][:, n, g, 256 + kv * HD:256 + (kv + 1) * HD]
                             for n in range(2) for g in range(2)]
                    for c in range(4):
                        pe.matmul(o, v[c], pt[:, c, cols], start=(c == 0), stop=False)
                    for n in range(3) if b >= 0 else [2]:
                        mm = pe.matmul(o, L.v_small[:, n, b if b >= 0 else NB, kv * HD:(kv + 1) * HD],
                                       pt[0:16, 4 + n, cols], start=False, stop=(n == 2))
                mm.then_inc(out_ready, 1)

            for i in range(NI + 1):
                if i < NI:
                    if i >= NP_:
                        turn_keys(i - NP_)
                    scores(i)
                if i >= 1:
                    turn_probs(i - 1)
                    outputs(i - 1)

        @block.vector
        def _(dve):
            def keys(b):
                dve.wait_ge(k_turned, 2 * b + 2)
                dve.wait_ge(k_taken, 2 * b + 1)
                dve.tensor_copy(KT[b % 2][:, 1].rearrange("p a k -> p (a k)"), bank[7][:]).then_inc(k_taken, 1)

            def weigh(i):
                st = stat[i % 2]
                dve.wait_ge(exped, 3 * i + 3)
                dve.tensor_scalar(st[:, 3], st[:, 2], 0.5, None, ALU.max).then_inc(summed, 1)
                dve.wait_ge(summed, 3 * i + 1)
                dve.reciprocal(st[:, 4], st[:, 3]).then_inc(summed, 1)
                dve.wait_ge(summed, 3 * i + 2)
                if i < NP_:
                    p, a, g, qt = items[i]
                    h = (2 * p + a) * G + g
                    gt = L.gate_tok[:, qt, 3 * h:3 * h + 3]
                else:
                    gt = L.gate_rows[:, i - NP_]
                dve.tensor_tensor(st[:, 3], st[:, 4], gt, ALU.mult).then_inc(summed, 1)
                dve.wait_ge(summed, 3 * i + 3)
                w = PR[i % 2]
                dve.tensor_scalar(w[:, 0], w[:, 0], st[:, 3, 1:2], None, ALU.mult)
                dve.tensor_scalar(w[:, 1], w[:, 1], st[:, 3, 2:3], None, ALU.mult)
                dve.tensor_scalar(w[:, 2, PAST:GW], w[:, 2, PAST:GW], st[:, 3, 0:1], None, ALU.mult
                                  ).then_inc(weighed, 1)

            for t in S:
                dve.memset(t[:], NEG).then_inc(filled, 1)
            for p in range(2):
                dve.tensor_copy(q_s[:, p].rearrange("p b (g t) -> p g b t", t=TS),
                                proj[:, T_NQ + 4 * p:T_NQ + 4 * p + 4, TP:T].rearrange("p g (b t) -> p g b t", t=TS)
                                ).then_inc(filled, 1)
            dve.wait_ge(filled, 2)
            for i in range(NI + 1):
                if i < NI:
                    sc, st = S[i % 2], stat[i % 2]
                    if i >= NP_:
                        keys(i - NP_)
                    dve.wait_ge(scored, i + 1)
                    if i >= 2:
                        dve.wait_ge(exped, 3 * (i - 1))
                    if i < NP_:
                        qt = items[i][3]
                        m = L.cst[:, K_CAUSAL + qt * TP:K_CAUSAL + (qt + 1) * TP]
                        m = m.unsqueeze(1).to_broadcast([P, 2, TP])
                        dve.tensor_tensor(sc[:, 0:2, 0:PAST], bank[0][:].rearrange("p (n k) -> p n k", n=2), m,
                                          ALU.add).then_inc(masked, 1)
                        dve.tensor_tensor(sc[:, 2, PAST:GW], bank[1][:, 32:48],
                                          L.cst[:, K_CMP + 16 * qt:K_CMP + 16 * qt + 16], ALU.add
                                          ).then_inc(masked, 1)
                    else:
                        dve.tensor_copy(sc[:, 0:2, 0:PAST], bank[0][:].rearrange("p (n k) -> p n k", n=2)
                                        ).then_inc(masked, 1)
                        dve.tensor_tensor(sc[:, :, PAST:GW], bank[1][:, 0:48].rearrange("p (n k) -> p n k", n=3),
                                          L.cst[:, K_NEW:K_NEW + 48].rearrange("p (n k) -> p n k", n=3), ALU.add
                                          ).then_inc(masked, 1)
                    dve.wait_ge(masked, 2 * i + 2)
                    if i >= 2:
                        dve.wait_ge(weighed, i - 1)
                    dve.tensor_reduce(st[:, 0, 1:3], sc[:, 0:2], AX.X, ALU.max).then_inc(maxed, 1)
                    dve.tensor_reduce(st[:, 0, 0:1], sc[:, 2, PAST:GW], AX.X, ALU.max).then_inc(maxed, 1)
                    dve.wait_ge(maxed, 3 * i + 2)
                    dve.tensor_scalar(st[:, 1], st[:, 0], FLOOR, -(HD ** -0.5), ALU.max, ALU.mult
                                      ).then_inc(maxed, 1)
                if i >= 1:
                    weigh(i - 1)

        @block.scalar
        def _(act):
            def take(i):
                act.wait_ge(turned, i + 1)
                if i >= 2:
                    act.wait_ge(out_ready, i - 1)
                act.activation(PT[i % 2][:, 0:4], bank[2][:].rearrange("p (n k) -> p n k", n=4), ACT.Copy
                               ).then_inc(taken, 1)
                n = 0 if i >= NP_ else 2
                act.activation(PT[i % 2][0:16, 4 + n:7], bank[3][0:16, n * P:3 * P].rearrange("p (n k) -> p n k", k=P),
                               ACT.Copy).then_inc(taken, 1)

            def out(i):
                act.wait_ge(out_ready, i + 1)
                o = bank[4 + i % 2]
                if i < NP_:
                    p, a, g, qt = items[i]
                    r = slice(a * HD, (a + 1) * HD)
                    act.activation(mix[r, 4 * p + g, qt * P:(qt + 1) * P], o[r, 0:P], ACT.Copy
                                   ).then_inc(out_taken, 1)
                else:
                    c = TP + (i - NP_) * TS
                    act.activation(mix[:, :, c:c + TS], o[:, 0:64].rearrange("p (g t) -> p g t", t=TS),
                                   ACT.Copy).then_inc(out_taken, 1)

            for i in range(NI + 2):
                if i < NI:
                    if i >= NP_:
                        b = i - NP_
                        act.wait_ge(k_turned, 2 * b + 1)
                        if b >= 1:
                            act.wait_ge(k_taken, 2 * b)
                        act.activation(KT[b % 2][:, 0].rearrange("p a k -> p (a k)"), bank[6][:], ACT.Copy
                                       ).then_inc(k_taken, 1)
                    act.wait_ge(maxed, 3 * i + 3)
                    if i >= 2:
                        act.wait_ge(turned, i - 1)
                    sc, w, st = S[i % 2], PR[i % 2], stat[i % 2]
                    sl = HD ** -0.5
                    for n in range(2):
                        act.activation(w[:, n], sc[:, n], ACT.Exp, scale=sl, bias=st[:, 1, n + 1:n + 2],
                                       accum_out=st[:, 2, n + 1:n + 2]).then_inc(exped, 1)
                    act.activation(w[:, 2, PAST:GW], sc[:, 2, PAST:GW], ACT.Exp, scale=sl, bias=st[:, 1, 0:1],
                                   accum_out=st[:, 2, 0:1]).then_inc(exped, 1)
                if 1 <= i <= NI:
                    take(i - 1)
                    out(i - 1)


def mix_projection(L):
    nc = L.nc
    w = L.A["w_out"][0]
    gla_rows = w[0:1024].rearrange("(k p) n -> p k n", p=P)
    nsa_rows = w[1024:2048].rearrange("(h a g d) n -> a d h g n", h=2, a=2, g=G)
    q0, y0 = L.q, L.y
    hi_made, lo_made = L.sem("mix_hi"), L.sem("mix_lo")
    NP = KD // 2
    scope = ExitStack()
    with scope:
        part = [L.proj[:, T_GR + a] for a in range(2)]
        with nc.Block() as block:
            @block.sync
            def _(sp):
                with sp.Fori(0, NP) as n:
                    for a in range(2):
                        sp.wait_ge(L.split[a], n + (q0 + 1))
                        cols = bass.ds(n * (2 * P) + a * P, P)
                        raw = L.raw[a][:].rearrange("p (k n) -> p k n", n=P)
                        sp.dma_start(raw[:, 0:8], gla_rows[:, :, cols]).then_inc(L.mixw_loaded[a], 16)
                        for h in range(2):
                            for half in range(2):
                                sp.dma_start(raw[half * HD:(half + 1) * HD, 8 + 4 * h:12 + 4 * h],
                                             nsa_rows[half, :, h, :, cols]).then_inc(L.mixw_loaded[a], 16)

            @block.scalar
            def _(act):
                for k in range(KD):
                    act.activation(L.xh[:, k], mix_tile(L, k), ACT.Copy).then_inc(hi_made, 1)
                with act.Fori(0, NP) as n:
                    take_parts(L, act, part, n + q0, n + y0, 1.0)

            @block.vector
            def _(dve):
                for k in range(KD):
                    dve.wait_ge(hi_made, k + 1)
                    dve.tensor_tensor(L.xl[:, k], mix_tile(L, k), L.xh[:, k].bitcast(F32), ALU.subtract
                                      ).then_inc(lo_made, 1)
                with dve.Fori(0, NP) as n:
                    split_pair(L, dve, n + q0, L.mixw_loaded, 5 * 16, n, KD)

            @block.tensor
            def _(pe):
                pe.wait_ge(lo_made, KD)
                with pe.Fori(0, NP) as n:
                    for a in range(2):
                        multiply_unit(L, pe, n + q0, a, KD, (L.xh, L.xl))

            @block.gpsimd
            def _(pool):
                with pool.Fori(0, NP) as n:
                    add_parts(L, pool, part, n + q0, n)
    L.q += NP
    L.y += NP


def mix_tile(L, k):
    return L.proj[:, T_OG + k] if k < 8 else L.proj[:, T_NQ + k - 8]


def write_outputs(L):
    nc, O, bank = L.nc, L.O, L.bank
    turned, taken = L.sem("y_turned"), L.sem("y_taken")
    y_out = [L.sem(f"y_out{i}") for i in range(2)]
    ident = L.cst[:, K_ID:K_ID + P]
    with ExitStack() as scope:
        y = [L.sb(f"y{i}", [P, D], scope=scope) for i in range(2)]
        with nc.Block() as block:
            @block.tensor
            def _(pe):
                for t in range(3):
                    rows = P if t < 2 else T - TP
                    for c in range(4):
                        i = 4 * t + c
                        if i >= 4:
                            pe.wait_ge(taken, i - 3)
                        for j in range(4):
                            mm = pe.transpose(bank[i % 4][0:rows, j * P:(j + 1) * P],
                                              L.xT[:, 4 * c + j, t * P:t * P + rows], ident)
                        mm.then_inc(turned, 1)

            @block.scalar
            def _(act):
                for t in range(3):
                    rows = P if t < 2 else T - TP
                    for c in range(4):
                        i = 4 * t + c
                        act.wait_ge(turned, i + 1)
                        if t == 2:
                            act.wait_ge(y_out[0], 16)
                        act.activation(y[t % 2][0:rows, c * 512:(c + 1) * 512], bank[i % 4][0:rows, :],
                                       ACT.Copy).then_inc(taken, 1)

            @block.sync
            def _(sp):
                for t in range(3):
                    sp.wait_ge(taken, 4 * t + 4)
                    if t < 2:
                        sp.dma_start(O["y_p"][0, t * P:(t + 1) * P], y[t][:]).then_inc(y_out[t % 2], 16)
                    else:
                        sp.dma_start(O["y_s"].rearrange("b t d -> (b t) d"), y[0][0:T - TP, :]
                                     ).then_inc(y_out[0], 16)
                sp.wait_ge(y_out[0], 32)
                sp.wait_ge(y_out[1], 16)
                sp.wait_ge(L.stored, 16 * L.n_stored)


_INS = ["x_prompt", "x_sample", "cache_cmp_kv", "cache_slc_kv", "cache_win_kv", "state_gla", "page_table",
        "w_ffn1_in", "w_ffn1_out", "w_in", "w_gla_gate2", "b_gla_gate2", "gla_norm_g", "cmp_pos", "cmp_w1",
        "cmp_w2", "w_out", "w_ffn2_in", "w_ffn2_out", "ln_g", "ln_b"]
_OUTS = [("y_p", (1, TP, D)), ("y_s", (NB, TS, D)),
         ("cmp_p", (1, 1, TP, 2, KV, HD)), ("slc_p", (1, 1, TP, 2, KV, HD)), ("win_p", (1, 1, PAST, 2, KV, HD)),
         ("gla_p", (1, 1, GH, P, DV)),
         ("cmp_s", (1, NB, TS, 2, KV, HD)), ("slc_s", (1, NB, TS, 2, KV, HD)), ("win_s", (1, NB, PAST, 2, KV, HD)),
         ("gla_s", (1, NB, GH, P, DV))]


def kernel(**inputs):
    import concourse.bacc as bacc
    from concourse.bass_utils import run_bass_kernel_spmd

    nc = bacc.Bacc("TRN2", target_bir_lowering=False, num_devices=1)
    arrays = {name: np.ascontiguousarray(inputs[name]) for name in _INS}
    arrays["consts"], arrays["levels"] = constants(), level_masks()
    A = {n: nc.dram_tensor("in_" + n, a.shape, mybir.dt.from_np(a.dtype), kind="ExternalInput").ap()
         for n, a in arrays.items()}
    O = {n: nc.dram_tensor("out_" + n, shape, F32, kind="ExternalOutput").ap() for n, shape in _OUTS}
    build(nc, A, O)
    r = run_bass_kernel_spmd(nc, [{"in_" + n: a for n, a in arrays.items()}], core_ids=[0])
    return tuple(r.results[0]["out_" + n] for n, _ in _OUTS)
```

```python
from contextlib import ExitStack

import numpy as np
import concourse.bass as bass
from concourse import mybir
from concourse.alu_op_type import AluOpType as ALU

ACT = mybir.ActivationFunctionType
F32 = mybir.dt.float32
F32R = mybir.dt.float32r
U8 = mybir.dt.uint8
I32 = mybir.dt.int32
AX = mybir.AxisListType

P = 128
D = 2048
KD = D // P
TP, NB, TS = 256, 8, 8
T = TP + NB * TS
PAST, PAGE = 256, 128
NPG = PAST // PAGE
D_FF = 5632
FT = D_FF // P
FC = 11
CH = FT // FC
GH, DV = 4, 256
NH, KV, G, HD = 16, 4, 4, 64
CL, CS = 32, 16
NC = (TP - CL) // CS + 1
assert NC == (PAST + TS - CL) // CS + 1 and (NC - 1) * CS + CL <= PAST
SEL_LEN, SEL_TOPN, WINDOW = 64, 16, 512
assert -(-(PAST + TS) // SEL_LEN) <= SEL_TOPN and TP // SEL_LEN <= SEL_TOPN
assert PAST + TS <= WINDOW
ALPHA = 2.0 ** 0.25
EPS = 1e-5
NEG = -1e30
FLOOR = -5e29
LEVELS = 8
GW = PAST + 16
C_GA, C_GR, C_NQ, C_KV, C_NG = 2048, 2064, 3088, 4112, 5648
T_GQ, T_GK, T_GV, T_GR, T_NQ, T_KV, NT = 0, 4, 8, 16, 24, 32, 44
T_OG = 0
K_ID, K_MEAN, K_RMS, K_ROT, K_COS, K_SIN = 0, 128, 256, 384, 512, 832
K_RESET, K_CAUSAL, K_CMP, K_NEW, K_SEQ = 1152, 1472, 1984, 2016, 2064
K_ALL = 2072


def constants():
    c = np.zeros((P, K_ALL), np.float32)
    c[:, K_ID:K_ID + P] = np.eye(P)
    c[:, K_MEAN:K_MEAN + P] = 1.0 / D
    c[:, K_RMS:K_RMS + P] = 1.0 / DV
    half = HD // 2
    for m in range(P):
        if m % HD < half:
            c[m + half, K_ROT + m] = -1.0
        else:
            c[m - half, K_ROT + m] = 1.0
    pos = np.concatenate([np.arange(TP), np.tile(PAST + np.arange(TS), NB)]).astype(np.float32)
    freq = np.float32(10000.0) ** (-np.arange(half, dtype=np.float32) / np.float32(half))
    ang = (freq.astype(np.float32)[np.arange(P) % half][:, None] * pos[None, :]).astype(np.float32)
    c[:, K_COS:K_COS + T] = np.cos(ang)
    c[:, K_SIN:K_SIN + T] = np.sin(ang)
    c[:, K_RESET:K_RESET + T] = 1.0
    c[:, K_RESET] = 0.0
    c[:, K_RESET + TP:K_RESET + T:TS] = 0.0
    i = np.arange(P)[:, None]
    for qt in range(2):
        j = np.arange(TP)[None, :]
        c[:, K_CAUSAL + qt * TP:K_CAUSAL + (qt + 1) * TP] = np.where(j <= i + qt * P, 0.0, NEG)
        n = np.arange(16)[None, :]
        c[:, K_CMP + qt * 16:K_CMP + qt * 16 + 16] = np.where(
            (n < NC) & (n * CS + CL - 1 <= i + qt * P), 0.0, NEG)
    n = np.arange(16)[None, :]
    own = np.where((n >= 8) & (n - 8 <= i % TS), 0.0, NEG)
    c[:, K_NEW:K_NEW + 16] = own
    c[:, K_NEW + 16:K_NEW + 32] = own
    c[:, K_NEW + 32:K_NEW + 48] = np.where(n < NC, 0.0, NEG)
    for b in range(NB):
        c[b * TS:(b + 1) * TS, K_SEQ + b] = 1.0
    return c


def level_masks():
    m = np.zeros((P, LEVELS, T), np.int32)
    for lv in range(LEVELS):
        for i in range(T):
            r = i % P
            for j in range(P if i < TP else T - TP):
                if i >= TP and lv > 3:
                    continue
                s = 1 << lv
                if lv == 0:
                    m[j, 0, i] = j == r
                elif j // s == r // s and j % s < s // 2 <= r % s:
                    m[j, lv, i] = 1
    return m


class Layer:
    pass



def build(nc, A, O):
    ctx = ExitStack()
    with ctx:
        L = Layer()
        L.nc, L.A, L.O, L.ctx = nc, A, O, ctx
        L.scope = ctx

        def sem(name):
            return ctx.enter_context(nc.semaphore(name))

        def sb(name, shape, dt=F32, scope=None):
            return (scope or ctx).enter_context(nc.sbuf_tensor(name, shape, dt))

        L.sem, L.sb = sem, sb
        L.bank = [ctx.enter_context(nc.psum_tensor(f"bank{i}", [P, 512], F32)) for i in range(8)]
        L.cst = sb("cst", [P, K_ALL])
        L.lvl = sb("lvl", [P, LEVELS, T], U8)
        L.ln_g = sb("ln_g", [P, 3, KD])
        L.ln_b = sb("ln_b", [P, 3, KD])
        L.xT = sb("xT", [P, KD, T])
        L.raw = [sb(f"raw{a}", [P, KD * P]) for a in range(2)]
        L.proj = sb("proj", [P, NT, T])
        L.gate = sb("gate", [P, T])
        L.loaded = [sem(f"loaded{a}") for a in range(2)]
        L.mixw_loaded = [sem(f"mixw_loaded{a}") for a in range(2)]
        L.hi = [sem(f"hi{a}") for a in range(2)]
        L.split = [sem(f"split{a}") for a in range(2)]
        L.multiplied = [sem(f"multiplied{a}") for a in range(2)]
        L.taken = [sem(f"taken{a}") for a in range(2)]
        L.added = [sem(f"added{a}") for a in range(2)]
        L.hidden_made = sem("hidden_made")
        L.cst_loaded = sem("cst_loaded")
        L.stored = sem("stored")
        L.n_stored = 0
        L.q = 0
        L.q_own = 0
        L.y = 0
        L.h = 0

        open_operands(L, "before")
        load_inputs(L)
        ffn(L, "ffn1", "w_ffn1_in", "w_ffn1_out")
        layer_norm(L, 0)
        projection(L)
        L.operands.close()
        with ExitStack() as mixing:
            L.kv_tok = sb("kv_tok", [P, 3, 12 * P], scope=mixing)
            L.gate_tok = sb("gate_tok", [P, 3, 48], scope=mixing)
            with ExitStack() as s:
                L.v_gla = sb("v_gla", [P, 3, GH * DV], scope=s)
                turn_projection(L)
                gla(L, s)
            with ExitStack() as s:
                L.k_cmp = sb("k_cmp", [P, NB + 1, 2, 16], scope=s)
                L.v_small = sb("v_small", [16, 3, NB + 1, 256], scope=s)
                L.gate_rows = sb("gate_rows", [P, NB, 3], scope=s)
                with ExitStack() as s2:
                    compress(L, s2)
                with ExitStack() as s2:
                    attention(L, s2)
        open_operands(L, "after")
        mix_projection(L)
        layer_norm(L, 1)
        ffn(L, "ffn2", "w_ffn2_in", "w_ffn2_out")
        L.operands.close()
        layer_norm(L, 2)
        write_outputs(L)


def open_operands(L, when):
    L.operands = ExitStack()
    L.xh = L.sb("xh_" + when, [P, KD, T], F32R, L.operands)
    L.xl = L.sb("xl_" + when, [P, KD, T], F32R, L.operands)
    L.wh = [L.sb(f"wh{a}_{when}", [P, KD * P], F32R, L.operands) for a in range(2)]
    L.wl = [L.sb(f"wl{a}_{when}", [P, KD * P], F32R, L.operands) for a in range(2)]


def load_inputs(L):
    nc, A, bank = L.nc, L.A, L.bank
    scope = ExitStack()
    with scope:
        x_tok = L.proj[:].rearrange("p k t -> p (k t)")[:, 0:3 * D].rearrange("p (t d) -> p t d", t=3)
        x_loaded, turned, hi_made, bank_free = (
            L.sem("x_loaded"), L.sem("x_turned"), L.sem("x_hi_made"), L.sem("x_bank_free"))
        levels = L.proj[:, 24:32].bitcast(I32)
        levels_loaded = L.sem("levels_loaded")
        ident = L.cst[:, K_ID:K_ID + P]
        with nc.Block() as block:
            @block.sync
            def _(sp):
                sp.dma_start(L.cst[:], A["consts"]).then_inc(L.cst_loaded, 16)
                sp.dma_start(x_tok[:, 0:2, :], A["x_prompt"][0].rearrange("(t p) d -> p t d", p=P)
                             ).then_inc(x_loaded, 16)
                sp.dma_start(x_tok[0:T - TP, 2, :], A["x_sample"].rearrange("b t d -> (b t) d")
                             ).then_inc(x_loaded, 16)
                sp.dma_start(levels, A["levels"]).then_inc(levels_loaded, 16)
                with nc.allow_non_contiguous_dma(reason="small vectors, feature-major"):
                    for n in range(3):
                        sp.dma_start(L.ln_g[:, n, :], A["ln_g"][0, n].rearrange("(k p) -> p k", p=P)
                                     ).then_inc(L.cst_loaded, 16)
                        sp.dma_start(L.ln_b[:, n, :], A["ln_b"][0, n].rearrange("(k p) -> p k", p=P)
                                     ).then_inc(L.cst_loaded, 16)
                sp.wait_ge(L.cst_loaded, 7 * 16)

            @block.gpsimd
            def _(pool):
                pool.wait_ge(levels_loaded, 16)
                pool.tensor_copy(L.lvl[:], levels)

            @block.tensor
            def _(pe):
                pe.wait_ge(L.cst_loaded, 7 * 16)
                pe.wait_ge(x_loaded, 32)
                for k in range(KD):
                    if k >= 4:
                        pe.wait_ge(bank_free, k - 3)
                    for t in range(3):
                        n = P if t < 2 else T - TP
                        last = pe.transpose(bank[k % 4][:, t * P:t * P + n],
                                            x_tok[0:n, t, k * P:(k + 1) * P], ident[0:n, 0:n])
                    last.then_inc(turned, 1)

            @block.scalar
            def _(act):
                for k in range(KD):
                    act.wait_ge(turned, k + 1)
                    act.activation(L.xT[:, k], bank[k % 4][:, 0:T], ACT.Copy, scale=ALPHA)
                    act.activation(L.xh[:, k], bank[k % 4][:, 0:T], ACT.Copy).then_inc(hi_made, 1)

            @block.vector
            def _(dve):
                for a in range(2):
                    for s in (L.split[a], L.multiplied[a], L.taken[a], L.added[a]):
                        dve.sem_inc(s, 1)
                dve.sem_inc(L.hidden_made, 1)
                for k in range(KD):
                    dve.wait_ge(hi_made, k + 1)
                    dve.tensor_tensor(L.xl[:, k], bank[k % 4][:, 0:T], L.xh[:, k].bitcast(F32),
                                      ALU.subtract).then_inc(bank_free, 1)


def multiply_unit(L, pe, q, a, nk, moving, first_wait=None):
    out = L.bank[a][:, 0:T]
    pe.wait_ge(L.split[a], q + 2)
    pe.wait_ge(L.taken[a], q + 1)
    hi, lo = moving
    for k in range(nk):
        if first_wait is not None:
            first_wait(k)
        w = slice(k * P, (k + 1) * P)
        pe.matmul(out, L.wh[a][:, w], hi[:, k], start=(k == 0), stop=False)
        pe.matmul(out, L.wh[a][:, w], lo[:, k], start=False, stop=False)
        last = pe.matmul(out, L.wl[a][:, w], hi[:, k], start=False, stop=(k == nk - 1))
    last.then_inc(L.multiplied[a], 1)


def split_pair(L, dve, q, landed, per, own_q, nk):
    n = nk * P
    for a in range(2):
        dve.wait_ge(landed[a], own_q * per + per)
        dve.wait_ge(L.multiplied[a], q + 1)
        dve.tensor_copy(L.wh[a][:, 0:n], L.raw[a][:, 0:n]).then_inc(L.hi[a], 1)
        dve.wait_ge(L.hi[a], q + 1)
        dve.tensor_tensor(L.wl[a][:, 0:n], L.raw[a][:, 0:n], L.wh[a][:, 0:n].bitcast(F32),
                          ALU.subtract).then_inc(L.split[a], 1)


def load_unit(L, sp, q, a, src, nk):
    sp.wait_ge(L.split[a], q + 1)
    sp.dma_start(L.raw[a][:, 0:nk * P].rearrange("p (k n) -> p k n", n=P), src
                 ).then_inc(L.loaded[a], 16)


def ffn(L, name, w_in, w_out):
    nc = L.nc
    wi = L.A[w_in][0].rearrange("(k p) n -> p k n", p=P)
    wo = L.A[w_out][0].rearrange("(c k p) n -> p (c k) n", p=P, k=FC)
    q0, own0, y0, h0 = L.q, L.q_own, L.y, L.h
    per = FC + KD // 2
    scope = ExitStack()
    with scope:
        hh = L.sb(name + "_hh", [P, FC, T], F32R, scope)
        hl = L.sb(name + "_hl", [P, FC, T], F32R, scope)
        gate, up, hid = (L.proj[:, i] for i in range(3))
        part = [L.proj[:, 3 + a] for a in range(2)]
        product, hi_done = L.sem(name + "_product"), L.sem(name + "_hidden_hi")
        with nc.Block() as block:
            @block.sync
            def _(sp):
                with sp.Fori(0, CH) as c:
                    with sp.Fori(0, FC) as f:
                        for a in range(2):
                            load_unit(L, sp, c * per + f + q0, a,
                                      wi[:, :, bass.ds(c * (FC * P) + f * P + a * D_FF, P)], KD)
                    with sp.Fori(0, KD // 2) as n:
                        for a in range(2):
                            load_unit(L, sp, c * per + n + (FC + q0), a,
                                      wo[:, bass.ds(c * FC, FC), bass.ds(n * (2 * P) + a * P, P)], FC)

            @block.vector
            def _(dve):
                with dve.Fori(0, CH) as c:
                    with dve.Fori(0, FC) as f:
                        split_pair(L, dve, c * per + f + q0, L.loaded, 16, c * per + f + own0, KD)
                    with dve.Fori(0, KD // 2) as n:
                        split_pair(L, dve, c * per + n + (FC + q0), L.loaded, 16,
                                   c * per + n + (FC + own0), FC)

            @block.tensor
            def _(pe):
                with pe.Fori(0, CH) as c:
                    with pe.Fori(0, FC) as f:
                        for a in range(2):
                            multiply_unit(L, pe, c * per + f + q0, a, KD, (L.xh, L.xl))

                    def hidden_there(k):
                        if k == 0:
                            pe.wait_ge(L.hidden_made, c * FC + (FC + h0))
                        if k == FC - 1:
                            pe.wait_ge(L.hidden_made, c * FC + (FC + h0 + 1))

                    with pe.Fori(0, KD // 2) as n:
                        for a in range(2):
                            multiply_unit(L, pe, c * per + n + (FC + q0), a, FC, (hh, hl),
                                          hidden_there if a == 0 else None)

            @block.scalar
            def _(act):
                with act.Fori(0, CH) as c:
                    with act.Fori(0, FC) as f:
                        act.wait_ge(L.multiplied[0], c * per + f + (q0 + 2))
                        act.wait_ge(L.hidden_made, c * FC + f + (h0 + 1))
                        act.activation(gate, L.bank[0][:, 0:T], ACT.Silu).then_inc(L.taken[0], 1)
                        act.wait_ge(L.multiplied[1], c * per + f + (q0 + 2))
                        act.activation(up, L.bank[1][:, 0:T], ACT.Copy).then_inc(L.taken[1], 1)
                    with act.Fori(0, KD // 2) as n:
                        take_parts(L, act, part, c * per + n + (FC + q0), c * (KD // 2) + n + y0, 0.5)

            @block.gpsimd
            def _(pool):
                with pool.Fori(0, CH) as c:
                    with pool.Fori(0, FC) as f:
                        pool.wait_ge(L.taken[0], c * per + f + (q0 + 2))
                        pool.wait_ge(L.taken[1], c * per + f + (q0 + 2))
                        pool.tensor_tensor(hid, gate, up, ALU.mult).then_inc(product, 1)
                        pool.wait_ge(product, c * FC + f + 1)
                        pool.tensor_copy(hh[:, bass.ds(f, 1), :], hid.rearrange("p (o t) -> p o t", o=1)
                                         ).then_inc(hi_done, 1)
                        pool.wait_ge(hi_done, c * FC + f + 1)
                        pool.tensor_tensor(hl[:, bass.ds(f, 1), :], hid.rearrange("p (o t) -> p o t", o=1),
                                           hh[:, bass.ds(f, 1), :].bitcast(F32), ALU.subtract
                                           ).then_inc(L.hidden_made, 1)
                    with pool.Fori(0, KD // 2) as n:
                        add_parts(L, pool, part, c * per + n + (FC + q0), n)
    L.q += CH * per
    L.q_own += CH * per
    L.y += CH * KD // 2
    L.h += FT


def take_parts(L, act, part, q, y, scale):
    for a in range(2):
        act.wait_ge(L.multiplied[a], q + 2)
        act.wait_ge(L.added[a], y + 1)
        act.activation(part[a], L.bank[a][:, 0:T], ACT.Copy, scale=scale).then_inc(L.taken[a], 1)


def add_parts(L, pool, part, q, n):
    for a in range(2):
        pool.wait_ge(L.taken[a], q + 2)
        x = L.xT[:, bass.ds(n * 2 + a, 1), :]
        pool.tensor_tensor(x, x, part[a].rearrange("p (o t) -> p o t", o=1), ALU.add
                           ).then_inc(L.added[a], 1)


def rsqrt_steps(L, act, dve, var, work, done, n0, part):
    v, r, t = work[:, 0], work[:, 1], work[:, 2]
    if part == 0:
        dve.tensor_scalar(v, var, EPS, None, ALU.add).then_inc(done, 1)
    if part == 1:
        act.wait_ge(done, n0 + 1)
        act.activation(t, v, ACT.Sqrt).then_inc(done, 1)
    if part == 2:
        steps = [
            lambda: dve.reciprocal(r, t),
            lambda: dve.tensor_tensor(t, v, r, ALU.mult),
            lambda: dve.tensor_tensor(t, t, r, ALU.mult),
            lambda: dve.tensor_scalar(t, t, -0.5, 1.5, ALU.mult, ALU.add),
            lambda: dve.tensor_tensor(r, r, t, ALU.mult),
        ]
        for i, s in enumerate(steps):
            dve.wait_ge(done, n0 + 2 + i)
            s().then_inc(done, 1)
        dve.wait_ge(done, n0 + 7)


def layer_norm(L, n):
    nc, bank, xT = L.nc, L.bank, L.xT
    last = n == 2
    mean_ready, centred, squared, summed, root, scaled, shifted, hi_made, lo_made, kept, warm = (
        L.sem(f"ln{n}_{s}") for s in ("mean", "centred", "squared", "summed", "root", "scaled",
                                     "shifted", "hi", "lo", "kept", "warm"))
    ones = L.cst[:, K_MEAN:K_MEAN + P]
    scope = ExitStack()
    with scope:
        sq, z, work = L.proj[:, 0:4], L.proj[:, 4:8], L.proj[:, 8:11]
        with nc.Block() as block:
            @block.tensor
            def _(pe):
                for k in range(KD):
                    mm = pe.matmul(bank[2][:, 0:T], ones, xT[:, k], start=(k == 0), stop=(k == KD - 1))
                mm.then_inc(mean_ready, 1)
                for k in range(KD):
                    pe.wait_ge(squared, k + 1)
                    pe.matmul(bank[3][:, 0:T], ones, sq[:, k % 4], start=(k == 0),
                              stop=(k == KD - 1)).then_inc(summed, 1)

            @block.scalar
            def _(act):
                for k in range(KD):
                    act.wait_ge(centred, k + 1)
                    if k >= 4:
                        act.wait_ge(summed, k - 3)
                    act.activation(sq[:, k % 4], xT[:, k], ACT.Square).then_inc(squared, 1)
                rsqrt_steps(L, act, None, None, work, root, 0, 1)
                for k in range(KD):
                    act.wait_ge(scaled, k + 1)
                    if not last and k >= 4:
                        act.wait_ge(lo_made, k - 3)
                        act.wait_ge(kept, k - 3)
                    out = xT[:, k] if last else z[:, k % 4]
                    act.activation(out, xT[:, k], ACT.Identity, scale=L.ln_g[:, n, k:k + 1],
                                   bias=L.ln_b[:, n, k:k + 1]).then_inc(shifted, 1)
                    if not last:
                        act.wait_ge(shifted, k + 1)
                        act.activation(L.xh[:, k], z[:, k % 4], ACT.Copy).then_inc(hi_made, 1)

            @block.vector
            def _(dve):
                dve.wait_ge(mean_ready, 1)
                for k in range(KD):
                    dve.tensor_tensor(xT[:, k], xT[:, k], bank[2][:, 0:T], ALU.subtract
                                      ).then_inc(centred, 1)
                dve.wait_ge(summed, KD)
                rsqrt_steps(L, None, dve, bank[3][:, 0:T], work, root, 0, 0)
                rsqrt_steps(L, None, dve, None, work, root, 0, 2)

                def lo(k):
                    dve.wait_ge(hi_made, k + 1)
                    dve.tensor_tensor(L.xl[:, k], z[:, k % 4], L.xh[:, k].bitcast(F32), ALU.subtract
                                      ).then_inc(lo_made, 1)

                for k in range(KD):
                    dve.tensor_tensor(xT[:, k], xT[:, k], work[:, 1], ALU.mult).then_inc(scaled, 1)
                    if not last and k >= 2:
                        lo(k - 2)
                if not last:
                    lo(KD - 2)
                    lo(KD - 1)

            @block.gpsimd
            def _(pool):
                if not last:
                    for k in range(KD):
                        pool.wait_ge(shifted, k + 1)
                        pool.tensor_scalar(xT[:, k], z[:, k % 4], ALPHA, None, ALU.mult
                                           ).then_inc(kept, 1)


def projection(L):
    nc = L.nc
    w = L.A["w_in"][0]
    seg_a = w[:, 0:C_GA].rearrange("(k p) n -> p k n", p=P)
    seg_r = w[:, C_GR:C_NQ].rearrange("(k p) n -> p k n", p=P)
    seg_q = [w[:, C_NQ + u * G * HD:C_KV].rearrange("(k p) n -> p k n", p=P) for u in range(2)]
    seg_kv = w[:, C_KV:C_NG].rearrange("(k p) n -> p k n", p=P)
    w_rows = w.rearrange("(k p) n -> p k n", p=P)
    q0, own0 = L.q, L.q_own
    NP = NT // 2
    q_loaded = [L.sem(f"q_loaded{a}") for a in range(2)]
    small_loaded, small_mult = L.sem("gates_w_loaded"), L.sem("gates_mult")
    small_taken = L.sem("gates_taken")
    scope = ExitStack()
    with scope:
        w_small = L.sb("w_small", [P, KD, 80], scope=scope)
        cleared = L.sem("w_small_cleared")
        with nc.Block() as block:
            @block.sync
            def _(sp):
                sp.wait_ge(cleared, 1)
                sp.dma_start(w_small[:, :, 0:48], w_rows[:, :, C_NG:C_NG + 48]).then_inc(small_loaded, 16)
                sp.dma_start(w_small[:, :, 64:80], w_rows[:, :, C_GA:C_GA + 16]).then_inc(small_loaded, 16)

                def segment(src, pairs, at):
                    with sp.Fori(0, pairs) as i:
                        for a in range(2):
                            load_unit(L, sp, i + (q0 + at), a, src[:, :, bass.ds(i * (2 * P) + a * P, P)], KD)

                segment(seg_a, 8, 0)
                segment(seg_r, 4, 8)
                with sp.Fori(0, 2) as h:
                    with sp.Fori(0, 2) as gg:
                        for a in range(2):
                            sp.wait_ge(L.split[a], h * 2 + gg + (q0 + 12 + 1))
                            to = L.raw[a][:].rearrange("p (k u d) -> p k u d", u=2, d=HD)
                            for u in range(2):
                                sp.dma_start(to[:, :, u], seg_q[u][:, :, bass.ds(h * (8 * HD) + gg * (2 * HD) + a * HD, HD)]
                                             ).then_inc(q_loaded[a], 16)
                segment(seg_kv, 6, 16)

            @block.vector
            def _(dve):
                dve.memset(w_small[:], 0.0).then_inc(cleared, 1)
                with dve.Fori(0, 12) as i:
                    split_pair(L, dve, i + q0, L.loaded, 16, i + own0, KD)
                with dve.Fori(0, 4) as i:
                    split_pair(L, dve, i + (q0 + 12), q_loaded, 32, i, KD)
                with dve.Fori(0, 6) as i:
                    split_pair(L, dve, i + (q0 + 16), L.loaded, 16, i + (own0 + 12), KD)

            @block.tensor
            def _(pe):
                with pe.Fori(0, NP) as i:
                    for a in range(2):
                        multiply_unit(L, pe, i + q0, a, KD, (L.xh, L.xl))
                pe.wait_ge(small_loaded, 32)
                for k in range(KD):
                    mm = pe.matmul(L.bank[2][0:80, 0:T], w_small[:, k], L.xT[:, k],
                                   start=(k == 0), stop=(k == KD - 1))
                mm.then_inc(small_mult, 1)

            @block.scalar
            def _(act):
                with act.Fori(0, NP) as i:
                    for a in range(2):
                        act.wait_ge(L.multiplied[a], i + (q0 + 2))
                        act.activation(L.proj[:, bass.ds(i * 2 + a, 1), :],
                                       L.bank[a][:, 0:T].rearrange("p (o t) -> p o t", o=1),
                                       ACT.Copy).then_inc(L.taken[a], 1)
                act.wait_ge(small_mult, 1)
                act.activation(L.gate[64:80], L.bank[2][64:80, 0:T], ACT.Copy, scale=1.0 / ALPHA)
                act.activation(L.gate[0:48], L.bank[2][0:48, 0:T], ACT.Sigmoid, scale=1.0 / ALPHA
                               ).then_inc(small_taken, 1)
    L.q += NP
    L.q_own += NP - 4


def turn_projection(L):
    nc, A, O, bank, proj = L.nc, L.A, L.O, L.bank, L.proj
    roped = [T_NQ + i for i in range(8)] + [T_KV + i for i in (0, 1, 4, 5, 8, 9)]
    NR = len(roped)
    ident = L.cst[:, K_ID:K_ID + P]
    rotated, by_cos, by_sin, rope_done = (L.sem("rope_" + s) for s in ("rotated", "cos", "sin", "done"))
    turned, turned_out = L.sem("turned"), L.sem("turned_out")
    L.kv_stored = L.sem("kv_stored")
    jobs = [("v", t, n) for t in range(3) for n in range(2)] + \
           [("kv", t, n) for t in range(3) for n in range(3)] + [("g", t, 0) for t in range(3)]
    with ExitStack() as scope:
        xc = L.sb("rope_xc", [P, 2, T], scope=scope)
        xs = L.sb("rope_xs", [P, 2, T], scope=scope)
        with nc.Block() as block:
            @block.tensor
            def _(pe):
                for i, t in enumerate(roped):
                    if i >= 2:
                        pe.wait_ge(by_sin, i - 1)
                    pe.matmul(bank[i % 2][:, 0:T], L.cst[:, K_ROT:K_ROT + P], proj[:, t],
                              start=True, stop=True).then_inc(rotated, 1)
                for i, (what, t, n) in enumerate(jobs):
                    if i >= 4:
                        pe.wait_ge(turned_out, i - 3)
                    if i == 6:
                        pe.wait_ge(rope_done, NR)
                    rows = P if t < 2 else T - TP
                    b = bank[2 + i % 4]
                    if what == "g":
                        mm = pe.transpose(b[0:rows, 0:48], L.gate[0:48, t * P:t * P + rows],
                                          ident[0:48, 0:48])
                    else:
                        base = (T_GV if what == "v" else T_KV) + 4 * n
                        for j in range(4):
                            mm = pe.transpose(b[0:rows, j * P:(j + 1) * P],
                                              proj[:, base + j, t * P:t * P + rows], ident)
                    mm.then_inc(turned, 1)

            @block.scalar
            def _(act):
                for i, (what, t, n) in enumerate(jobs):
                    act.wait_ge(turned, i + 1)
                    rows = P if t < 2 else T - TP
                    b = bank[2 + i % 4]
                    if what == "g":
                        act.activation(L.gate_tok[0:rows, t], b[0:rows, 0:48], ACT.Copy).then_inc(turned_out, 1)
                    else:
                        to = L.v_gla if what == "v" else L.kv_tok
                        act.activation(to[0:rows, t, n * 512:(n + 1) * 512], b[0:rows, :], ACT.Copy
                                       ).then_inc(turned_out, 1)

            @block.gpsimd
            def _(pool):
                for i, t in enumerate(roped):
                    if i >= 2:
                        pool.wait_ge(rope_done, i - 1)
                    pool.tensor_tensor(xc[:, i % 2], proj[:, t], L.cst[:, K_COS:K_COS + T], ALU.mult
                                       ).then_inc(by_cos, 1)

            @block.vector
            def _(dve):
                for i, t in enumerate(roped):
                    dve.wait_ge(rotated, i + 1)
                    dve.tensor_tensor(xs[:, i % 2], bank[i % 2][:, 0:T], L.cst[:, K_SIN:K_SIN + T],
                                      ALU.mult).then_inc(by_sin, 1)
                    dve.wait_ge(by_sin, i + 1)
                    dve.wait_ge(by_cos, i + 1)
                    dve.tensor_tensor(proj[:, t], xc[:, i % 2], xs[:, i % 2], ALU.add
                                      ).then_inc(rope_done, 1)

            @block.sync
            def _(sp):
                sp.dma_start(O["win_s"][0, :, 0:PAST - TS].rearrange("b r s k d -> b r (s k d)"),
                             A["cache_win_kv"][0, :, TS:PAST].rearrange("b r s k d -> b r (s k d)")
                             ).then_inc(L.stored, 16)
                L.n_stored += 1
                for t in range(3):
                    for n, what in enumerate(("cmp", "slc", "win")):
                        sp.wait_ge(turned_out, 6 + 3 * t + n + 1)
                        if t < 2:
                            dst = O[what + "_p"][0, 0, t * P:(t + 1) * P].rearrange("r s k d -> r (s k d)")
                            src = L.kv_tok[:, t, n * 512:(n + 1) * 512]
                            sp.dma_start(dst, src).then_inc(L.kv_stored, 16)
                        elif what != "win":
                            dst = O[what + "_s"][0].rearrange("b t s k d -> (b t) (s k d)")
                            sp.dma_start(dst, L.kv_tok[0:64, 2, n * 512:(n + 1) * 512]
                                         ).then_inc(L.kv_stored, 16)
                        else:
                            for b in range(NB):
                                dst = O["win_s"][0, b, PAST - TS:PAST].rearrange("t s k d -> t (s k d)")
                                sp.dma_start(dst, L.kv_tok[b * TS:(b + 1) * TS, 2, 1024:1536]
                                             ).then_inc(L.kv_stored, 16)
                sp.wait_ge(L.kv_stored, 16 * (6 + 2 + NB))


class Chain:

    def __init__(self, eng, sem):
        self.eng, self.sem, self.n = eng, sem, 0

    def __call__(self, ins):
        self.n += 1
        ins.then_inc(self.sem, 1)

    def settle(self):
        self.eng.wait_ge(self.sem, self.n)


def gla(L, s):
    nc, A, O, bank, proj = L.nc, L.A, L.O, L.bank, L.proj
    TT = GH * T
    NS = NB * TS
    gw2 = L.sb("gw2", [P, GH * P], scope=s)
    gb2 = L.sb("gb2", [P, GH], scope=s)
    norm_g = L.sb("norm_g", [P, 2], scope=s)
    B = L.sb("decay", [P, GH, T], scope=s)
    EE = L.sb("decay_e", [P, 2, GH, T], scope=s)
    E, E2 = EE[:, 0], EE[:, 1]
    three = L.sb("gla_three", [P, 3, GH, T], scope=s)
    QL, KL, att = three[:, 0], three[:, 1], three[:, 2]
    attx = L.sb("gla_attx", [P, GH, P], scope=s)
    k_tok = L.sb("k_tok", [P, 3, GH * P], scope=s)
    q = proj[:, T_GQ:T_GQ + GH]
    k = proj[:, T_GK:T_GK + GH]
    ident = L.cst[:, K_ID:K_ID + P]
    w_loaded = L.sem("gla_w_loaded")
    logit, biased, dve_s, act_s, pool_s = (L.sem("gla_" + x) for x in
                                           ("logit", "biased", "dve", "act", "pool"))
    with nc.Block() as block:
        @block.sync
        def _(sp):
            sp.dma_start(gw2[64:80], A["w_gla_gate2"][0]).then_inc(w_loaded, 16)
            with nc.allow_non_contiguous_dma(reason="small vectors, feature-major"):
                sp.dma_start(gb2[:], A["b_gla_gate2"][0].rearrange("(h p) -> p h", p=P)).then_inc(w_loaded, 16)
                sp.dma_start(norm_g[:], A["gla_norm_g"][0].rearrange("(h p) -> p h", p=P)).then_inc(w_loaded, 16)

        @block.tensor
        def _(pe):
            pe.wait_ge(w_loaded, 48)
            for h in range(GH):
                pe.matmul(bank[h][:, 0:T], gw2[64:80, h * P:(h + 1) * P], L.gate[64:80, :],
                          start=True, stop=True).then_inc(logit, 1)

        @block.scalar
        def _(act):
            act.wait_ge(w_loaded, 48)
            for h in range(GH):
                act.wait_ge(logit, h + 1)
                act.activation(B[:, h], bank[h][:, 0:T], ACT.Identity, bias=gb2[:, h:h + 1]).then_inc(biased, 1)
            act.wait_ge(biased, GH)
            act.activation(E, B[:], ACT.Abs).then_inc(act_s, 1)
            act.wait_ge(act_s, 1)
            act.activation(E, E, ACT.Exp, scale=-1.0).then_inc(act_s, 1)
            act.wait_ge(act_s, 2)
            act.activation(E, E, ACT.Ln, bias=1.0).then_inc(act_s, 1)

        @block.vector
        def _(dve):
            dve.wait_ge(biased, GH)
            dve.wait_ge(act_s, 1)
            dve.tensor_scalar(B[:], B[:], 0.0, None, ALU.min).then_inc(dve_s, 1)
            dve.wait_ge(act_s, 3)
            dve.wait_ge(dve_s, 1)
            dve.tensor_tensor(B[:], B[:], E, ALU.subtract).then_inc(dve_s, 1)
            dve.wait_ge(dve_s, 2)
            dve.tensor_scalar(E, B[:], 1.0 / 16.0, None, ALU.mult).then_inc(dve_s, 1)
            dve.wait_ge(dve_s, 3)
            for h in range(GH):
                dve.tensor_tensor_scan(B[:, h], L.cst[:, K_RESET:K_RESET + T], E[:, h], 0.0,
                                       ALU.mult, ALU.add).then_inc(dve_s, 1)
            dve.tensor_scalar(proj[:, T_GQ:T_GQ + GH], proj[:, T_GQ:T_GQ + GH], P ** -0.5, None, ALU.mult
                              ).then_inc(dve_s, 1)

    diff, made_e, made_q, made_k, scored, merged = (L.sem("gla_lv_" + x) for x in
                                                    ("diff", "e", "q", "k", "scored", "merged"))
    made_abs = L.sem("gla_lv_abs")
    with nc.Block() as block:
        @block.vector
        def _(dve):
            dve.memset(att, 0.0).then_inc(merged, 1)
            for lv in range(LEVELS + 1):
                if lv > 0:
                    S = 1 << lv
                    if lv >= 2:
                        dve.wait_ge(made_e, lv - 1)
                    if lv <= 6:
                        v = B[:].rearrange("p h (n s) -> p (h n) s", s=S)
                        e = E.rearrange("p h (n s) -> p (h n) s", s=S)
                        r = v[:, :, S // 2 - 1:S // 2].to_broadcast([P, GH * T // S, S])
                        ins = dve.tensor_tensor(e, v, r, ALU.subtract)
                    else:
                        for h in range(GH):
                            v = B[:, h, 0:TP].rearrange("p (n s) -> p n s", s=S)
                            e = E[:, h, 0:TP].rearrange("p (n s) -> p n s", s=S)
                            r = v[:, :, S // 2 - 1:S // 2].to_broadcast([P, TP // S, S])
                            ins = dve.tensor_tensor(e, v, r, ALU.subtract)
                    ins.then_inc(diff, 1)
                    dve.wait_ge(made_e, lv)
                    if lv >= 1:
                        dve.wait_ge(scored, GH * lv)
                    dve.tensor_tensor(QL, q, E2, ALU.mult).then_inc(made_q, 1)
                for h in range(GH):
                    dve.wait_ge(scored, GH * lv + h + 1)
                    b = bank[(GH * lv + h) % 8]
                    dve.wait_ge(merged, 1 + (GH * lv + h))
                    if lv == LEVELS:
                        dve.tensor_copy(attx[:, h], b[:, 0:P]).then_inc(merged, 1)
                    elif lv <= 3:
                        dve.copy_predicated(att[:, h, 0:TP], L.lvl[:, lv, 0:TP], b[:, 0:TP])
                        dve.copy_predicated(att[0:NS, h, TP:T], L.lvl[0:NS, lv, TP:T], b[0:NS, TP:T]
                                            ).then_inc(merged, 1)
                    else:
                        dve.copy_predicated(att[:, h, 0:TP], L.lvl[:, lv, 0:TP], b[:, 0:TP]
                                            ).then_inc(merged, 1)

        @block.scalar
        def _(act):
            for lv in range(1, LEVELS + 1):
                act.wait_ge(diff, lv)
                if lv >= 2:
                    act.wait_ge(made_q, lv - 1)
                    act.wait_ge(made_k, lv - 1)
                act.activation(E, E, ACT.Abs).then_inc(made_abs, 1)
                act.wait_ge(made_abs, lv)
                act.activation(E2, E, ACT.Exp, scale=-1.0).then_inc(made_e, 1)

        @block.gpsimd
        def _(pool):
            for lv in range(1, LEVELS + 1):
                pool.wait_ge(made_e, lv)
                pool.wait_ge(scored, GH * lv)
                pool.tensor_tensor(KL, k, E2, ALU.mult).then_inc(made_k, 1)

        @block.tensor
        def _(pe):
            for lv in range(LEVELS + 1):
                ql, kl = (QL, KL) if lv else (q, k)
                if lv:
                    pe.wait_ge(made_q, lv)
                    pe.wait_ge(made_k, lv)
                for h in range(GH):
                    n = GH * lv + h
                    b = bank[n % 8]
                    if n >= 8:
                        pe.wait_ge(merged, 1 + n - 7)
                    if lv == LEVELS:
                        mm = pe.matmul(b[:, 0:P], kl[:, h, 0:P], ql[:, h, P:TP], start=True, stop=True)
                    else:
                        for t in range(3 if lv <= 3 else 2):
                            rows = P if t < 2 else NS
                            c = slice(t * P, t * P + rows)
                            mm = pe.matmul(b[0:rows, c], kl[:, h, c], ql[:, h, c], start=True, stop=True)
                    mm.then_inc(scored, 1)

    decayed, eb_made, q_in, k_out, turned, k_tok_made, o_ready, o_taken = (
        L.sem("gla_o_" + x) for x in ("decayed", "eb", "q_in", "k_out", "turned", "k_tok", "ready", "taken"))
    v_made, st_mult, st_made, sp_ready, sp_taken, joined, squared, ms_ready = (
        L.sem("gla_s_" + x) for x in ("v", "mult", "made", "p_ready", "p_taken", "joined", "squared", "ms"))
    st_in = [L.sem(f"state_in{i}") for i in range(2)]
    st_out = [L.sem(f"state_out{i}") for i in range(2)]
    s0 = [L.raw[0][:, i * 1024:(i + 1) * 1024].rearrange("p (h v) -> p h v", h=GH) for i in range(2)]
    s_new = [L.raw[1][:, i * 1024:(i + 1) * 1024].rearrange("p (h v) -> p h v", h=GH) for i in range(2)]
    v_one = [L.sb(f"v_one{i}", [64, GH * DV], scope=s) for i in range(2)]
    s_prompt = L.sb("s_prompt", [P, GH, DV], scope=s)
    last_e = L.sb("last_e", [P, GH, NB], scope=s)
    og = proj[:, T_GV:T_GV + 2 * GH]
    sq = L.sb("gla_sq", [P, 2 * GH, T], scope=s)
    inter = bank[4]
    ms_bank = [bank[i] for i in (2, 3, 6, 7)]
    with nc.Block() as block:
        @block.vector
        def _(dve):
            for h in range(GH):
                dve.tensor_tensor(E[:, h, 0:TP], B[:, h, TP - 1:TP].to_broadcast([P, TP]),
                                  B[:, h, 0:TP], ALU.subtract).then_inc(decayed, 1)
                v = B[:, h, TP:T].rearrange("p (n s) -> p n s", s=TS)
                dve.tensor_tensor(E[:, h, TP:T].rearrange("p (n s) -> p n s", s=TS),
                                  v[:, :, TS - 1:TS].to_broadcast([P, NB, TS]), v, ALU.subtract
                                  ).then_inc(decayed, 1)
            dve.wait_ge(eb_made, 1)
            dve.tensor_tensor(KL, k, E2, ALU.mult).then_inc(k_out, 1)
            dve.wait_ge(eb_made, 2)
            dve.tensor_tensor(QL[:, :, TP:T], q[:, :, TP:T], E[:, :, TP:T], ALU.mult).then_inc(q_in, 1)
            dve.tensor_copy(last_e[:], E[:, :, TP + TS - 1:T:TS]).then_inc(q_in, 1)
            dve.wait_ge(q_in, 2)
            for b in range(NB):
                if b >= 2:
                    dve.wait_ge(st_mult, GH * (b - 1))
                dve.tensor_scalar(v_one[b % 2][:], L.v_gla[0:64, 2], L.cst[0:64, K_SEQ + b:K_SEQ + b + 1],
                                  None, ALU.mult).then_inc(v_made, 1)
                if b >= 2:
                    dve.wait_ge(st_out[b % 2], 16 * (b // 2))
                dve.wait_ge(st_in[b % 2], 16 * (b // 2 + 1))
                for h in range(GH):
                    dve.wait_ge(st_mult, GH * b + h + 1)
                    dve.scalar_tensor_tensor(out=s_new[b % 2][:, h], in0=s0[b % 2][:, h],
                                             scalar=last_e[:, h, b:b + 1],
                                             in1=bank[5 + h % 2][:, 0:DV], op0=ALU.mult, op1=ALU.add
                                             ).then_inc(st_made, 1)
            dve.wait_ge(o_taken, 2 * GH)
            for n in range(2 * GH):
                o = og[:, n, TP:T].rearrange("p (b t) -> p b t", t=TS)
                dve.tensor_tensor(o, o, inter[:].rearrange("p (b n t) -> p n b t", n=2 * GH, t=TS)[:, n],
                                  ALU.add).then_inc(joined, 1)

        @block.scalar
        def _(act):
            act.wait_ge(decayed, 2 * GH)
            act.activation(E2, E, ACT.Exp).then_inc(eb_made, 1)
            act.wait_ge(eb_made, 1)
            act.activation(E[:, :, TP:T], B[:, :, TP:T], ACT.Exp).then_inc(eb_made, 1)
            for t in range(3):
                rows = P if t < 2 else NS
                act.wait_ge(turned, t + 1)
                act.activation(k_tok[0:rows, t], bank[t][0:rows, :], ACT.Copy).then_inc(k_tok_made, 1)
            for n in range(2 * GH):
                act.wait_ge(o_ready, n + 1)
                act.activation(og[:, n], bank[n % 4][:, 0:T], ACT.Copy).then_inc(o_taken, 1)
            for i in range(2):
                act.wait_ge(sp_ready, i + 1)
                act.activation(s_prompt[:, 2 * i:2 * i + 2], bank[i][:].rearrange("p (h v) -> p h v", h=2),
                               ACT.Copy).then_inc(sp_taken, 1)
            act.wait_ge(joined, 2 * GH)
            act.activation(sq[:], og, ACT.Square).then_inc(squared, 1)

        @block.sync
        def _(sp):
            for b in range(NB):
                if b >= 2:
                    sp.wait_ge(st_made, GH * (b - 1))
                sp.dma_start(s0[b % 2], A["state_gla"][0, b].rearrange("h k v -> k h v")
                             ).then_inc(st_in[b % 2], 16)
                if b >= 1:
                    sp.wait_ge(st_made, GH * b)
                    sp.dma_start(O["gla_s"][0, b - 1].rearrange("h k v -> k h v"), s_new[(b - 1) % 2]
                                 ).then_inc(st_out[(b - 1) % 2], 16)
            sp.wait_ge(st_made, GH * NB)
            sp.dma_start(O["gla_s"][0, NB - 1].rearrange("h k v -> k h v"), s_new[(NB - 1) % 2]
                         ).then_inc(st_out[(NB - 1) % 2], 16)
            sp.wait_ge(sp_taken, 2)
            sp.dma_start(O["gla_p"][0, 0].rearrange("h k v -> k h v"), s_prompt[:]).then_inc(L.stored, 16)
            L.n_stored += 1
            for i in range(2):
                sp.wait_ge(st_out[i], 16 * NB // 2)
            sp.wait_ge(L.stored, 16 * L.n_stored)

        @block.tensor
        def _(pe):
            pe.wait_ge(k_out, 1)
            for t in range(3):
                rows = P if t < 2 else NS
                for h in range(GH):
                    mm = pe.transpose(bank[t][0:rows, h * P:(h + 1) * P], KL[:, h, t * P:t * P + rows], ident)
                mm.then_inc(turned, 1)
            pe.wait_ge(k_tok_made, 3)
            for n in range(2 * GH):
                h, c = n // 2, n % 2
                b = bank[n % 4]
                vc = slice(h * DV + c * P, h * DV + (c + 1) * P)
                if n >= 4:
                    pe.wait_ge(o_taken, n - 3)
                pe.matmul(b[:, 0:P], L.v_gla[:, 0, vc], att[:, h, 0:P], start=True, stop=False,
                          skip_group_check=True)
                pe.matmul(b[:, P:TP], L.v_gla[:, 0, vc], attx[:, h], start=False, stop=False,
                          skip_group_check=True)
                pe.matmul(b[:, P:TP], L.v_gla[:, 1, vc], att[:, h, P:TP], start=False, stop=False,
                          skip_group_check=True)
                pe.matmul(b[:, TP:T], L.v_gla[0:NS, 2, vc], att[0:NS, h, TP:T], start=False, stop=True,
                          skip_group_check=True).then_inc(o_ready, 1)
            pe.wait_ge(q_in, 2)
            for b in range(NB):
                pe.wait_ge(st_in[b % 2], 16 * (b // 2 + 1))
                for n in range(2 * GH):
                    h, c = n // 2, n % 2
                    at = (b * 2 * GH + n) * TS
                    pe.matmul(inter[:, at:at + TS], s0[b % 2][:, h, c * P:(c + 1) * P],
                              QL[:, h, TP + b * TS:TP + (b + 1) * TS], start=True, stop=True)
                pe.wait_ge(v_made, b + 1)
                for h in range(GH):
                    if b * GH + h >= 2:
                        pe.wait_ge(st_made, b * GH + h - 1)
                    pe.matmul(bank[5 + h % 2][:, 0:DV], k_tok[0:NS, 2, h * P:(h + 1) * P],
                              v_one[b % 2][:, h * DV:(h + 1) * DV], start=True, stop=True
                              ).then_inc(st_mult, 1)
            pe.wait_ge(o_taken, 2 * GH)
            for h in range(GH):
                for t in range(2):
                    mm = pe.matmul(bank[h // 2][:, (h % 2) * DV:(h % 2 + 1) * DV],
                                   k_tok[:, t, h * P:(h + 1) * P], L.v_gla[:, t, h * DV:(h + 1) * DV],
                                   start=(t == 0), stop=(t == 1))
                if h % 2:
                    mm.then_inc(sp_ready, 1)
            pe.wait_ge(squared, 1)
            pe.wait_ge(st_made, GH * NB)
            for h in range(GH):
                for c in range(2):
                    mm = pe.matmul(ms_bank[h][:, 0:T], L.cst[:, K_RMS:K_RMS + P], sq[:, 2 * h + c],
                                   start=(c == 0), stop=(c == 1))
            mm.then_inc(ms_ready, 1)

    v, r, t = QL, KL, att
    nd, na, silu = L.sem("gla_n_dve"), L.sem("gla_n_root"), L.sem("gla_n_silu")
    with nc.Block() as block:
        @block.scalar
        def _(act):
            act.wait_ge(nd, GH)
            act.activation(t, v, ACT.Sqrt).then_inc(na, 1)
            act.activation(sq[:], proj[:, T_GR:T_GR + 2 * GH], ACT.Silu).then_inc(silu, 1)

        @block.vector
        def _(dve):
            ch = Chain(dve, nd)
            for h in range(GH):
                ch(dve.tensor_scalar(v[:, h], ms_bank[h][:, 0:T], EPS, None, ALU.add))
            dve.wait_ge(na, 1)
            for step in (lambda: dve.reciprocal(r, t),
                         lambda: dve.tensor_tensor(t, v, r, ALU.mult),
                         lambda: dve.tensor_tensor(t, t, r, ALU.mult),
                         lambda: dve.tensor_scalar(t, t, -0.5, 1.5, ALU.mult, ALU.add),
                         lambda: dve.tensor_tensor(r, r, t, ALU.mult)):
                ch.settle()
                ch(step())
            ch.settle()
            for n in range(2 * GH):
                ch(dve.tensor_tensor(og[:, n], og[:, n], r[:, n // 2], ALU.mult))
            ch.settle()
            dve.wait_ge(silu, 1)
            for n in range(2 * GH):
                ch(dve.scalar_tensor_tensor(out=proj[:, T_OG + n], in0=og[:, n], scalar=norm_g[:, n % 2:n % 2 + 1],
                                            in1=sq[:, n], op0=ALU.mult, op1=ALU.mult))
            ch.settle()


def compress(L, s):
    nc, A, O, bank = L.nc, L.A, L.O, L.bank
    NQ = NB + 1
    LT = CL // 2
    ident = L.cst[:, K_ID:K_ID + P]
    rows = [L.sb(f"cmp_rows{i}", [P, 2, KV, 2, HD], scope=s) for i in range(2)]
    R = [L.sb(f"cmp_turned{n}", [P, NQ, KV, P], scope=s) for n in range(2)]
    w1 = [L.raw[n][:].rearrange("p (l m) -> p l m", m=P) for n in range(2)]
    w2 = L.sb("cmp_w2", [P, 2, HD], scope=s)
    pos = L.sb("cmp_pos_rows", [32, P], scope=s)
    posT = L.sb("cmp_pos_cols", [P, 32], scope=s)
    bias = L.sb("cmp_bias", [P, 2], scope=s)
    hid = [L.sb(f"cmp_hid{n}", [P, NQ, KV, NC], scope=s) for n in range(2)]
    table = L.sb("table", [1, NB * NPG], I32, scope=s)
    scratch = nc.dram_tensor("gate_scratch", [NB * TS, 48], F32, kind="Internal").ap()
    w_in, table_in, gate_out, small_in = (L.sem("cmp_" + x) for x in ("w", "table", "gate", "small"))
    rows_in = [L.sem(f"cmp_rows_in{i}") for i in range(2)]
    taken = [L.sem(f"cmp_taken{n}") for n in range(2)]
    turned, cleared, pos_turned, pos_taken, biased, bias_taken, hidden, acted, k_ready, v_ready, done = (
        L.sem("cmp_" + x) for x in ("turned", "cleared", "pos_turned", "pos_taken", "biased",
                                    "bias_taken", "hidden", "acted", "k", "v", "done"))
    with nc.Block() as block:
        @block.sync
        def _(sp):
            sp.dma_start(table[:], A["page_table"].rearrange("b p -> (b p)").unsqueeze(0)).then_inc(table_in, 16)
            sp.dma_start(pos[:], A["cmp_pos"][0].rearrange("s (l a) d -> (s l) (a d)", a=2)).then_inc(w_in, 16)
            for n in range(2):
                sp.dma_start(w1[n], A["cmp_w1"][0, n].rearrange("(l p) m -> p l m", p=P)).then_inc(w_in, 16)
                sp.dma_start(w2[:, n], A["cmp_w2"][0, n]).then_inc(w_in, 16)
            sp.dma_start(scratch, L.gate_tok[0:64, 2]).then_inc(gate_out, 16)
            sp.wait_ge(table_in, 16)
            for b in range(NQ):
                if b >= 2:
                    sp.wait_ge(turned, 2 * (b - 1))
                for g in range(NPG):
                    dst = rows[b % 2][g * 64:(g + 1) * 64].rearrange("m s k a d -> m (s k) a d")
                    if b < NB:
                        page = sp.value_load(table[0:1, b * NPG + g:b * NPG + g + 1], min_val=0,
                                             max_val=A["cache_cmp_kv"].shape[1] - 1)
                        src = A["cache_cmp_kv"][0, bass.ds(page, 1)].rearrange(
                            "o (m a) s k d -> (o m) a (s k) d", a=2)
                    else:
                        src = O["cmp_p"][0, 0, g * PAGE:(g + 1) * PAGE].rearrange("(m a) s k d -> m a (s k) d", a=2)
                    for r in range(2):
                        sp.dma_start(dst[:, :, r], src[:, r]).then_inc(rows_in[b % 2], 16)
            sp.wait_ge(cleared, 2)
            sp.wait_ge(gate_out, 16)
            for b in range(NB):
                for g, what in ((0, "slc_s"), (1, "win_s")):
                    src = O[what][0, b, (PAST - TS if g else 0):(PAST if g else TS), 1]
                    sp.dma_start(L.v_small[8:16, g, b], src.rearrange("t k d -> t (k d)")
                                 ).then_inc(small_in, 16)
            with nc.allow_non_contiguous_dma(reason="gates by (head, token)"):
                for h in range(NH):
                    sp.dma_start(L.gate_rows[h * TS:(h + 1) * TS],
                                 scratch[:, 3 * h:3 * h + 3].rearrange("(b t) r -> t b r", t=TS)
                                 ).then_inc(small_in, 16)
            sp.wait_ge(small_in, 16 * (2 * NB + NH))

        @block.tensor
        def _(pe):
            pe.wait_ge(w_in, 16 * 5)
            pe.transpose(bank[6][:, 0:32], pos[:], ident[0:32, 0:32]).then_inc(pos_turned, 1)
            pe.wait_ge(pos_taken, 1)
            for n in range(2):
                for l in range(LT):
                    mm = pe.matmul(bank[7][:, n:n + 1], w1[n][:, l], posT[:, n * LT + l:n * LT + l + 1],
                                   start=(l == 0), stop=(l == LT - 1))
            mm.then_inc(biased, 1)
            for b in range(NQ):
                pe.wait_ge(rows_in[b % 2], 32 * NPG * (b // 2 + 1))
                for n in range(2):
                    if b >= 1:
                        pe.wait_ge(taken[n], b)
                    for kv in range(KV):
                        mm = pe.transpose(bank[n][:, kv * P:(kv + 1) * P], rows[b % 2][:, n, kv].rearrange("p a d -> p (a d)"), ident)
                    mm.then_inc(turned, 1)
            for n in range(2):
                pe.wait_ge(taken[n], NQ)
            for n in range(2):
                for l in range(LT):
                    pe.matmul(bank[2 + n][:, 0:NB * KV * NC], w1[n][:, l],
                              R[n][:, 0:NB, :, l:l + 8 * (NC - 1) + 1:8].rearrange("p b k n -> p (b k) n"),
                              start=(l == 0), stop=(l == LT - 1))
                for l in range(LT):
                    mm = pe.matmul(bank[4 + n][:, 0:KV * NC], w1[n][:, l],
                                   R[n][:, NB, :, l:l + 8 * (NC - 1) + 1:8], start=(l == 0), stop=(l == LT - 1))
                mm.then_inc(hidden, 1)
            pe.wait_ge(acted, 2)
            for a in range(2):
                mm = pe.matmul(bank[0][a * HD:(a + 1) * HD, 0:NQ * 2 * NC], w2[:, 0],
                               hid[0][:, :, a:KV:2, :].rearrange("p b k n -> p b k n"), start=True, stop=True)
            mm.then_inc(k_ready, 1)
            pe.wait_ge(acted, 4)
            for b in range(NQ):
                if b >= 2:
                    pe.wait_ge(done, b)
                for kv in range(KV):
                    mm = pe.matmul(bank[6 + b % 2][0:NC, kv * HD:(kv + 1) * HD], hid[1][:, b, kv],
                                   w2[:, 1], start=True, stop=True)
                mm.then_inc(v_ready, 1)

        @block.scalar
        def _(act):
            act.wait_ge(pos_turned, 1)
            act.activation(posT[:], bank[6][:, 0:32], ACT.Copy).then_inc(pos_taken, 1)
            for i in range(0, 2 * NQ, 2):
                act.wait_ge(turned, i + 1)
                act.activation(R[0][:, i // 2].rearrange("p k m -> p (k m)"), bank[0][:], ACT.Copy
                               ).then_inc(taken[0], 1)
            act.wait_ge(bias_taken, 1)
            for n in range(2):
                act.wait_ge(hidden, n + 1)
                act.activation(hid[n][:, 0:NB].rearrange("p b k n -> p (b k n)"), bank[2 + n][:, 0:NB * KV * NC],
                               ACT.Gelu_apprx_tanh, bias=bias[:, n:n + 1]).then_inc(acted, 1)
                act.activation(hid[n][:, NB].rearrange("p k n -> p (k n)"), bank[4 + n][:, 0:KV * NC],
                               ACT.Gelu_apprx_tanh, bias=bias[:, n:n + 1]).then_inc(acted, 1)

        @block.vector
        def _(dve):
            dve.memset(L.k_cmp[:], 0.0).then_inc(cleared, 1)
            dve.memset(L.v_small[:], 0.0).then_inc(cleared, 1)
            dve.wait_ge(biased, 1)
            dve.tensor_copy(bias[:], bank[7][:, 0:2]).then_inc(bias_taken, 1)
            for i in range(1, 2 * NQ, 2):
                dve.wait_ge(turned, i + 1)
                dve.tensor_copy(R[1][:, i // 2].rearrange("p k m -> p (k m)"), bank[1][:]).then_inc(taken[1], 1)
            dve.wait_ge(k_ready, 1)
            dve.wait_ge(cleared, 2)
            dve.tensor_copy(L.k_cmp[:, :, :, 0:NC],
                            bank[0][:, 0:NQ * 2 * NC].rearrange("p (b k n) -> p b k n", b=NQ, k=2)
                            ).then_inc(done, 1)
            for b in range(NQ):
                dve.wait_ge(v_ready, b + 1)
                dve.tensor_copy(L.v_small[0:NC, 2, b], bank[6 + b % 2][0:NC, 0:256]).then_inc(done, 1)


def attention(L, s):
    nc, A, O, bank, proj = L.nc, L.A, L.O, L.bank, L.proj
    mix = proj[:, T_NQ:T_NQ + 8]
    ident = L.cst[:, K_ID:K_ID + P]
    S = [L.sb(f"scores{i}", [P, 2, GW], scope=s) for i in range(2)]
    S_cmp = [L.sb(f"scores_cmp{i}", [P, 16], scope=s) for i in range(2)]
    PR = [L.sb(f"probs{i}", [P, 2, GW], scope=s) for i in range(3)]
    PR_cmp = [L.sb(f"probs_cmp{i}", [P, 16], scope=s) for i in range(3)]
    PT = [L.sb(f"probs_turned{i}", [P, 7, P], scope=s) for i in range(2)]
    stat = [L.sb(f"stat{i}", [P, 5, 3], scope=s) for i in range(3)]
    past_k = [L.sb(f"past_rows_k{i}", [P, 2, NPG, 256], scope=s) for i in range(2)]
    past_v = [L.sb(f"past_rows_v{i}", [P, 2, NPG, 256], scope=s) for i in range(5)]
    KT = [L.sb(f"past_k{i}", [P, 2, 2, PAST], scope=s) for i in range(2)]
    table = L.sb("table2", [1, NB * NPG], I32, scope=s)
    q_s = proj[:, T_KV:T_KV + 4].rearrange("p k t -> p (k t)")[:, 0:2 * NB * 2 * G * TS].rearrange(
        "p (h b a c) -> p h b a c", h=2, b=NB, a=2)
    items = [(p, a, g, qt) for qt in range(2) for p in range(2) for g in range(G) for a in range(2)]
    NP_, NI = len(items), len(items) + NB
    turns = []
    for i in range(NI):
        if NP_ <= i + 3 < NI:
            turns.append(-1 - (i + 3 - NP_))
        turns.append(i)
    turn_no = {x: n for n, x in enumerate(turns)}
    table_in = L.sem("att_table")
    k_in = [L.sem(f"past_k_in{i}") for i in range(2)]
    v_in = [L.sem(f"past_v_in{i}") for i in range(5)]
    scored, masked, maxed, exped, summed, weighed, turned, taken, out_ready, out_taken, filled = (
        L.sem("att_" + x) for x in ("scored", "masked", "maxed", "exped", "summed", "weighed", "turned",
                                    "taken", "out_ready", "out_taken", "filled"))

    def width(i):
        return GW if i >= NP_ else (items[i][3] + 1) * P

    with nc.Block() as block:
        @block.sync
        def _(sp):
            sp.dma_start(table[:], A["page_table"].rearrange("b p -> (b p)").unsqueeze(0)).then_inc(table_in, 16)
            sp.wait_ge(table_in, 16)
            for b in range(NB):
                if b >= 2:
                    sp.wait_ge(turned, turn_no[-1 - (b - 2)] + 1)
                if b >= 5:
                    sp.wait_ge(out_ready, NP_ + b - 4)
                for g in range(NPG):
                    page = sp.value_load(table[0:1, b * NPG + g:b * NPG + g + 1], min_val=0,
                                         max_val=A["cache_slc_kv"].shape[1] - 1)
                    slc = A["cache_slc_kv"][0, bass.ds(page, 1)].rearrange("o r s k d -> (o r) s (k d)")
                    win = A["cache_win_kv"][0, b, g * P:(g + 1) * P].rearrange("r s k d -> r s (k d)")
                    for n, src in enumerate((slc, win)):
                        sp.dma_start(past_k[b % 2][:, n, g], src[:, 0]).then_inc(k_in[b % 2], 16)
                        sp.dma_start(past_v[b % 5][:, n, g], src[:, 1]).then_inc(v_in[b % 5], 16)

        @block.tensor
        def _(pe):
            def scores(i):
                if i >= 2:
                    pe.wait_ge(masked, 2 * (i - 1))
                main, small = bank[i % 2], bank[2 + i % 2]
                if i < NP_:
                    p, a, g, qt = items[i]
                    w = width(i)
                    r = slice(a * HD, (a + 1) * HD)
                    qT = proj[r, T_NQ + 4 * p + g, qt * P:(qt + 1) * P]
                    for n in range(2):
                        pe.matmul(main[:, n * w:(n + 1) * w], qT, proj[r, T_KV + 4 + 4 * n + p, 0:w],
                                  start=True, stop=True)
                    pe.matmul(small[:, 32:48], qT, L.k_cmp[r, NB, p], start=True, stop=True).then_inc(scored, 1)
                    return
                b = i - NP_
                pe.wait_ge(taken, 2 * turn_no[-1 - b] + 2)
                pe.wait_ge(filled, 6)
                c = TP + b * TS
                for p in range(2):
                    o = slice(64 * p, 64 * p + 64)
                    qT = q_s[:, p, b].rearrange("p a c -> p (a c)")
                    for n in range(2):
                        pe.matmul(main[o, n * 256:(n + 1) * 256], qT, KT[b % 2][:, n, p], start=True, stop=True)
                        pe.matmul(small[o, 16 * n:16 * n + 16], qT, proj[:, T_KV + 4 + 4 * n + p, c - TS:c + TS],
                                  start=True, stop=True)
                    mm = pe.matmul(small[o, 32:48], qT, L.k_cmp[:, b, p], start=True, stop=True)
                mm.then_inc(scored, 1)

            def turn(x):
                if turn_no[x]:
                    pe.wait_ge(taken, 2 * turn_no[x])
                if x < 0:
                    b = -1 - x
                    pe.wait_ge(k_in[b % 2], 64 * (b // 2 + 1))
                    for n in range(2):
                        for p in range(2):
                            for g in range(NPG):
                                mm = pe.transpose(bank[4 + n][:, p * PAST + g * P:p * PAST + (g + 1) * P],
                                                  past_k[b % 2][:, n, g, p * P:(p + 1) * P], ident)
                    mm.then_inc(turned, 1)
                    return
                pe.wait_ge(weighed, x + 1)
                w = PR[x % 3]
                chunks = min(width(x), PAST) // P
                for n in range(2):
                    for g in range(chunks):
                        pe.transpose(bank[4][:, (chunks * n + g) * P:(chunks * n + g + 1) * P],
                                     w[:, n, g * P:(g + 1) * P], ident)
                if x >= NP_:
                    for n in range(2):
                        pe.transpose(bank[5][0:16, n * P:(n + 1) * P], w[:, n, PAST:GW], ident)
                pe.transpose(bank[5][0:16, 2 * P:3 * P], PR_cmp[x % 3][:], ident).then_inc(turned, 1)

            def outputs(i):
                pe.wait_ge(taken, 2 * turn_no[i] + 2)
                if i >= 2:
                    pe.wait_ge(out_taken, i - 1)
                pt = PT[i % 2]
                o_bank = bank[6 + i % 2]
                if i < NP_:
                    p, a, g, qt = items[i]
                    kv = 2 * p + a
                    o = o_bank[a * HD:(a + 1) * HD, 0:P]
                    chunks = width(i) // P
                    for n in range(2):
                        for c in range(chunks):
                            at = (3 + 2 * n) * 256 + kv * HD
                            pe.matmul(o, L.kv_tok[:, c, at:at + HD], pt[:, chunks * n + c],
                                      start=(n == 0 and c == 0), stop=False)
                    pe.matmul(o, L.v_small[:, 2, NB, kv * HD:(kv + 1) * HD], pt[0:16, 6],
                              start=False, stop=True).then_inc(out_ready, 1)
                    return
                b = i - NP_
                pe.wait_ge(v_in[b % 5], 64 * (b // 5 + 1))
                for p in range(2):
                    o, q = o_bank[:, p * 64:(p + 1) * 64], slice(64 * p, 64 * p + 64)
                    for n in range(2):
                        for c in range(2):
                            pe.matmul(o, past_v[b % 5][:, n, c, p * P:(p + 1) * P], pt[:, 2 * n + c, q],
                                      start=(n == 0 and c == 0), stop=False)
                    for n in range(3):
                        mm = pe.matmul(o, L.v_small[:, n, b, p * P:(p + 1) * P], pt[0:16, 4 + n, q],
                                       start=False, stop=(n == 2))
                mm.then_inc(out_ready, 1)

            for i in range(NI + 3):
                if i < NI:
                    scores(i)
                if 2 <= i < NI + 2:
                    k = turn_no[i - 2]
                    if k and turns[k - 1] < 0:
                        turn(turns[k - 1])
                    turn(i - 2)
                if i >= 3:
                    outputs(i - 3)

        @block.vector
        def _(dve):
            def weigh(i):
                st, w, wc = stat[i % 3], PR[i % 3], PR_cmp[i % 3]
                dve.wait_ge(exped, 3 * i + 3)
                dve.tensor_scalar(st[:, 3], st[:, 2], 0.5, None, ALU.max).then_inc(summed, 1)
                dve.wait_ge(summed, 3 * i + 1)
                dve.reciprocal(st[:, 4], st[:, 3]).then_inc(summed, 1)
                dve.wait_ge(summed, 3 * i + 2)
                if i < NP_:
                    p, a, g, qt = items[i]
                    h = (2 * p + a) * G + g
                    gt = L.gate_tok[:, qt, 3 * h:3 * h + 3]
                else:
                    gt = L.gate_rows[:, i - NP_]
                dve.tensor_tensor(st[:, 3], st[:, 4], gt, ALU.mult).then_inc(summed, 1)
                dve.wait_ge(summed, 3 * i + 3)
                wd = width(i)
                dve.tensor_scalar(w[:, 0, 0:wd], w[:, 0, 0:wd], st[:, 3, 1:2], None, ALU.mult)
                dve.tensor_scalar(w[:, 1, 0:wd], w[:, 1, 0:wd], st[:, 3, 2:3], None, ALU.mult)
                dve.tensor_scalar(wc[:], wc[:], st[:, 3, 0:1], None, ALU.mult).then_inc(weighed, 1)

            def take_scores(i):
                sc, scc, st = S[i % 2], S_cmp[i % 2], stat[i % 3]
                main, small = bank[i % 2], bank[2 + i % 2]
                dve.wait_ge(scored, i + 1)
                if i >= 2:
                    dve.wait_ge(exped, 3 * (i - 1))
                wd = width(i)
                if i < NP_:
                    qt = items[i][3]
                    m = L.cst[:, K_CAUSAL + qt * TP:K_CAUSAL + qt * TP + wd].unsqueeze(1).to_broadcast([P, 2, wd])
                    dve.tensor_tensor(sc[:, :, 0:wd], main[:, 0:2 * wd].rearrange("p (n k) -> p n k", n=2), m,
                                      ALU.add).then_inc(masked, 1)
                    dve.tensor_tensor(scc[:], small[:, 32:48], L.cst[:, K_CMP + 16 * qt:K_CMP + 16 * qt + 16],
                                      ALU.add).then_inc(masked, 1)
                else:
                    new = L.cst[:, K_NEW:K_NEW + 32].rearrange("p (n k) -> p n k", n=2)
                    dve.tensor_copy(sc[:, :, 0:PAST], main[:].rearrange("p (n k) -> p n k", n=2))
                    dve.tensor_tensor(sc[:, :, PAST:GW], small[:, 0:32].rearrange("p (n k) -> p n k", n=2), new,
                                      ALU.add).then_inc(masked, 1)
                    dve.tensor_tensor(scc[:], small[:, 32:48], L.cst[:, K_NEW + 32:K_NEW + 48], ALU.add
                                      ).then_inc(masked, 1)
                dve.wait_ge(masked, 2 * i + 2)
                dve.tensor_reduce(st[:, 0, 1:3], sc[:, :, 0:wd], AX.X, ALU.max).then_inc(maxed, 1)
                dve.tensor_reduce(st[:, 0, 0:1], scc[:], AX.X, ALU.max).then_inc(maxed, 1)
                dve.wait_ge(maxed, 3 * i + 2)
                dve.tensor_scalar(st[:, 1], st[:, 0], FLOOR, -(HD ** -0.5), ALU.max, ALU.mult
                                  ).then_inc(maxed, 1)

            for i in range(2):
                take_scores(i)
                if i == 1:
                    weigh(0)
            dve.memset(q_s, 0.0).then_inc(filled, 1)
            dve.wait_ge(filled, 1)
            for p in range(2):
                for a in range(2):
                    r = slice(a * HD, (a + 1) * HD)
                    for g in range(G):
                        last = dve.tensor_copy(
                            q_s[r, p, :, a, g * TS:(g + 1) * TS],
                            proj[r, T_NQ + 4 * p + g, TP:T].rearrange("p (b t) -> p b t", t=TS))
                    last.then_inc(filled, 1)
            dve.sem_inc(filled, 1)
            for i in range(2, NI + 1):
                if i < NI:
                    take_scores(i)
                weigh(i - 1)

        @block.scalar
        def _(act):
            def exps(i):
                act.wait_ge(maxed, 3 * i + 3)
                if i >= 3:
                    act.wait_ge(turned, turn_no[i - 3] + 1)
                sc, scc, w, wc, st = S[i % 2], S_cmp[i % 2], PR[i % 3], PR_cmp[i % 3], stat[i % 3]
                sl, wd = HD ** -0.5, width(i)
                for n in range(2):
                    act.activation(w[:, n, 0:wd], sc[:, n, 0:wd], ACT.Exp, scale=sl, bias=st[:, 1, n + 1:n + 2],
                                   accum_out=st[:, 2, n + 1:n + 2]).then_inc(exped, 1)
                act.activation(wc[:], scc[:], ACT.Exp, scale=sl, bias=st[:, 1, 0:1],
                               accum_out=st[:, 2, 0:1]).then_inc(exped, 1)

            def take(x):
                act.wait_ge(turned, turn_no[x] + 1)
                if x < 0:
                    b = -1 - x
                    if b >= 2:
                        act.wait_ge(scored, NP_ + b - 1)
                    for n in range(2):
                        act.activation(KT[b % 2][:, n].rearrange("p a k -> p (a k)"), bank[4 + n][:], ACT.Copy
                                       ).then_inc(taken, 1)
                    return
                if x >= 2:
                    act.wait_ge(out_ready, x - 1)
                m = 2 * min(width(x), PAST) // P
                act.activation(PT[x % 2][:, 0:m], bank[4][:, 0:m * P].rearrange("p (n k) -> p n k", n=m), ACT.Copy
                               ).then_inc(taken, 1)
                n = 0 if x >= NP_ else 2
                act.activation(PT[x % 2][0:16, 4 + n:7], bank[5][0:16, n * P:3 * P].rearrange("p (n k) -> p n k", k=P),
                               ACT.Copy).then_inc(taken, 1)

            def out(i):
                act.wait_ge(out_ready, i + 1)
                o = bank[6 + i % 2]
                if i < NP_:
                    p, a, g, qt = items[i]
                    r = slice(a * HD, (a + 1) * HD)
                    act.activation(mix[r, 4 * p + g, qt * P:(qt + 1) * P], o[r, 0:P], ACT.Copy
                                   ).then_inc(out_taken, 1)
                    return
                c = TP + (i - NP_) * TS
                for p in range(2):
                    for a in range(2):
                        r = slice(a * HD, (a + 1) * HD)
                        at = p * 64 + a * 32
                        last = act.activation(mix[r, 4 * p:4 * p + 4, c:c + TS],
                                              o[r, at:at + 32].rearrange("p (g t) -> p g t", t=TS), ACT.Copy)
                last.then_inc(out_taken, 1)

            for i in range(NI + 3):
                if i < NI:
                    exps(i)
                if 2 <= i < NI + 2:
                    k = turn_no[i - 2]
                    if k and turns[k - 1] < 0:
                        take(turns[k - 1])
                    take(i - 2)
                if i >= 3:
                    out(i - 3)


def mix_projection(L):
    nc = L.nc
    w = L.A["w_out"][0]
    gla_rows = w[0:1024].rearrange("(k p) n -> p k n", p=P)
    nsa_rows = w[1024:2048].rearrange("(h a g d) n -> a d h g n", h=2, a=2, g=G)
    q0, y0 = L.q, L.y
    hi_made, lo_made = L.sem("mix_hi"), L.sem("mix_lo")
    NP = KD // 2
    scope = ExitStack()
    with scope:
        part = [L.proj[:, T_GR + a] for a in range(2)]
        with nc.Block() as block:
            @block.sync
            def _(sp):
                with sp.Fori(0, NP) as n:
                    for a in range(2):
                        sp.wait_ge(L.split[a], n + (q0 + 1))
                        cols = bass.ds(n * (2 * P) + a * P, P)
                        raw = L.raw[a][:].rearrange("p (k n) -> p k n", n=P)
                        sp.dma_start(raw[:, 0:8], gla_rows[:, :, cols]).then_inc(L.mixw_loaded[a], 16)
                        for h in range(2):
                            for half in range(2):
                                sp.dma_start(raw[half * HD:(half + 1) * HD, 8 + 4 * h:12 + 4 * h],
                                             nsa_rows[half, :, h, :, cols]).then_inc(L.mixw_loaded[a], 16)

            @block.scalar
            def _(act):
                for k in range(KD):
                    act.activation(L.xh[:, k], mix_tile(L, k), ACT.Copy).then_inc(hi_made, 1)
                with act.Fori(0, NP) as n:
                    take_parts(L, act, part, n + q0, n + y0, 1.0)

            @block.vector
            def _(dve):
                for k in range(KD):
                    dve.wait_ge(hi_made, k + 1)
                    dve.tensor_tensor(L.xl[:, k], mix_tile(L, k), L.xh[:, k].bitcast(F32), ALU.subtract
                                      ).then_inc(lo_made, 1)
                with dve.Fori(0, NP) as n:
                    split_pair(L, dve, n + q0, L.mixw_loaded, 5 * 16, n, KD)

            @block.tensor
            def _(pe):
                pe.wait_ge(lo_made, KD)
                with pe.Fori(0, NP) as n:
                    for a in range(2):
                        multiply_unit(L, pe, n + q0, a, KD, (L.xh, L.xl))

            @block.gpsimd
            def _(pool):
                with pool.Fori(0, NP) as n:
                    add_parts(L, pool, part, n + q0, n)
    L.q += NP
    L.y += NP


def mix_tile(L, k):
    return L.proj[:, T_OG + k] if k < 8 else L.proj[:, T_NQ + k - 8]


def write_outputs(L):
    nc, O, bank = L.nc, L.O, L.bank
    turned, taken = L.sem("y_turned"), L.sem("y_taken")
    y_out = [L.sem(f"y_out{i}") for i in range(2)]
    ident = L.cst[:, K_ID:K_ID + P]
    with ExitStack() as scope:
        y = [L.sb(f"y{i}", [P, D], scope=scope) for i in range(2)]
        with nc.Block() as block:
            @block.tensor
            def _(pe):
                for t in range(3):
                    rows = P if t < 2 else T - TP
                    for c in range(4):
                        i = 4 * t + c
                        if i >= 4:
                            pe.wait_ge(taken, i - 3)
                        for j in range(4):
                            mm = pe.transpose(bank[i % 4][0:rows, j * P:(j + 1) * P],
                                              L.xT[:, 4 * c + j, t * P:t * P + rows], ident)
                        mm.then_inc(turned, 1)

            @block.scalar
            def _(act):
                for t in range(3):
                    rows = P if t < 2 else T - TP
                    for c in range(4):
                        i = 4 * t + c
                        act.wait_ge(turned, i + 1)
                        if t == 2:
                            act.wait_ge(y_out[0], 16)
                        act.activation(y[t % 2][0:rows, c * 512:(c + 1) * 512], bank[i % 4][0:rows, :],
                                       ACT.Copy).then_inc(taken, 1)

            @block.sync
            def _(sp):
                for t in range(3):
                    sp.wait_ge(taken, 4 * t + 4)
                    if t < 2:
                        sp.dma_start(O["y_p"][0, t * P:(t + 1) * P], y[t][:]).then_inc(y_out[t % 2], 16)
                    else:
                        sp.dma_start(O["y_s"].rearrange("b t d -> (b t) d"), y[0][0:T - TP, :]
                                     ).then_inc(y_out[0], 16)
                sp.wait_ge(y_out[0], 32)
                sp.wait_ge(y_out[1], 16)
                sp.wait_ge(L.stored, 16 * L.n_stored)


_INS = ["x_prompt", "x_sample", "cache_cmp_kv", "cache_slc_kv", "cache_win_kv", "state_gla", "page_table",
        "w_ffn1_in", "w_ffn1_out", "w_in", "w_gla_gate2", "b_gla_gate2", "gla_norm_g", "cmp_pos", "cmp_w1",
        "cmp_w2", "w_out", "w_ffn2_in", "w_ffn2_out", "ln_g", "ln_b"]
_OUTS = [("y_p", (1, TP, D)), ("y_s", (NB, TS, D)),
         ("cmp_p", (1, 1, TP, 2, KV, HD)), ("slc_p", (1, 1, TP, 2, KV, HD)), ("win_p", (1, 1, PAST, 2, KV, HD)),
         ("gla_p", (1, 1, GH, P, DV)),
         ("cmp_s", (1, NB, TS, 2, KV, HD)), ("slc_s", (1, NB, TS, 2, KV, HD)), ("win_s", (1, NB, PAST, 2, KV, HD)),
         ("gla_s", (1, NB, GH, P, DV))]


def kernel(**inputs):
    import concourse.bacc as bacc
    from concourse.bass_utils import run_bass_kernel_spmd

    nc = bacc.Bacc("TRN2", target_bir_lowering=False, num_devices=1)
    arrays = {name: np.ascontiguousarray(inputs[name]) for name in _INS}
    arrays["consts"], arrays["levels"] = constants(), level_masks()
    A = {n: nc.dram_tensor("in_" + n, a.shape, mybir.dt.from_np(a.dtype), kind="ExternalInput").ap()
         for n, a in arrays.items()}
    O = {n: nc.dram_tensor("out_" + n, shape, F32, kind="ExternalOutput").ap() for n, shape in _OUTS}
    build(nc, A, O)
    r = run_bass_kernel_spmd(nc, [{"in_" + n: a for n, a in arrays.items()}], core_ids=[0])
    return tuple(r.results[0]["out_" + n] for n, _ in _OUTS)
```

```python
from contextlib import ExitStack

import numpy as np
import concourse.bass as bass
from concourse import mybir
from concourse.alu_op_type import AluOpType as ALU

ACT = mybir.ActivationFunctionType
F32 = mybir.dt.float32
F32R = mybir.dt.float32r
U8 = mybir.dt.uint8
I32 = mybir.dt.int32
AX = mybir.AxisListType

P = 128
D = 2048
KD = D // P
TP, NB, TS = 256, 8, 8
T = TP + NB * TS
PAST, PAGE = 256, 128
NPG = PAST // PAGE
D_FF = 5632
FT = D_FF // P
FC = 11
CH = FT // FC
GH, DV = 4, 256
NH, KV, G, HD = 16, 4, 4, 64
CL, CS = 32, 16
NC = (TP - CL) // CS + 1
assert NC == (PAST + TS - CL) // CS + 1 and (NC - 1) * CS + CL <= PAST
SEL_LEN, SEL_TOPN, WINDOW = 64, 16, 512
assert -(-(PAST + TS) // SEL_LEN) <= SEL_TOPN and TP // SEL_LEN <= SEL_TOPN
assert PAST + TS <= WINDOW
ALPHA = 2.0 ** 0.25
EPS = 1e-5
NEG = -1e30
FLOOR = -5e29
LEVELS = 8
GW = PAST + 16
C_GA, C_GR, C_NQ, C_KV, C_NG = 2048, 2064, 3088, 4112, 5648
T_GQ, T_GK, T_GV, T_GR, T_NQ, T_KV, NT = 0, 4, 8, 16, 24, 32, 44
T_OG = 0
K_ID, K_MEAN, K_RMS, K_ROT, K_COS, K_SIN = 0, 128, 256, 384, 512, 832
K_RESET, K_CAUSAL, K_CMP, K_NEW, K_SEQ = 1152, 1472, 1984, 2016, 2064
K_ALL = 2072


def constants():
    c = np.zeros((P, K_ALL), np.float32)
    c[:, K_ID:K_ID + P] = np.eye(P)
    c[:, K_MEAN:K_MEAN + P] = 1.0 / D
    c[:, K_RMS:K_RMS + P] = 1.0 / DV
    half = HD // 2
    for m in range(P):
        if m % HD < half:
            c[m + half, K_ROT + m] = -1.0
        else:
            c[m - half, K_ROT + m] = 1.0
    pos = np.concatenate([np.arange(TP), np.tile(PAST + np.arange(TS), NB)]).astype(np.float32)
    freq = np.float32(10000.0) ** (-np.arange(half, dtype=np.float32) / np.float32(half))
    ang = (freq.astype(np.float32)[np.arange(P) % half][:, None] * pos[None, :]).astype(np.float32)
    c[:, K_COS:K_COS + T] = np.cos(ang)
    c[:, K_SIN:K_SIN + T] = np.sin(ang)
    c[:, K_RESET:K_RESET + T] = 1.0
    c[:, K_RESET] = 0.0
    c[:, K_RESET + TP:K_RESET + T:TS] = 0.0
    i = np.arange(P)[:, None]
    for qt in range(2):
        j = np.arange(TP)[None, :]
        c[:, K_CAUSAL + qt * TP:K_CAUSAL + (qt + 1) * TP] = np.where(j <= i + qt * P, 0.0, NEG)
        n = np.arange(16)[None, :]
        c[:, K_CMP + qt * 16:K_CMP + qt * 16 + 16] = np.where(
            (n < NC) & (n * CS + CL - 1 <= i + qt * P), 0.0, NEG)
    n = np.arange(16)[None, :]
    own = np.where((n >= 8) & (n - 8 <= i % TS), 0.0, NEG)
    c[:, K_NEW:K_NEW + 16] = own
    c[:, K_NEW + 16:K_NEW + 32] = own
    c[:, K_NEW + 32:K_NEW + 48] = np.where(n < NC, 0.0, NEG)
    for b in range(NB):
        c[b * TS:(b + 1) * TS, K_SEQ + b] = 1.0
    return c


def level_masks():
    m = np.zeros((P, LEVELS, T), np.int32)
    for lv in range(LEVELS):
        for i in range(T):
            r = i % P
            for j in range(P if i < TP else T - TP):
                if i >= TP and lv > 3:
                    continue
                s = 1 << lv
                if lv == 0:
                    m[j, 0, i] = j == r
                elif j // s == r // s and j % s < s // 2 <= r % s:
                    m[j, lv, i] = 1
    return m


class Layer:
    pass



def build(nc, A, O):
    ctx = ExitStack()
    with ctx:
        L = Layer()
        L.nc, L.A, L.O, L.ctx = nc, A, O, ctx
        L.scope = ctx

        def sem(name):
            return ctx.enter_context(nc.semaphore(name))

        def sb(name, shape, dt=F32, scope=None):
            return (scope or ctx).enter_context(nc.sbuf_tensor(name, shape, dt))

        L.sem, L.sb = sem, sb
        L.bank = [ctx.enter_context(nc.psum_tensor(f"bank{i}", [P, 512], F32)) for i in range(8)]
        L.cst = sb("cst", [P, K_ALL])
        L.lvl = sb("lvl", [P, LEVELS, T], U8)
        L.ln_gb = sb("ln_gb", [P, 2, 3, KD])
        L.xT = sb("xT", [P, KD, T])
        L.raw = [sb(f"raw{a}", [P, KD * P]) for a in range(2)]
        L.proj = sb("proj", [P, NT, T])
        L.gate = sb("gate", [P, T])
        L.hid = [sb(f"cmp_hid{n}", [P, NB + 1, KV, NC]) for n in range(2)]
        L.cmp_bias = sb("cmp_bias", [P, 2])
        L.table = sb("table", [1, NB * NPG], I32)
        L.loaded = [sem(f"loaded{a}") for a in range(2)]
        L.mixw_loaded = [sem(f"mixw_loaded{a}") for a in range(2)]
        L.hi = [sem(f"hi{a}") for a in range(2)]
        L.split = [sem(f"split{a}") for a in range(2)]
        L.multiplied = [sem(f"multiplied{a}") for a in range(2)]
        L.taken = [sem(f"taken{a}") for a in range(2)]
        L.added = [sem(f"added{a}") for a in range(2)]
        L.hidden_made = sem("hidden_made")
        L.cst_loaded = sem("cst_loaded")
        L.stored = sem("stored")
        L.sum_added = sem("sum_added")
        L.total = L.proj[:, 12]
        L.ln = {x: sem("ln_" + x) for x in ("mean", "centred", "squared", "summed", "root", "scaled",
                                            "shifted", "hi", "lo", "kept")}
        L.sums = 0
        L.n_stored = 0
        L.q = 0
        L.q_own = 0
        L.y = 0
        L.h = 0

        open_operands(L, "before")
        blocks = SampleBlocks(L)
        ffn(L, "ffn1", "w_ffn1_in", "w_ffn1_out", LoadInputs(L), side=blocks)
        projection(L, LayerNorm(L, 0), blocks)
        L.operands.close()
        with ExitStack() as mixing:
            L.kv_tok = sb("kv_tok", [P, 3, 12 * P], scope=mixing)
            L.gate_tok = sb("gate_tok", [P, 3, 48], scope=mixing)
            L.cmp_w2 = sb("cmp_w2", [P, 2, HD], scope=mixing)
            with ExitStack() as s:
                L.v_gla = sb("v_gla", [P, 3, GH * DV], scope=s)
                turn_projection(L)
                gla(L, s)
            with ExitStack() as s:
                attention(L, s)
        open_operands(L, "after")
        mix_projection(L)
        ffn(L, "ffn2", "w_ffn2_in", "w_ffn2_out", LayerNorm(L, 1))
        L.operands.close()
        write_outputs(L, LayerNorm(L, 2))


def open_operands(L, when):
    L.operands = ExitStack()
    L.xh = L.sb("xh_" + when, [P, KD, T], F32R, L.operands)
    L.xl = L.sb("xl_" + when, [P, KD, T], F32R, L.operands)
    L.wh = [L.sb(f"wh{a}_{when}", [P, KD * P], F32R, L.operands) for a in range(2)]
    L.wl = [L.sb(f"wl{a}_{when}", [P, KD * P], F32R, L.operands) for a in range(2)]


class LoadInputs:

    def __init__(self, L):
        self.L = L
        flat = L.proj[:].rearrange("p k t -> p (k t)")
        self.x_tok = flat[:, 0:3 * D].rearrange("p (t d) -> p t d", t=3)
        self.levels = flat[:, 6144:6144 + LEVELS * T].rearrange("p (l t) -> p l t", t=T).bitcast(I32)
        self.vectors = flat[0:96, 8704:8704 + P]
        self.x_loaded, self.levels_loaded, self.vectors_loaded = (
            L.sem(x + "_loaded") for x in ("x", "levels", "vectors"))
        self.turned, self.hi_made, self.bank_free, self.vectors_turned = (
            L.sem("x_" + x) for x in ("turned", "hi_made", "bank_free", "vectors_turned"))

    def sync(self, sp):
        L, A = self.L, self.L.A
        sp.dma_start(L.cst[:], A["consts"]).then_inc(L.cst_loaded, 16)
        sp.dma_start(self.x_tok[:, 0:2, :], A["x_prompt"][0].rearrange("(t p) d -> p t d", p=P)
                     ).then_inc(self.x_loaded, 16)
        sp.dma_start(self.x_tok[0:T - TP, 2, :], A["x_sample"].rearrange("b t d -> (b t) d")
                     ).then_inc(self.x_loaded, 16)

    def ready(self, pe, k):
        pe.wait_ge(self.bank_free, k + 1)

    def tensor(self, pe):
        L = self.L
        ident = L.cst[:, K_ID:K_ID + P]
        pe.wait_ge(L.cst_loaded, 16)
        pe.wait_ge(self.x_loaded, 32)
        for k in range(KD):
            if k >= 4:
                pe.wait_ge(self.bank_free, k - 3)
            for t in range(3):
                n = P if t < 2 else T - TP
                last = pe.transpose(L.bank[2 + k % 4][:, t * P:t * P + n],
                                    self.x_tok[0:n, t, k * P:(k + 1) * P], ident[0:n, 0:n])
            last.then_inc(self.turned, 1)
        pe.wait_ge(self.vectors_loaded, 32)
        pe.transpose(L.bank[6][:, 0:96], self.vectors, ident[0:96, 0:96]).then_inc(self.vectors_turned, 1)

    def scalar(self, act):
        L = self.L
        for n, name in enumerate(("ln_g", "ln_b")):
            act.dma_start(self.vectors[n * 48:(n + 1) * 48], L.A[name][0].rearrange("n (k p) -> (n k) p", p=P)
                          ).then_inc(self.vectors_loaded, 16)
        act.dma_start(self.levels, L.A["levels"]).then_inc(self.levels_loaded, 16)
        for k in range(KD):
            act.wait_ge(self.turned, k + 1)
            act.activation(L.xh[:, k], L.bank[2 + k % 4][:, 0:T], ACT.Copy).then_inc(self.hi_made, 1)
            act.activation(L.xT[:, k], L.bank[2 + k % 4][:, 0:T], ACT.Copy, scale=ALPHA
                           ).then_inc(self.hi_made, 1)
        act.wait_ge(self.vectors_turned, 1)
        act.activation(L.ln_gb[:].rearrange("p v n k -> p (v n k)"), L.bank[6][:, 0:96], ACT.Copy)

    def vector(self, dve, split):
        L = self.L
        for a in range(2):
            for s in (L.split[a], L.multiplied[a], L.taken[a], L.added[a]):
                dve.sem_inc(s, 1)
        dve.sem_inc(L.hidden_made, 1)
        for k in range(KD):
            dve.wait_ge(self.hi_made, 2 * k + 2)
            dve.tensor_tensor(L.xl[:, k], L.bank[2 + k % 4][:, 0:T], L.xh[:, k].bitcast(F32),
                              ALU.subtract).then_inc(self.bank_free, 1)
        split(0)
        split(1)

    def gpsimd(self, pool):
        pool.wait_ge(self.levels_loaded, 16)
        pool.tensor_copy(self.L.lvl[:], self.levels)


def multiply_unit(L, pe, q, a, nk, moving, first_wait=None):
    out = L.bank[a][:, 0:T]
    pe.wait_ge(L.split[a], q + 2)
    pe.wait_ge(L.taken[a], q + 1)
    hi, lo = moving
    for k in range(nk):
        if first_wait is not None:
            first_wait(pe, k)
        w = slice(k * P, (k + 1) * P)
        pe.matmul(out, L.wh[a][:, w], hi[:, k], start=(k == 0), stop=False)
        pe.matmul(out, L.wh[a][:, w], lo[:, k], start=False, stop=False)
        last = pe.matmul(out, L.wl[a][:, w], hi[:, k], start=False, stop=(k == nk - 1))
    last.then_inc(L.multiplied[a], 1)


def split_pair(L, dve, q, landed, per, own_q, nk):
    for a in range(2):
        split_unit(L, dve, q, a, landed, per, own_q, nk)


def split_unit(L, dve, q, a, landed, per, own_q, nk):
    n = nk * P
    dve.wait_ge(landed[a], own_q * per + per)
    dve.wait_ge(L.multiplied[a], q + 1)
    dve.tensor_copy(L.wh[a][:, 0:n], L.raw[a][:, 0:n]).then_inc(L.hi[a], 1)
    dve.wait_ge(L.hi[a], q + 1)
    dve.tensor_tensor(L.wl[a][:, 0:n], L.raw[a][:, 0:n], L.wh[a][:, 0:n].bitcast(F32),
                      ALU.subtract).then_inc(L.split[a], 1)


def load_unit(L, sp, q, a, src, nk):
    sp.wait_ge(L.split[a], q + 1)
    sp.dma_start(L.raw[a][:, 0:nk * P].rearrange("p (k n) -> p k n", n=P), src
                 ).then_inc(L.loaded[a], 16)


class SampleBlocks:

    def __init__(self, L):
        self.L = L
        flat = L.proj[:].rearrange("p k t -> p (k t)")
        self.R = flat[:, 5120:9216].rearrange("p (b k m) -> p b k m", b=NB, k=KV)
        self.w1 = flat[:, 9216:11264].rearrange("p (l m) -> p l m", m=P)
        self.rows = [flat[:, 11264 + 512 * i:11776 + 512 * i].rearrange("p (k a d) -> p k a d", k=KV, a=2)
                     for i in range(4)]
        self.pos = flat[0:32, 13312:13440]
        self.posT = flat[:, 13440:13472]
        self.rows_in = [L.sem(f"blocks_rows_in{i}") for i in range(4)]
        self.w_in, self.table_in, self.pos_in = (L.sem("blocks_" + x) for x in ("w_in", "table_in", "pos_in"))
        self.turned, self.taken, self.hidden, self.acted, self.pos_turned, self.pos_taken = (
            L.sem("blocks_" + x) for x in ("turned", "taken", "hidden", "acted", "pos_turned", "pos_taken"))
        self.biased, self.bias_taken = L.sem("blocks_biased"), L.sem("blocks_bias_taken")

    def load_w1(self, sp, n):
        L = self.L
        if n:
            sp.wait_ge(self.hidden, 1)
        sp.dma_start(self.w1, L.A["cmp_w1"][0, n].rearrange("(l p) m -> p l m", p=P)).then_inc(self.w_in, 16)

    def sync(self, sp, h):
        L = self.L
        if h == 0:
            sp.dma_start(L.table[:], L.A["page_table"].rearrange("b p -> (b p)").unsqueeze(0)
                         ).then_inc(self.table_in, 16)
            sp.dma_start(self.pos, L.A["cmp_pos"][0].rearrange("s (l a) d -> (s l) (a d)", a=2)
                         ).then_inc(self.pos_in, 16)
            sp.wait_ge(self.table_in, 16)
        if h == 1:
            self.load_w1(sp, 0)
        if h == 5:
            self.load_w1(sp, 1)
        for j in (2 * h, 2 * h + 1):
            n, b = j // NB, j % NB
            if j >= 4:
                sp.wait_ge(self.turned, j - 3)
            for g in range(NPG):
                page = sp.value_load(L.table[0:1, b * NPG + g:b * NPG + g + 1], min_val=0,
                                     max_val=L.A["cache_cmp_kv"].shape[1] - 1)
                src = L.A["cache_cmp_kv"][0, bass.ds(page, 1), :, n].rearrange("o (m a) k d -> (o m) a k d", a=2)
                for r in range(2):
                    sp.dma_start(self.rows[j % 4][g * 64:(g + 1) * 64, :, r], src[:, r]
                                 ).then_inc(self.rows_in[j % 4], 16)

    def tensor(self, pe, h):
        L = self.L
        ident = L.cst[:, K_ID:K_ID + P]
        if h == 0:
            pe.wait_ge(self.pos_in, 16)
            pe.transpose(L.bank[6][:, 0:32], self.pos, ident[0:32, 0:32]).then_inc(self.pos_turned, 1)
        for j in (2 * h, 2 * h + 1):
            pe.wait_ge(self.rows_in[j % 4], 64 * (j // 4 + 1))
            if j >= 4:
                pe.wait_ge(self.taken, j - 3)
            for kv in range(KV):
                mm = pe.transpose(L.bank[2 + j % 4][:, kv * P:(kv + 1) * P],
                                  self.rows[j % 4][:, kv].rearrange("p a d -> p (a d)"), ident)
            mm.then_inc(self.turned, 1)
        if h == 3:
            self.tensor_hidden(pe, 0)

    def tensor_hidden(self, pe, n):
        L, LT = self.L, CL // 2
        pe.wait_ge(self.w_in, 16 * (n + 1))
        pe.wait_ge(self.pos_taken, 1)
        if n:
            pe.wait_ge(self.acted, 1)
            pe.wait_ge(self.bias_taken, 1)
        for l in range(LT):
            mm = pe.matmul(L.bank[7][:, 0:1], self.w1[:, l], self.posT[:, n * LT + l:n * LT + l + 1],
                           start=(l == 0), stop=(l == LT - 1))
        mm.then_inc(self.biased, 1)
        pe.wait_ge(self.taken, NB * (n + 1))
        for l in range(LT):
            mm = pe.matmul(L.bank[6][:, 0:NB * KV * NC], self.w1[:, l],
                           self.R[:, :, :, l:l + 8 * (NC - 1) + 1:8].rearrange("p b k n -> p (b k) n"),
                           start=(l == 0), stop=(l == LT - 1))
        mm.then_inc(self.hidden, 1)

    def scalar(self, act, h):
        L = self.L
        if h == 0:
            act.wait_ge(self.pos_turned, 1)
            act.activation(self.posT, L.bank[6][:, 0:32], ACT.Copy).then_inc(self.pos_taken, 1)
        for j in (2 * h, 2 * h + 1):
            act.wait_ge(self.turned, j + 1)
            if j == NB:
                act.wait_ge(self.hidden, 1)
            act.activation(self.R[:, j % NB].rearrange("p k m -> p (k m)"), L.bank[2 + j % 4][:], ACT.Copy
                           ).then_inc(self.taken, 1)
        if h == 3:
            self.scalar_hidden(act, 0)

    def scalar_hidden(self, act, n):
        L = self.L
        act.wait_ge(self.biased, n + 1)
        act.activation(L.cmp_bias[:, n:n + 1], L.bank[7][:, 0:1], ACT.Copy).then_inc(self.bias_taken, 1)
        act.wait_ge(self.bias_taken, n + 1)
        act.wait_ge(self.hidden, n + 1)
        act.activation(L.hid[n][:, 0:NB].rearrange("p b k n -> p (b k n)"), L.bank[6][:, 0:NB * KV * NC],
                       ACT.Gelu_apprx_tanh, bias=L.cmp_bias[:, n:n + 1]).then_inc(self.acted, 1)


def ffn(L, name, w_in, w_out, before, side=None):
    nc = L.nc
    wi = L.A[w_in][0].rearrange("(k p) n -> p k n", p=P)
    wo = L.A[w_out][0].rearrange("(c k p) n -> p (c k) n", p=P, k=FC)
    q0, own0, y0, h0, sums0 = L.q, L.q_own, L.y, L.h, L.sums
    per = FC + KD // 2
    scope = ExitStack()
    with scope:
        hh = L.sb(name + "_hh", [P, FC, T], F32R, scope)
        hl = L.sb(name + "_hl", [P, FC, T], F32R, scope)
        gate, up, hid = (L.proj[:, i] for i in range(3))
        part = [L.proj[:, 3 + a] for a in range(2)]
        product, hi_done = L.sem(name + "_product"), L.sem(name + "_hidden_hi")
        with nc.Block() as block:
            @block.sync
            def _(sp):
                def load_in(c, f):
                    for a in range(2):
                        load_unit(L, sp, f + (c * per + q0), a,
                                  wi[:, :, bass.ds(f * P + (c * (FC * P) + a * D_FF), P)], KD)

                before.sync(sp)
                load_in(0, 0)
                for c in range(CH):
                    if side:
                        side.sync(sp, 2 * c)
                    with sp.Fori(0 if c else 1, FC) as f:
                        load_in(c, f)
                    if side:
                        side.sync(sp, 2 * c + 1)
                    with sp.Fori(0, KD // 2) as n:
                        for a in range(2):
                            load_unit(L, sp, n + (c * per + (FC + q0)), a,
                                      wo[:, c * FC:(c + 1) * FC, bass.ds(n * (2 * P) + a * P, P)], FC)

            @block.vector
            def _(dve):
                before.vector(dve, lambda a: split_unit(L, dve, q0, a, L.loaded, 16, own0, KD))
                for c in range(CH):
                    with dve.Fori(0 if c else 1, FC) as f:
                        split_pair(L, dve, f + (c * per + q0), L.loaded, 16, f + (c * per + own0), KD)
                    with dve.Fori(0, KD // 2) as n:
                        split_pair(L, dve, n + (c * per + (FC + q0)), L.loaded, 16,
                                   n + (c * per + (FC + own0)), FC)

            @block.tensor
            def _(pe):
                before.tensor(pe)
                for a in range(2):
                    multiply_unit(L, pe, q0, a, KD, (L.xh, L.xl), before.ready if a == 0 else None)
                for c in range(CH):
                    def hidden_there(pe, k):
                        if k == 0:
                            pe.wait_ge(L.hidden_made, c * FC + (FC + h0))
                        if k == FC - 1:
                            pe.wait_ge(L.hidden_made, c * FC + (FC + h0 + 1))

                    with pe.Fori(0 if c else 1, FC) as f:
                        for a in range(2):
                            multiply_unit(L, pe, f + (c * per + q0), a, KD, (L.xh, L.xl))
                    if side:
                        side.tensor(pe, 2 * c)
                    with pe.Fori(0, KD // 2) as n:
                        for a in range(2):
                            multiply_unit(L, pe, n + (c * per + (FC + q0)), a, FC, (hh, hl),
                                          hidden_there if a == 0 else None)
                    if side:
                        side.tensor(pe, 2 * c + 1)

            @block.scalar
            def _(act):
                before.scalar(act)
                for c in range(CH):
                    with act.Fori(0, FC) as f:
                        act.wait_ge(L.multiplied[0], f + (c * per + (q0 + 2)))
                        act.wait_ge(L.hidden_made, f + (c * FC + (h0 + 1)))
                        act.activation(gate, L.bank[0][:, 0:T], ACT.Silu).then_inc(L.taken[0], 1)
                        act.wait_ge(L.multiplied[1], f + (c * per + (q0 + 2)))
                        act.activation(up, L.bank[1][:, 0:T], ACT.Copy).then_inc(L.taken[1], 1)
                    if side:
                        side.scalar(act, 2 * c)
                    with act.Fori(0, KD // 2) as n:
                        take_parts(L, act, part, n + (c * per + (FC + q0)), n + (c * (KD // 2) + y0), 0.5)
                    if side:
                        side.scalar(act, 2 * c + 1)

            @block.gpsimd
            def _(pool):
                before.gpsimd(pool)
                for c in range(CH):
                    with pool.Fori(0, FC) as f:
                        pool.wait_ge(L.taken[0], f + (c * per + (q0 + 2)))
                        pool.wait_ge(L.taken[1], f + (c * per + (q0 + 2)))
                        pool.tensor_tensor(hid, gate, up, ALU.mult).then_inc(product, 1)
                        pool.wait_ge(product, f + (c * FC + 1))
                        one = hid.rearrange("p (o t) -> p o t", o=1)
                        pool.tensor_copy(hh[:, bass.ds(f, 1), :], one).then_inc(hi_done, 1)
                        pool.wait_ge(hi_done, f + (c * FC + 1))
                        pool.tensor_tensor(hl[:, bass.ds(f, 1), :], one, hh[:, bass.ds(f, 1), :].bitcast(F32),
                                           ALU.subtract).then_inc(L.hidden_made, 1)
                    if c < CH - 1:
                        with pool.Fori(0, KD // 2) as n:
                            add_parts(L, pool, part, n + (c * per + (FC + q0)), n)
                        continue
                    add_last_parts(L, pool, part, c * per + FC + q0, c * (KD // 2) + y0, sums0)
    L.q += CH * per
    L.q_own += CH * per
    L.y += CH * KD // 2
    L.h += FT
    L.sums += 1 + KD


def take_parts(L, act, part, q, y, scale):
    for a in range(2):
        act.wait_ge(L.multiplied[a], q + 2)
        act.wait_ge(L.added[a], y + 1)
        act.activation(part[a], L.bank[a][:, 0:T], ACT.Copy, scale=scale).then_inc(L.taken[a], 1)


def add_parts(L, pool, part, q, n):
    for a in range(2):
        pool.wait_ge(L.taken[a], q + 2)
        x = L.xT[:, bass.ds(n * 2 + a, 1), :]
        pool.tensor_tensor(x, x, part[a].rearrange("p (o t) -> p o t", o=1), ALU.add
                           ).then_inc(L.added[a], 1)


def add_last_parts(L, pool, part, q, y, sums0):
    pool.memset(L.total, 0.0).then_inc(L.sum_added, 1)
    for n in range(KD // 2):
        for a in range(2):
            x = L.xT[:, 2 * n + a]
            pool.wait_ge(L.taken[a], q + n + 2)
            pool.tensor_tensor(x, x, part[a], ALU.add).then_inc(L.added[a], 1)
            pool.wait_ge(L.added[a], y + n + 2)
            pool.wait_ge(L.sum_added, sums0 + 2 * n + a + 1)
            pool.tensor_tensor(L.total, L.total, x, ALU.add).then_inc(L.sum_added, 1)


def rsqrt_steps(L, act, dve, var, work, done, n0, part):
    v, r, t = work[:, 0], work[:, 1], work[:, 2]
    if part == 0:
        dve.tensor_scalar(v, var, EPS, None, ALU.add).then_inc(done, 1)
    if part == 1:
        act.wait_ge(done, n0 + 1)
        act.activation(t, v, ACT.Sqrt).then_inc(done, 1)
    if part == 2:
        steps = [
            lambda: dve.reciprocal(r, t),
            lambda: dve.tensor_tensor(t, v, r, ALU.mult),
            lambda: dve.tensor_tensor(t, t, r, ALU.mult),
            lambda: dve.tensor_scalar(t, t, -0.5, 1.5, ALU.mult, ALU.add),
            lambda: dve.tensor_tensor(r, r, t, ALU.mult),
        ]
        for i, s in enumerate(steps):
            dve.wait_ge(done, n0 + 2 + i)
            s().then_inc(done, 1)
        dve.wait_ge(done, n0 + 7)


class LayerNorm:

    def __init__(self, L, n):
        self.L, self.n, self.last = L, n, n == 2
        self.t0 = n * KD
        self.sq, self.z, self.work = L.proj[:, 0:4], L.proj[:, 4:8], L.proj[:, 8:11]

    def sync(self, sp):
        pass

    def ready(self, pe, k):
        if self.last:
            pe.wait_ge(self.L.ln["shifted"], self.t0 + k + 1)
        else:
            pe.wait_ge(self.L.ln["lo"], self.t0 + k + 1)

    def tensor(self, pe):
        L, ln, t0, ones = self.L, self.L.ln, self.t0, self.L.cst[:, K_MEAN:K_MEAN + P]
        pe.matmul(L.bank[2][:, 0:T], ones, L.total, start=True, stop=True).then_inc(ln["mean"], 1)
        for k in range(KD):
            pe.wait_ge(ln["squared"], t0 + k + 1)
            pe.matmul(L.bank[3][:, 0:T], ones, self.sq[:, k % 4], start=(k == 0),
                      stop=(k == KD - 1)).then_inc(ln["summed"], 1)

    def scalar(self, act):
        L, ln, t0, n, xT, z = self.L, self.L.ln, self.t0, self.n, self.L.xT, self.z
        for k in range(KD):
            act.wait_ge(ln["centred"], t0 + k + 1)
            if k >= 4:
                act.wait_ge(ln["summed"], t0 + k - 3)
            act.activation(self.sq[:, k % 4], xT[:, k], ACT.Square).then_inc(ln["squared"], 1)
        rsqrt_steps(L, act, None, None, self.work, ln["root"], 7 * n, 1)
        for k in range(KD):
            act.wait_ge(ln["scaled"], t0 + k + 1)
            if not self.last and k >= 4:
                act.wait_ge(ln["lo"], t0 + k - 3)
                act.wait_ge(ln["kept"], t0 + k - 3)
            out = xT[:, k] if self.last else z[:, k % 4]
            act.activation(out, xT[:, k], ACT.Identity, scale=L.ln_gb[:, 0, n, k:k + 1],
                           bias=L.ln_gb[:, 1, n, k:k + 1]).then_inc(ln["shifted"], 1)
            if not self.last:
                act.wait_ge(ln["shifted"], t0 + k + 1)
                act.activation(L.xh[:, k], z[:, k % 4], ACT.Copy).then_inc(ln["hi"], 1)
        if not self.last:
            act.wait_ge(ln["kept"], t0 + KD)

    def vector(self, dve, split):
        L, ln, t0, n, xT = self.L, self.L.ln, self.t0, self.n, self.L.xT
        dve.wait_ge(ln["mean"], n + 1)
        for k in range(KD):
            dve.tensor_tensor(xT[:, k], xT[:, k], L.bank[2][:, 0:T], ALU.subtract
                              ).then_inc(ln["centred"], 1)
        if not self.last:
            split(0)
        dve.wait_ge(ln["summed"], t0 + KD)
        rsqrt_steps(L, None, dve, L.bank[3][:, 0:T], self.work, ln["root"], 7 * n, 0)
        rsqrt_steps(L, None, dve, None, self.work, ln["root"], 7 * n, 2)

        def lo(k):
            dve.wait_ge(ln["hi"], t0 + k + 1)
            dve.tensor_tensor(L.xl[:, k], self.z[:, k % 4], L.xh[:, k].bitcast(F32), ALU.subtract
                              ).then_inc(ln["lo"], 1)

        for k in range(KD):
            dve.tensor_tensor(xT[:, k], xT[:, k], self.work[:, 1], ALU.mult).then_inc(ln["scaled"], 1)
            if not self.last and k >= 2:
                lo(k - 2)
        if not self.last:
            lo(KD - 2)
            lo(KD - 1)
            split(1)

    def gpsimd(self, pool):
        if self.last:
            return
        for k in range(KD):
            pool.wait_ge(self.L.ln["shifted"], self.t0 + k + 1)
            pool.tensor_scalar(self.L.xT[:, k], self.z[:, k % 4], ALPHA, None, ALU.mult
                               ).then_inc(self.L.ln["kept"], 1)
        pool.wait_ge(self.L.ln["kept"], self.t0 + KD)


def projection(L, before, blocks):
    nc = L.nc
    w = L.A["w_in"][0]
    seg_a = w[:, 0:C_GA].rearrange("(k p) n -> p k n", p=P)
    seg_r = w[:, C_GR:C_NQ].rearrange("(k p) n -> p k n", p=P)
    seg_q = [w[:, C_NQ + u * G * HD:C_KV].rearrange("(k p) n -> p k n", p=P) for u in range(2)]
    seg_kv = w[:, C_KV:C_NG].rearrange("(k p) n -> p k n", p=P)
    w_rows = w.rearrange("(k p) n -> p k n", p=P)
    q0, own0 = L.q, L.q_own
    NP = NT // 2
    q_loaded = [L.sem(f"q_loaded{a}") for a in range(2)]
    small_loaded, small_mult = L.sem("gates_w_loaded"), L.sem("gates_mult")
    small_taken = L.sem("gates_taken")
    scope = ExitStack()
    with scope:
        w_small = L.sb("w_small", [P, KD, 80], scope=scope)
        cleared = L.sem("w_small_cleared")
        with nc.Block() as block:
            @block.sync
            def _(sp):
                for a in range(2):
                    load_unit(L, sp, q0, a, seg_a[:, :, a * P:(a + 1) * P], KD)
                sp.wait_ge(cleared, 1)
                sp.dma_start(w_small[:, :, 0:48], w_rows[:, :, C_NG:C_NG + 48]).then_inc(small_loaded, 16)
                sp.dma_start(w_small[:, :, 64:80], w_rows[:, :, C_GA:C_GA + 16]).then_inc(small_loaded, 16)

                def segment(src, pairs, at, done=0):
                    with sp.Fori(done, pairs) as i:
                        for a in range(2):
                            load_unit(L, sp, i + (q0 + at), a, src[:, :, bass.ds(i * (2 * P) + a * P, P)], KD)

                segment(seg_a, 8, 0, 1)
                segment(seg_r, 4, 8)
                with sp.Fori(0, 2) as h:
                    with sp.Fori(0, 2) as gg:
                        for a in range(2):
                            sp.wait_ge(L.split[a], h * 2 + gg + (q0 + 12 + 1))
                            to = L.raw[a][:].rearrange("p (k u d) -> p k u d", u=2, d=HD)
                            for u in range(2):
                                sp.dma_start(to[:, :, u], seg_q[u][:, :, bass.ds(h * (8 * HD) + gg * (2 * HD) + a * HD, HD)]
                                             ).then_inc(q_loaded[a], 16)
                segment(seg_kv, 6, 16)

            @block.vector
            def _(dve):
                dve.memset(w_small[:], 0.0).then_inc(cleared, 1)
                before.vector(dve, lambda a: split_unit(L, dve, q0, a, L.loaded, 16, own0, KD))
                with dve.Fori(1, 12) as i:
                    split_pair(L, dve, i + q0, L.loaded, 16, i + own0, KD)
                with dve.Fori(0, 4) as i:
                    split_pair(L, dve, i + (q0 + 12), q_loaded, 32, i, KD)
                with dve.Fori(0, 6) as i:
                    split_pair(L, dve, i + (q0 + 16), L.loaded, 16, i + (own0 + 12), KD)

            @block.tensor
            def _(pe):
                before.tensor(pe)
                blocks.tensor_hidden(pe, 1)
                for a in range(2):
                    multiply_unit(L, pe, q0, a, KD, (L.xh, L.xl), before.ready if a == 0 else None)
                with pe.Fori(1, NP) as i:
                    for a in range(2):
                        multiply_unit(L, pe, i + q0, a, KD, (L.xh, L.xl))
                pe.wait_ge(small_loaded, 32)
                pe.wait_ge(L.ln["kept"], before.t0 + KD)
                for k in range(KD):
                    mm = pe.matmul(L.bank[2][0:80, 0:T], w_small[:, k], L.xT[:, k],
                                   start=(k == 0), stop=(k == KD - 1))
                mm.then_inc(small_mult, 1)

            @block.scalar
            def _(act):
                before.scalar(act)
                blocks.scalar_hidden(act, 1)
                with act.Fori(0, NP) as i:
                    for a in range(2):
                        act.wait_ge(L.multiplied[a], i + (q0 + 2))
                        act.activation(L.proj[:, bass.ds(i * 2 + a, 1), :],
                                       L.bank[a][:, 0:T].rearrange("p (o t) -> p o t", o=1),
                                       ACT.Copy).then_inc(L.taken[a], 1)
                act.wait_ge(small_mult, 1)
                act.activation(L.gate[64:80], L.bank[2][64:80, 0:T], ACT.Copy, scale=1.0 / ALPHA)
                act.activation(L.gate[0:48], L.bank[2][0:48, 0:T], ACT.Sigmoid, scale=1.0 / ALPHA
                               ).then_inc(small_taken, 1)

            @block.gpsimd
            def _(pool):
                before.gpsimd(pool)
    L.q += NP
    L.q_own += NP - 4


def turn_projection(L):
    nc, A, O, bank, proj = L.nc, L.A, L.O, L.bank, L.proj
    roped = [T_NQ + i for i in range(8)] + [T_KV + i for i in (0, 1, 4, 5, 8, 9)]
    NR = len(roped)
    ident = L.cst[:, K_ID:K_ID + P]
    rotated, by_cos, by_sin, rope_done = (L.sem("rope_" + s) for s in ("rotated", "cos", "sin", "done"))
    turned, turned_out = L.sem("turned"), L.sem("turned_out")
    L.kv_stored, L.cmp_w_in = L.sem("kv_stored"), L.sem("cmp_w_in")
    L.cmp_w1 = [L.raw[n][:].rearrange("p (l m) -> p l m", m=P) for n in range(2)]
    jobs = [("v", t, n) for t in range(3) for n in range(2)] + \
           [("kv", t, n) for t in range(3) for n in range(3)] + [("g", t, 0) for t in range(3)]
    with ExitStack() as scope:
        xc = L.sb("rope_xc", [P, 2, T], scope=scope)
        xs = L.sb("rope_xs", [P, 2, T], scope=scope)
        with nc.Block() as block:
            @block.tensor
            def _(pe):
                for i, t in enumerate(roped):
                    if i >= 2:
                        pe.wait_ge(by_sin, i - 1)
                    pe.matmul(bank[i % 2][:, 0:T], L.cst[:, K_ROT:K_ROT + P], proj[:, t],
                              start=True, stop=True).then_inc(rotated, 1)
                for i, (what, t, n) in enumerate(jobs):
                    if i >= 4:
                        pe.wait_ge(turned_out, i - 3)
                    if i == 6:
                        pe.wait_ge(rope_done, NR)
                    rows = P if t < 2 else T - TP
                    b = bank[2 + i % 4]
                    if what == "g":
                        mm = pe.transpose(b[0:rows, 0:48], L.gate[0:48, t * P:t * P + rows],
                                          ident[0:48, 0:48])
                    else:
                        base = (T_GV if what == "v" else T_KV) + 4 * n
                        for j in range(4):
                            mm = pe.transpose(b[0:rows, j * P:(j + 1) * P],
                                              proj[:, base + j, t * P:t * P + rows], ident)
                    mm.then_inc(turned, 1)

            @block.scalar
            def _(act):
                for i, (what, t, n) in enumerate(jobs):
                    act.wait_ge(turned, i + 1)
                    rows = P if t < 2 else T - TP
                    b = bank[2 + i % 4]
                    if what == "g":
                        act.activation(L.gate_tok[0:rows, t], b[0:rows, 0:48], ACT.Copy).then_inc(turned_out, 1)
                    else:
                        to = L.v_gla if what == "v" else L.kv_tok
                        act.activation(to[0:rows, t, n * 512:(n + 1) * 512], b[0:rows, :], ACT.Copy
                                       ).then_inc(turned_out, 1)

            @block.gpsimd
            def _(pool):
                for i, t in enumerate(roped):
                    if i >= 2:
                        pool.wait_ge(rope_done, i - 1)
                    pool.tensor_tensor(xc[:, i % 2], proj[:, t], L.cst[:, K_COS:K_COS + T], ALU.mult
                                       ).then_inc(by_cos, 1)

            @block.vector
            def _(dve):
                for i, t in enumerate(roped):
                    dve.wait_ge(rotated, i + 1)
                    dve.tensor_tensor(xs[:, i % 2], bank[i % 2][:, 0:T], L.cst[:, K_SIN:K_SIN + T],
                                      ALU.mult).then_inc(by_sin, 1)
                    dve.wait_ge(by_sin, i + 1)
                    dve.wait_ge(by_cos, i + 1)
                    dve.tensor_tensor(proj[:, t], xc[:, i % 2], xs[:, i % 2], ALU.add
                                      ).then_inc(rope_done, 1)

            @block.sync
            def _(sp):
                for n in range(2):
                    sp.dma_start(L.cmp_w2[:, n], A["cmp_w2"][0, n]).then_inc(L.cmp_w_in, 16)
                    sp.dma_start(L.cmp_w1[n], A["cmp_w1"][0, n].rearrange("(l p) m -> p l m", p=P)
                                 ).then_inc(L.cmp_w_in, 16)
                sp.dma_start(O["win_s"][0, :, 0:PAST - TS].rearrange("b r s k d -> b r (s k d)"),
                             A["cache_win_kv"][0, :, TS:PAST].rearrange("b r s k d -> b r (s k d)")
                             ).then_inc(L.stored, 16)
                L.n_stored += 1
                for t in range(3):
                    for n, what in enumerate(("cmp", "slc", "win")):
                        sp.wait_ge(turned_out, 6 + 3 * t + n + 1)
                        if t < 2:
                            dst = O[what + "_p"][0, 0, t * P:(t + 1) * P].rearrange("r s k d -> r (s k d)")
                            src = L.kv_tok[:, t, n * 512:(n + 1) * 512]
                            sp.dma_start(dst, src).then_inc(L.kv_stored, 16)
                        elif what != "win":
                            dst = O[what + "_s"][0].rearrange("b t s k d -> (b t) (s k d)")
                            sp.dma_start(dst, L.kv_tok[0:64, 2, n * 512:(n + 1) * 512]
                                         ).then_inc(L.kv_stored, 16)
                        else:
                            for b in range(NB):
                                dst = O["win_s"][0, b, PAST - TS:PAST].rearrange("t s k d -> t (s k d)")
                                sp.dma_start(dst, L.kv_tok[b * TS:(b + 1) * TS, 2, 1024:1536]
                                             ).then_inc(L.kv_stored, 16)
                sp.wait_ge(L.kv_stored, 16 * (6 + 2 + NB))


class Chain:

    def __init__(self, eng, sem):
        self.eng, self.sem, self.n = eng, sem, 0

    def __call__(self, ins):
        self.n += 1
        ins.then_inc(self.sem, 1)

    def settle(self):
        self.eng.wait_ge(self.sem, self.n)


def gla(L, s):
    nc, A, O, bank, proj = L.nc, L.A, L.O, L.bank, L.proj
    TT = GH * T
    NS = NB * TS
    gw2 = L.sb("gw2", [P, GH * P], scope=s)
    gb2 = L.sb("gb2", [P, GH], scope=s)
    norm_g = L.sb("norm_g", [P, 2], scope=s)
    B = L.sb("decay", [P, GH, T], scope=s)
    D_ = [L.sb(f"decay_diff{i}", [P, GH, T], scope=s) for i in range(2)]
    E_ = [L.sb(f"decay_e{i}", [P, GH, T], scope=s) for i in range(2)]
    E = D_[0]
    sq = L.sb("gla_sq", [P, 2 * GH, T], scope=s)
    QL = [L.sb("q_level", [P, GH, T], scope=s), sq[:, 0:GH]]
    KL = [L.sb("k_level", [P, GH, T], scope=s), sq[:, GH:2 * GH]]
    att = L.sb("gla_att", [P, GH, T], scope=s)
    attx = L.sb("gla_attx", [P, GH, P], scope=s)
    k_tok = L.sb("k_tok", [P, 3, GH * P], scope=s)
    q = proj[:, T_GQ:T_GQ + GH]
    k = proj[:, T_GK:T_GK + GH]
    gr = proj[:, T_GR:T_GR + 2 * GH]
    ident = L.cst[:, K_ID:K_ID + P]
    w_loaded = L.sem("gla_w_loaded")
    logit, biased, dve_s, act_s, pool_s = (L.sem("gla_" + x) for x in
                                           ("logit", "biased", "dve", "act", "pool"))
    R = QL[0][:].rearrange("p h t -> p (h t)")[:, 0:2 * KV * P].rearrange("p (n k m) -> p n k m", n=2, k=KV)
    paired, hidden, acted = (L.sem("cmp_" + x) for x in ("paired", "hidden", "acted"))
    with nc.Block() as block:
        @block.sync
        def _(sp):
            sp.dma_start(gw2[64:80], A["w_gla_gate2"][0]).then_inc(w_loaded, 16)
            with nc.allow_non_contiguous_dma(reason="small vectors, feature-major"):
                sp.dma_start(gb2[:], A["b_gla_gate2"][0].rearrange("(h p) -> p h", p=P)).then_inc(w_loaded, 16)
                sp.dma_start(norm_g[:], A["gla_norm_g"][0].rearrange("(h p) -> p h", p=P)).then_inc(w_loaded, 16)

        @block.tensor
        def _(pe):
            pe.wait_ge(w_loaded, 48)
            for h in range(GH):
                pe.matmul(bank[h][:, 0:T], gw2[64:80, h * P:(h + 1) * P], L.gate[64:80, :],
                          start=True, stop=True).then_inc(logit, 1)
            pe.wait_ge(L.cmp_w_in, 64)
            for n in range(2):
                pe.wait_ge(paired, 8 * (n + 1))
                for l in range(CL // 2):
                    mm = pe.matmul(bank[4 + n][:, 0:KV * NC], L.cmp_w1[n][:, l],
                                   R[:, n, :, l:l + 8 * (NC - 1) + 1:8], start=(l == 0), stop=(l == CL // 2 - 1))
                mm.then_inc(hidden, 1)

        @block.gpsimd
        def _(pool):
            for n in range(2):
                for kv in range(KV):
                    for r in range(2):
                        src = proj[kv % 2 * HD:(kv % 2 + 1) * HD, T_KV + 2 * n + kv // 2, r:TP:2]
                        pool.tensor_copy(R[r * HD:(r + 1) * HD, n, kv], src).then_inc(paired, 1)

        @block.scalar
        def _(act):
            act.wait_ge(w_loaded, 48)
            for h in range(GH):
                act.wait_ge(logit, h + 1)
                act.activation(B[:, h], bank[h][:, 0:T], ACT.Identity, bias=gb2[:, h:h + 1]).then_inc(biased, 1)
            act.wait_ge(biased, GH)
            act.activation(E[:], B[:], ACT.Abs).then_inc(act_s, 1)
            act.wait_ge(act_s, 1)
            act.activation(E[:], E[:], ACT.Exp, scale=-1.0).then_inc(act_s, 1)
            act.wait_ge(act_s, 2)
            act.activation(E[:], E[:], ACT.Ln, bias=1.0).then_inc(act_s, 1)
            for n in range(2):
                act.wait_ge(hidden, n + 1)
                act.activation(L.hid[n][:, NB].rearrange("p k n -> p (k n)"), bank[4 + n][:, 0:KV * NC],
                               ACT.Gelu_apprx_tanh, bias=L.cmp_bias[:, n:n + 1]).then_inc(acted, 1)
            act.activation(gr, gr, ACT.Silu).then_inc(acted, 1)

        @block.vector
        def _(dve):
            dve.wait_ge(biased, GH)
            dve.wait_ge(act_s, 1)
            dve.tensor_scalar(B[:], B[:], 0.0, None, ALU.min).then_inc(dve_s, 1)
            dve.wait_ge(act_s, 3)
            dve.wait_ge(dve_s, 1)
            dve.tensor_tensor(B[:], B[:], E[:], ALU.subtract).then_inc(dve_s, 1)
            dve.wait_ge(dve_s, 2)
            dve.tensor_scalar(E[:], B[:], 1.0 / 16.0, None, ALU.mult).then_inc(dve_s, 1)
            dve.wait_ge(dve_s, 3)
            for h in range(GH):
                dve.tensor_tensor_scan(B[:, h], L.cst[:, K_RESET:K_RESET + T], E[:, h], 0.0,
                                       ALU.mult, ALU.add).then_inc(dve_s, 1)
            dve.tensor_scalar(proj[:, T_GQ:T_GQ + GH], proj[:, T_GQ:T_GQ + GH], P ** -0.5, None, ALU.mult
                              ).then_inc(dve_s, 1)

    diff, made_abs, made_e, made_q, made_k, scored, merged = (
        L.sem("gla_lv_" + x) for x in ("diff", "abs", "e", "q", "k", "scored", "merged"))
    turned, k_tok_made, o_ready, o_taken, eb_made, q_in = (
        L.sem("gla_o_" + x) for x in ("turned", "k_tok", "ready", "taken", "eb", "q_in"))
    k_made, st_mult, st_made, sp_ready, sp_taken, joined, squared, ms_ready = (
        L.sem("gla_s_" + x) for x in ("k", "mult", "made", "p_ready", "p_taken", "joined", "squared", "ms"))
    st_in = [L.sem(f"state_in{i}") for i in range(2)]
    st_out = [L.sem(f"state_out{i}") for i in range(2)]
    s0 = [L.raw[0][:, i * 1024:(i + 1) * 1024].rearrange("p (h v) -> p h v", h=GH) for i in range(2)]
    s_new = [L.raw[1][:, i * 1024:(i + 1) * 1024].rearrange("p (h v) -> p h v", h=GH) for i in range(2)]
    k_one = [L.sb(f"k_one{i}", [NS, GH * P], scope=s) for i in range(2)]
    EB = L.sb("decay_samples", [P, GH, NS], scope=s)
    QS = L.sb("q_samples", [P, GH, NS], scope=s)
    og = proj[:, T_GV:T_GV + 2 * GH]
    inter = bank[4]
    ms_bank = bank[0:4]
    var_made, rooted = L.sem("gla_n_var"), L.sem("gla_n_root")
    L.o_var, L.o_t = ([proj[:, at + h] for h in range(GH)] for at in (T_GQ, T_GK))
    L.o_r = [proj[:, T_KV + 6 + 4 * (h // 2) + h % 2] for h in range(GH)]
    s_prompt = D_[1][:].rearrange("p h t -> p (h t)")[:, 0:GH * DV].rearrange("p (h v) -> p h v", h=GH)
    assert NB == LEVELS
    with nc.Block() as block:
        @block.vector
        def _(dve):
            def difference(n):
                if n >= 2:
                    dve.wait_ge(made_e, n - 1)
                D1 = D_[n % 2]
                if n == 0:
                    dve.tensor_tensor(D1[:, :, 0:TP], B[:, :, 0:TP],
                                      B[:, :, TP - 1:TP].to_broadcast([P, GH, TP]), ALU.subtract)
                    v, d = (x[:, :, TP:T].rearrange("p h (n s) -> p h n s", s=TS) for x in (B, D1))
                    ins = dve.tensor_tensor(d, v, v[:, :, :, TS - 1:TS].to_broadcast([P, GH, NB, TS]),
                                            ALU.subtract)
                elif n <= 6:
                    S = 1 << n
                    v, d = (x[:].rearrange("p h (n s) -> p (h n) s", s=S) for x in (B, D1))
                    ins = dve.tensor_tensor(d, v, v[:, :, S // 2 - 1:S // 2].to_broadcast([P, GH * T // S, S]),
                                            ALU.subtract)
                else:
                    S = 1 << n
                    for h in range(GH):
                        v, d = (x[:, h, 0:TP].rearrange("p (n s) -> p n s", s=S) for x in (B, D1))
                        ins = dve.tensor_tensor(d, v, v[:, :, S // 2 - 1:S // 2].to_broadcast([P, TP // S, S]),
                                                ALU.subtract)
                ins.then_inc(diff, 1)

            def merge(lv):
                for h in range(GH):
                    dve.wait_ge(scored, GH * lv + h + 1)
                    dve.wait_ge(merged, 1 + GH * lv + h)
                    b = bank[h]
                    if lv == LEVELS:
                        ins = dve.tensor_copy(attx[:, h], b[:, 0:P])
                    else:
                        ins = dve.copy_predicated(att[:, h, 0:TP], L.lvl[:, lv, 0:TP], b[:, 0:TP])
                        if lv <= 3:
                            ins = dve.copy_predicated(att[0:NS, h, TP:T], L.lvl[0:NS, lv, TP:T],
                                                      b[0:NS, TP:T])
                    ins.then_inc(merged, 1)

            def state(b):
                if b >= 2:
                    dve.wait_ge(st_out[b % 2], 16 * (b // 2))
                dve.wait_ge(st_in[b % 2], 16 * (b // 2 + 1))
                for h in range(GH):
                    dve.wait_ge(st_mult, GH * b + 2 * (h // 2) + 2)
                    at = (h % 2) * DV
                    dve.scalar_tensor_tensor(out=s_new[b % 2][:, h], in0=s0[b % 2][:, h],
                                             scalar=EB[:, h, (b + 1) * TS - 1:(b + 1) * TS],
                                             in1=bank[5 + h // 2][:, at:at + DV], op0=ALU.mult, op1=ALU.add
                                             ).then_inc(st_made, 1)

            difference(0)
            difference(1)
            dve.memset(att[:], 0.0).then_inc(merged, 1)
            dve.wait_ge(eb_made, 1)
            dve.tensor_tensor(QS[:], q[:, :, TP:T], EB[:], ALU.mult).then_inc(q_in, 1)
            for lv in range(1, LEVELS + 1):
                if lv < LEVELS:
                    difference(lv + 1)
                dve.wait_ge(made_e, lv + 1)
                if lv >= 2:
                    dve.wait_ge(scored, GH * (lv - 1))
                dve.tensor_tensor(QL[lv % 2][:], q, E_[lv % 2][:], ALU.mult).then_inc(made_q, 1)
                merge(lv - 1)
                if lv >= 2:
                    state(lv - 2)
            merge(LEVELS)
            state(NB - 1)
            dve.wait_ge(st_mult, GH * NB)
            for n in range(2 * GH):
                dve.wait_ge(o_taken, n + 1)
                o = og[:, n, TP:T].rearrange("p (b t) -> p b t", t=TS)
                dve.tensor_tensor(o, o, inter[:].rearrange("p (b n t) -> p n b t", n=2 * GH, t=TS)[:, n],
                                  ALU.add).then_inc(joined, 1)
            dve.wait_ge(ms_ready, 1)
            for h in range(GH):
                dve.tensor_scalar(L.o_var[h], ms_bank[h][:, 0:T], EPS, None, ALU.add).then_inc(var_made, 1)
            for h in range(GH):
                dve.wait_ge(rooted, h + 1)
                dve.reciprocal(L.o_r[h], L.o_t[h])

        @block.scalar
        def _(act):
            def one_sequence(b):
                if b >= 2:
                    act.wait_ge(st_mult, GH * (b - 1))
                act.activation(k_one[b % 2][:], k_tok[0:NS, 2], ACT.Copy,
                               scale=L.cst[0:NS, K_SEQ + b:K_SEQ + b + 1]).then_inc(k_made, 1)

            act.activation(EB[:], B[:, :, TP:T], ACT.Exp).then_inc(eb_made, 1)
            for n in range(LEVELS + 1):
                act.wait_ge(diff, n + 1)
                if n >= 2:
                    act.wait_ge(made_k, n - 1)
                if n >= 3:
                    act.wait_ge(made_q, n - 2)
                act.activation(D_[n % 2][:], D_[n % 2][:], ACT.Abs).then_inc(made_abs, 1)
                act.wait_ge(made_abs, n + 1)
                act.activation(E_[n % 2][:], D_[n % 2][:], ACT.Exp, scale=-1.0).then_inc(made_e, 1)
                if n == 1:
                    for t in range(3):
                        rows = P if t < 2 else NS
                        act.wait_ge(turned, t + 1)
                        act.activation(k_tok[0:rows, t], bank[5 + t][0:rows, :], ACT.Copy
                                       ).then_inc(k_tok_made, 1)
                    act.wait_ge(k_tok_made, 3)
                if n >= 2:
                    one_sequence(n - 2)
            one_sequence(NB - 1)
            for n in range(2 * GH):
                act.wait_ge(o_ready, n + 1)
                act.activation(og[:, n], bank[n % 4][:, 0:T], ACT.Copy).then_inc(o_taken, 1)
            for h in range(GH):
                act.wait_ge(joined, 2 * h + 2)
                act.activation(sq[:, 2 * h:2 * h + 2], og[:, 2 * h:2 * h + 2], ACT.Square).then_inc(squared, 1)
            for i in range(2):
                act.wait_ge(sp_ready, i + 1)
                act.activation(s_prompt[:, 2 * i:2 * i + 2], bank[5 + i][:].rearrange("p (h v) -> p h v", h=2),
                               ACT.Copy).then_inc(sp_taken, 1)
            for h in range(GH):
                act.wait_ge(var_made, h + 1)
                act.activation(L.o_t[h], L.o_var[h], ACT.Sqrt).then_inc(rooted, 1)

        @block.gpsimd
        def _(pool):
            for n in range(LEVELS + 1):
                pool.wait_ge(made_e, n + 1)
                if n == 2:
                    pool.wait_ge(turned, 3)
                if n >= 3:
                    pool.wait_ge(scored, GH * (n - 1))
                pool.tensor_tensor(KL[n % 2][:], k, E_[n % 2][:], ALU.mult).then_inc(made_k, 1)
            for n in range(2 * GH):
                pool.tensor_scalar(gr[:, n], gr[:, n], norm_g[:, n % 2:n % 2 + 1], None, ALU.mult)

        @block.sync
        def _(sp):
            for b in range(NB):
                if b >= 2:
                    sp.wait_ge(st_made, GH * (b - 1))
                sp.dma_start(s0[b % 2], A["state_gla"][0, b].rearrange("h k v -> k h v")
                             ).then_inc(st_in[b % 2], 16)
                if b >= 1:
                    sp.wait_ge(st_made, GH * b)
                    sp.dma_start(O["gla_s"][0, b - 1].rearrange("h k v -> k h v"), s_new[(b - 1) % 2]
                                 ).then_inc(st_out[(b - 1) % 2], 16)
            sp.wait_ge(st_made, GH * NB)
            sp.dma_start(O["gla_s"][0, NB - 1].rearrange("h k v -> k h v"), s_new[(NB - 1) % 2]
                         ).then_inc(st_out[(NB - 1) % 2], 16)
            sp.wait_ge(sp_taken, 2)
            sp.dma_start(O["gla_p"][0, 0].rearrange("h k v -> k h v"), s_prompt).then_inc(L.stored, 16)
            L.n_stored += 1
            for i in range(2):
                sp.wait_ge(st_out[i], 16 * NB // 2)
            sp.wait_ge(L.stored, 16 * L.n_stored)

        @block.tensor
        def _(pe):
            def scores(lv):
                ql, kl = (QL[lv % 2], KL[lv % 2]) if lv else (q, k)
                if lv:
                    pe.wait_ge(made_q, lv)
                    pe.wait_ge(made_k, lv + 1)
                for h in range(GH):
                    b = bank[h]
                    if lv:
                        pe.wait_ge(merged, 1 + GH * (lv - 1) + h + 1)
                    if lv == LEVELS:
                        mm = pe.matmul(b[:, 0:P], kl[:, h, 0:P], ql[:, h, P:TP], start=True, stop=True)
                    else:
                        for t in range(3 if lv <= 3 else 2):
                            rows = P if t < 2 else NS
                            c = slice(t * P, t * P + rows)
                            mm = pe.matmul(b[0:rows, c], kl[:, h, c], ql[:, h, c], start=True, stop=True)
                    mm.then_inc(scored, 1)

            def state(b):
                pe.wait_ge(st_in[b % 2], 16 * (b // 2 + 1))
                for n in range(2 * GH):
                    h, c = n // 2, n % 2
                    at = (b * 2 * GH + n) * TS
                    pe.matmul(inter[:, at:at + TS], s0[b % 2][:, h, c * P:(c + 1) * P],
                              QS[:, h, b * TS:(b + 1) * TS], start=True, stop=True)
                pe.wait_ge(k_made, b + 1)
                for h in range(GH):
                    if b:
                        pe.wait_ge(st_made, (b - 1) * GH + 2 * (h // 2) + 2)
                    at = (h % 2) * DV
                    pe.matmul(bank[5 + h // 2][:, at:at + DV], k_one[b % 2][:, h * P:(h + 1) * P],
                              L.v_gla[0:NS, 2, h * DV:(h + 1) * DV], start=True, stop=True
                              ).then_inc(st_mult, 1)

            scores(0)
            pe.wait_ge(made_k, 1)
            for t in range(3):
                rows = P if t < 2 else NS
                for h in range(GH):
                    mm = pe.transpose(bank[5 + t][0:rows, h * P:(h + 1) * P],
                                      KL[0][:, h, t * P:t * P + rows], ident)
                mm.then_inc(turned, 1)
            pe.wait_ge(q_in, 1)
            for lv in range(1, LEVELS + 1):
                scores(lv)
                if lv == 1:
                    pe.wait_ge(k_tok_made, 3)
                state(lv - 1)
            for n in range(2 * GH):
                h, c = n // 2, n % 2
                b = bank[n % 4]
                vc = slice(h * DV + c * P, h * DV + (c + 1) * P)
                if n == 0:
                    pe.wait_ge(merged, 1 + GH * (LEVELS + 1))
                if n >= 4:
                    pe.wait_ge(o_taken, n - 3)
                pe.matmul(b[:, 0:P], L.v_gla[:, 0, vc], att[:, h, 0:P], start=True, stop=False,
                          skip_group_check=True)
                pe.matmul(b[:, P:TP], L.v_gla[:, 0, vc], attx[:, h], start=False, stop=False,
                          skip_group_check=True)
                pe.matmul(b[:, P:TP], L.v_gla[:, 1, vc], att[:, h, P:TP], start=False, stop=False,
                          skip_group_check=True)
                pe.matmul(b[:, TP:T], L.v_gla[0:NS, 2, vc], att[0:NS, h, TP:T], start=False, stop=True,
                          skip_group_check=True).then_inc(o_ready, 1)
            pe.wait_ge(st_made, GH * NB)
            for h in range(GH):
                for t in range(2):
                    mm = pe.matmul(bank[5 + h // 2][:, (h % 2) * DV:(h % 2 + 1) * DV],
                                   k_tok[:, t, h * P:(h + 1) * P], L.v_gla[:, t, h * DV:(h + 1) * DV],
                                   start=(t == 0), stop=(t == 1))
                if h % 2:
                    mm.then_inc(sp_ready, 1)
            pe.wait_ge(o_taken, 2 * GH)
            for h in range(GH):
                pe.wait_ge(squared, h + 1)
                for c in range(2):
                    mm = pe.matmul(ms_bank[h][:, 0:T], L.cst[:, K_RMS:K_RMS + P], sq[:, 2 * h + c],
                                   start=(c == 0), stop=(c == 1))
            mm.then_inc(ms_ready, 1)


def attention(L, s):
    nc, A, O, bank, proj = L.nc, L.A, L.O, L.bank, L.proj
    mix = proj[:, T_NQ:T_NQ + 8]
    ident = L.cst[:, K_ID:K_ID + P]
    LAG = 3
    RING = LAG + 1
    S = [L.sb(f"scores{i}", [P, 2, GW], scope=s) for i in range(2)]
    S_cmp = [L.sb(f"scores_cmp{i}", [P, 16], scope=s) for i in range(2)]
    PR = [L.sb(f"probs{i}", [P, 2, GW], scope=s) for i in range(RING)]
    PR_cmp = [L.sb(f"probs_cmp{i}", [P, 16], scope=s) for i in range(RING)]
    PT = [L.sb(f"probs_turned{i}", [P, 7, P], scope=s) for i in range(2)]
    stat = [L.sb(f"stat{i}", [P, 5, 3], scope=s) for i in range(RING)]
    k_cmp = L.sb("k_cmp", [P, NB + 1, 2, 16], scope=s)
    v_small = L.sb("v_small", [16, 3, NB + 1, 256], scope=s)
    gate_rows = L.sb("gate_rows", [P, NB, 3], scope=s)
    scratch = nc.dram_tensor("gate_scratch", [NB * TS, 48], F32, kind="Internal").ap()
    gate_out, small_in, cleared, k_ready, v_ready, v_done, o_step = (
        L.sem("cmp_" + x) for x in ("gate", "small", "cleared", "k", "v", "done", "o_step"))
    NQ = NB + 1
    past_k = [L.sb(f"past_rows_k{i}", [P, 2, NPG, 256], scope=s) for i in range(2)]
    past_v = [L.sb(f"past_rows_v{i}", [P, 2, NPG, 256], scope=s) for i in range(5)]
    KT = [L.raw[i][:, 0:4 * PAST].rearrange("p (n a k) -> p n a k", n=2, a=2) for i in range(2)]
    table = L.table
    q_s = proj[:, T_KV:T_KV + 4].rearrange("p k t -> p (k t)")[:, 0:2 * NB * 2 * G * TS].rearrange(
        "p (h b a c) -> p h b a c", h=2, b=NB, a=2)
    items = [(p, a, g, qt) for qt in range(2) for p in range(2) for g in range(G) for a in range(2)]
    NP_, NI = len(items), len(items) + NB
    turns = []
    for i in range(NI):
        if 0 <= i + LAG + 1 - NP_ < NB:
            turns.append(-1 - (i + LAG + 1 - NP_))
        turns.append(i)
    turn_no = {x: n for n, x in enumerate(turns)}
    k_in = [L.sem(f"past_k_in{i}") for i in range(2)]
    v_in = [L.sem(f"past_v_in{i}") for i in range(5)]
    scored, masked, maxed, exped, summed, weighed, turned, taken, out_ready, out_taken, filled = (
        L.sem("att_" + x) for x in ("scored", "masked", "maxed", "exped", "summed", "weighed", "turned",
                                    "taken", "out_ready", "out_taken", "filled"))

    def width(i):
        return GW if i >= NP_ else (items[i][3] + 1) * P

    with nc.Block() as block:
        @block.sync
        def _(sp):
            def load(b, kv, buffer, landed):
                for g in range(NPG):
                    page = sp.value_load(table[0:1, b * NPG + g:b * NPG + g + 1], min_val=0,
                                         max_val=A["cache_slc_kv"].shape[1] - 1)
                    slc = A["cache_slc_kv"][0, bass.ds(page, 1), :, kv].rearrange("o r k d -> (o r) (k d)")
                    win = A["cache_win_kv"][0, b, g * P:(g + 1) * P, kv].rearrange("r k d -> r (k d)")
                    for n, src in enumerate((slc, win)):
                        sp.dma_start(buffer[:, n, g], src).then_inc(landed, 16)

            sp.dma_start(scratch, L.gate_tok[0:64, 2]).then_inc(gate_out, 16)
            for b in range(NB + 1):
                if b == 2:
                    for g, what in ((0, "slc_s"), (1, "win_s")):
                        src = O[what][0, :, (PAST - TS if g else 0):(PAST if g else TS), 1]
                        sp.dma_start(v_small[8:16, g, 0:NB], src.rearrange("b t k d -> t b (k d)")
                                     ).then_inc(small_in, 16)
                    sp.wait_ge(gate_out, 16)
                    with nc.allow_non_contiguous_dma(reason="gates by (head, token)"):
                        for h in range(NH):
                            sp.dma_start(gate_rows[h * TS:(h + 1) * TS],
                                         scratch[:, 3 * h:3 * h + 3].rearrange("(b t) r -> t b r", t=TS)
                                         ).then_inc(small_in, 16)
                if b < NB:
                    if b >= 2:
                        sp.wait_ge(turned, turn_no[-1 - (b - 2)] + 1)
                    load(b, 0, past_k[b % 2], k_in[b % 2])
                if b >= 1:
                    v = b - 1
                    if v >= 5:
                        sp.wait_ge(out_ready, NP_ + v - 4)
                    load(v, 1, past_v[v % 5], v_in[v % 5])

        @block.tensor
        def _(pe):
            def scores(i):
                if i >= 2:
                    pe.wait_ge(masked, 2 * (i - 1))
                main, small = bank[i % 2], bank[2 + i % 2]
                if i < NP_:
                    p, a, g, qt = items[i]
                    w = width(i)
                    r = slice(a * HD, (a + 1) * HD)
                    qT = proj[r, T_NQ + 4 * p + g, qt * P:(qt + 1) * P]
                    for n in range(2):
                        pe.matmul(main[:, n * w:(n + 1) * w], qT, proj[r, T_KV + 4 + 4 * n + p, 0:w],
                                  start=True, stop=True)
                    pe.matmul(small[:, 32:48], qT, k_cmp[r, NB, p], start=True, stop=True).then_inc(scored, 1)
                    return
                b = i - NP_
                pe.wait_ge(taken, 2 * turn_no[-1 - b] + 2)
                pe.wait_ge(filled, 6)
                c = TP + b * TS
                for p in range(2):
                    o = slice(64 * p, 64 * p + 64)
                    qT = q_s[:, p, b].rearrange("p a c -> p (a c)")
                    for n in range(2):
                        pe.matmul(main[o, n * 256:(n + 1) * 256], qT, KT[b % 2][:, n, p], start=True, stop=True)
                        pe.matmul(small[o, 16 * n:16 * n + 16], qT, proj[:, T_KV + 4 + 4 * n + p, c - TS:c + TS],
                                  start=True, stop=True)
                    mm = pe.matmul(small[o, 32:48], qT, k_cmp[:, b, p], start=True, stop=True)
                mm.then_inc(scored, 1)

            def turn(x):
                if turn_no[x]:
                    pe.wait_ge(taken, 2 * turn_no[x])
                if x < 0:
                    b = -1 - x
                    pe.wait_ge(k_in[b % 2], 64 * (b // 2 + 1))
                    for n in range(2):
                        for p in range(2):
                            for g in range(NPG):
                                mm = pe.transpose(bank[4 + n][:, p * PAST + g * P:p * PAST + (g + 1) * P],
                                                  past_k[b % 2][:, n, g, p * P:(p + 1) * P], ident)
                    mm.then_inc(turned, 1)
                    return
                pe.wait_ge(weighed, x + 1)
                w = PR[x % RING]
                chunks = min(width(x), PAST) // P
                for n in range(2):
                    for g in range(chunks):
                        pe.transpose(bank[4][:, (chunks * n + g) * P:(chunks * n + g + 1) * P],
                                     w[:, n, g * P:(g + 1) * P], ident)
                if x >= NP_:
                    for n in range(2):
                        pe.transpose(bank[5][0:16, n * P:(n + 1) * P], w[:, n, PAST:GW], ident)
                pe.transpose(bank[5][0:16, 2 * P:3 * P], PR_cmp[x % RING][:], ident).then_inc(turned, 1)

            def outputs(i):
                pe.wait_ge(taken, 2 * turn_no[i] + 2)
                if i >= 2:
                    pe.wait_ge(out_taken, i - 1)
                pt = PT[i % 2]
                o_bank = bank[6 + i % 2]
                if i < NP_:
                    p, a, g, qt = items[i]
                    kv = 2 * p + a
                    o = o_bank[a * HD:(a + 1) * HD, 0:P]
                    chunks = width(i) // P
                    for n in range(2):
                        for c in range(chunks):
                            at = (3 + 2 * n) * 256 + kv * HD
                            pe.matmul(o, L.kv_tok[:, c, at:at + HD], pt[:, chunks * n + c],
                                      start=(n == 0 and c == 0), stop=False)
                    pe.matmul(o, v_small[:, 2, NB, kv * HD:(kv + 1) * HD], pt[0:16, 6],
                              start=False, stop=True).then_inc(out_ready, 1)
                    return
                b = i - NP_
                pe.wait_ge(v_in[b % 5], 64 * (b // 5 + 1))
                pe.wait_ge(small_in, 16 * (2 + NH))
                pe.wait_ge(cleared, 3)
                for p in range(2):
                    o, q = o_bank[:, p * 64:(p + 1) * 64], slice(64 * p, 64 * p + 64)
                    for n in range(2):
                        for c in range(2):
                            pe.matmul(o, past_v[b % 5][:, n, c, p * P:(p + 1) * P], pt[:, 2 * n + c, q],
                                      start=(n == 0 and c == 0), stop=False)
                    for n in range(3):
                        mm = pe.matmul(o, v_small[:, n, b, p * P:(p + 1) * P], pt[0:16, 4 + n, q],
                                       start=False, stop=(n == 2))
                mm.then_inc(out_ready, 1)

            for a in range(2):
                mm = pe.matmul(bank[0][a * HD:(a + 1) * HD, 0:NQ * 2 * NC], L.cmp_w2[:, 0],
                               L.hid[0][:, :, a:KV:2, :], start=True, stop=True)
            mm.then_inc(k_ready, 1)
            for b in range(NQ):
                if b >= 4:
                    pe.wait_ge(v_done, b - 3)
                for kv in range(KV):
                    mm = pe.matmul(bank[4 + b % 4][0:NC, kv * HD:(kv + 1) * HD], L.hid[1][:, b, kv],
                                   L.cmp_w2[:, 1], start=True, stop=True)
                mm.then_inc(v_ready, 1)
            pe.wait_ge(v_done, NQ)
            for i in range(NI + LAG + 1):
                if 0 <= i + 1 - NP_ < NB:
                    turn(-1 - (i + 1 - NP_))
                if i < NI:
                    scores(i)
                if LAG <= i < NI + LAG:
                    turn(i - LAG)
                if i > LAG:
                    outputs(i - LAG - 1)

        @block.vector
        def _(dve):
            def weigh(i):
                st, w, wc = stat[i % RING], PR[i % RING], PR_cmp[i % RING]
                dve.wait_ge(exped, 3 * i + 3)
                dve.tensor_scalar(st[:, 3], st[:, 2], 0.5, None, ALU.max).then_inc(summed, 1)
                dve.wait_ge(summed, 3 * i + 1)
                dve.reciprocal(st[:, 4], st[:, 3]).then_inc(summed, 1)
                dve.wait_ge(summed, 3 * i + 2)
                if i < NP_:
                    p, a, g, qt = items[i]
                    h = (2 * p + a) * G + g
                    gt = L.gate_tok[:, qt, 3 * h:3 * h + 3]
                else:
                    dve.wait_ge(small_in, 16 * (2 + NH))
                    gt = gate_rows[:, i - NP_]
                dve.tensor_tensor(st[:, 3], st[:, 4], gt, ALU.mult).then_inc(summed, 1)
                dve.wait_ge(summed, 3 * i + 3)
                wd = width(i)
                dve.tensor_scalar(w[:, 0, 0:wd], w[:, 0, 0:wd], st[:, 3, 1:2], None, ALU.mult)
                dve.tensor_scalar(w[:, 1, 0:wd], w[:, 1, 0:wd], st[:, 3, 2:3], None, ALU.mult)
                dve.tensor_scalar(wc[:], wc[:], st[:, 3, 0:1], None, ALU.mult).then_inc(weighed, 1)

            def take_scores(i):
                sc, scc, st = S[i % 2], S_cmp[i % 2], stat[i % RING]
                main, small = bank[i % 2], bank[2 + i % 2]
                dve.wait_ge(scored, i + 1)
                if i >= 2:
                    dve.wait_ge(exped, 3 * (i - 1))
                wd = width(i)
                if i < NP_:
                    qt = items[i][3]
                    m = L.cst[:, K_CAUSAL + qt * TP:K_CAUSAL + qt * TP + wd].unsqueeze(1).to_broadcast([P, 2, wd])
                    dve.tensor_tensor(sc[:, :, 0:wd], main[:, 0:2 * wd].rearrange("p (n k) -> p n k", n=2), m,
                                      ALU.add).then_inc(masked, 1)
                    dve.tensor_tensor(scc[:], small[:, 32:48], L.cst[:, K_CMP + 16 * qt:K_CMP + 16 * qt + 16],
                                      ALU.add).then_inc(masked, 1)
                else:
                    new = L.cst[:, K_NEW:K_NEW + 32].rearrange("p (n k) -> p n k", n=2)
                    dve.tensor_copy(sc[:, :, 0:PAST], main[:].rearrange("p (n k) -> p n k", n=2))
                    dve.tensor_tensor(sc[:, :, PAST:GW], small[:, 0:32].rearrange("p (n k) -> p n k", n=2), new,
                                      ALU.add).then_inc(masked, 1)
                    dve.tensor_tensor(scc[:], small[:, 32:48], L.cst[:, K_NEW + 32:K_NEW + 48], ALU.add
                                      ).then_inc(masked, 1)
                dve.wait_ge(masked, 2 * i + 2)
                dve.tensor_reduce(st[:, 0, 1:3], sc[:, :, 0:wd], AX.X, ALU.max).then_inc(maxed, 1)
                dve.tensor_reduce(st[:, 0, 0:1], scc[:], AX.X, ALU.max).then_inc(maxed, 1)
                dve.wait_ge(maxed, 3 * i + 2)
                dve.tensor_scalar(st[:, 1], st[:, 0], FLOOR, -(HD ** -0.5), ALU.max, ALU.mult
                                  ).then_inc(maxed, 1)

            dve.wait_ge(k_ready, 1)
            dve.wait_ge(cleared, 2)
            dve.tensor_copy(k_cmp[:, :, :, 0:NC],
                            bank[0][:, 0:NQ * 2 * NC].rearrange("p (b k n) -> p b k n", b=NQ, k=2))
            for b in range(NQ):
                dve.wait_ge(v_ready, b + 1)
                dve.tensor_copy(v_small[0:NC, 2, b], bank[4 + b % 4][0:NC, 0:256]).then_inc(v_done, 1)
            for i in range(2):
                take_scores(i)
                if i == 1:
                    weigh(0)
            dve.memset(q_s, 0.0).then_inc(filled, 1)
            dve.wait_ge(filled, 1)
            for p in range(2):
                for a in range(2):
                    r = slice(a * HD, (a + 1) * HD)
                    for g in range(G):
                        last = dve.tensor_copy(
                            q_s[r, p, :, a, g * TS:(g + 1) * TS],
                            proj[r, T_NQ + 4 * p + g, TP:T].rearrange("p (b t) -> p b t", t=TS))
                    last.then_inc(filled, 1)
            dve.sem_inc(filled, 1)
            for i in range(2, NI + 1):
                if i < NI:
                    take_scores(i)
                weigh(i - 1)

        @block.gpsimd
        def _(pool):
            pool.memset(v_small[:, 2], 0.0).then_inc(cleared, 1)
            pool.memset(k_cmp[:], 0.0).then_inc(cleared, 1)
            pool.memset(v_small[0:8, 0:2], 0.0).then_inc(cleared, 1)
            ch = Chain(pool, o_step)
            var, t, r = L.o_var, L.o_t, L.o_r
            for step in (lambda h: pool.tensor_tensor(t[h], var[h], r[h], ALU.mult),
                         lambda h: pool.tensor_tensor(t[h], t[h], r[h], ALU.mult),
                         lambda h: pool.tensor_scalar(t[h], t[h], -0.5, 1.5, ALU.mult, ALU.add),
                         lambda h: pool.tensor_tensor(r[h], r[h], t[h], ALU.mult)):
                for h in range(GH):
                    ch(step(h))
                ch.settle()
            for n in range(2 * GH):
                ch(pool.tensor_tensor(proj[:, T_OG + n], proj[:, T_GV + n], r[n // 2], ALU.mult))
            ch.settle()
            for n in range(2 * GH):
                pool.tensor_tensor(proj[:, T_OG + n], proj[:, T_OG + n], proj[:, T_GR + n], ALU.mult)

        @block.scalar
        def _(act):
            def exps(i):
                act.wait_ge(maxed, 3 * i + 3)
                if i >= RING:
                    act.wait_ge(turned, turn_no[i - RING] + 1)
                sc, scc, w, wc, st = S[i % 2], S_cmp[i % 2], PR[i % RING], PR_cmp[i % RING], stat[i % RING]
                sl, wd = HD ** -0.5, width(i)
                for n in range(2):
                    act.activation(w[:, n, 0:wd], sc[:, n, 0:wd], ACT.Exp, scale=sl, bias=st[:, 1, n + 1:n + 2],
                                   accum_out=st[:, 2, n + 1:n + 2]).then_inc(exped, 1)
                act.activation(wc[:], scc[:], ACT.Exp, scale=sl, bias=st[:, 1, 0:1],
                               accum_out=st[:, 2, 0:1]).then_inc(exped, 1)

            def take(x):
                act.wait_ge(turned, turn_no[x] + 1)
                if x < 0:
                    b = -1 - x
                    if b >= 2:
                        act.wait_ge(scored, NP_ + b - 1)
                    for n in range(2):
                        act.activation(KT[b % 2][:, n].rearrange("p a k -> p (a k)"), bank[4 + n][:], ACT.Copy
                                       ).then_inc(taken, 1)
                    return
                if x >= 2:
                    act.wait_ge(out_ready, x - 1)
                m = 2 * min(width(x), PAST) // P
                act.activation(PT[x % 2][:, 0:m], bank[4][:, 0:m * P].rearrange("p (n k) -> p n k", n=m), ACT.Copy
                               ).then_inc(taken, 1)
                n = 0 if x >= NP_ else 2
                act.activation(PT[x % 2][0:16, 4 + n:7], bank[5][0:16, n * P:3 * P].rearrange("p (n k) -> p n k", k=P),
                               ACT.Copy).then_inc(taken, 1)

            def out(i):
                act.wait_ge(out_ready, i + 1)
                o = bank[6 + i % 2]
                if i < NP_:
                    p, a, g, qt = items[i]
                    r = slice(a * HD, (a + 1) * HD)
                    act.activation(mix[r, 4 * p + g, qt * P:(qt + 1) * P], o[r, 0:P], ACT.Copy
                                   ).then_inc(out_taken, 1)
                    return
                c = TP + (i - NP_) * TS
                for p in range(2):
                    for a in range(2):
                        r = slice(a * HD, (a + 1) * HD)
                        at = p * 64 + a * 32
                        last = act.activation(mix[r, 4 * p:4 * p + 4, c:c + TS],
                                              o[r, at:at + 32].rearrange("p (g t) -> p g t", t=TS), ACT.Copy)
                last.then_inc(out_taken, 1)

            for i in range(NI + LAG + 1):
                if 0 <= i + 1 - NP_ < NB:
                    take(-1 - (i + 1 - NP_))
                if LAG <= i < NI + LAG:
                    take(i - LAG)
                if i < NI:
                    exps(i)
                if i > LAG:
                    out(i - LAG - 1)


def mix_projection(L):
    nc = L.nc
    w = L.A["w_out"][0]
    gla_rows = w[0:1024].rearrange("(k p) n -> p k n", p=P)
    nsa_rows = w[1024:2048].rearrange("(h a g d) n -> a d h g n", h=2, a=2, g=G)
    q0, y0, sums0 = L.q, L.y, L.sums
    hi_made, lo_made = L.sem("mix_hi"), L.sem("mix_lo")
    NP = KD // 2
    scope = ExitStack()
    with scope:
        part = [L.proj[:, T_GR + a] for a in range(2)]
        with nc.Block() as block:
            @block.sync
            def _(sp):
                with sp.Fori(0, NP) as n:
                    for a in range(2):
                        sp.wait_ge(L.split[a], n + (q0 + 1))
                        cols = bass.ds(n * (2 * P) + a * P, P)
                        raw = L.raw[a][:].rearrange("p (k n) -> p k n", n=P)
                        sp.dma_start(raw[:, 0:8], gla_rows[:, :, cols]).then_inc(L.mixw_loaded[a], 16)
                        for h in range(2):
                            for half in range(2):
                                sp.dma_start(raw[half * HD:(half + 1) * HD, 8 + 4 * h:12 + 4 * h],
                                             nsa_rows[half, :, h, :, cols]).then_inc(L.mixw_loaded[a], 16)

            @block.scalar
            def _(act):
                for k in range(KD):
                    act.activation(L.xh[:, k], mix_tile(L, k), ACT.Copy).then_inc(hi_made, 1)
                with act.Fori(0, NP) as n:
                    take_parts(L, act, part, n + q0, n + y0, 1.0)

            @block.vector
            def _(dve):
                for k in range(KD):
                    dve.wait_ge(hi_made, k + 1)
                    dve.tensor_tensor(L.xl[:, k], mix_tile(L, k), L.xh[:, k].bitcast(F32), ALU.subtract
                                      ).then_inc(lo_made, 1)
                with dve.Fori(0, NP) as n:
                    split_pair(L, dve, n + q0, L.mixw_loaded, 5 * 16, n, KD)

            @block.tensor
            def _(pe):
                for a in range(2):
                    multiply_unit(L, pe, q0, a, KD, (L.xh, L.xl),
                                  (lambda pe, k: pe.wait_ge(lo_made, k + 1)) if a == 0 else None)
                with pe.Fori(1, NP) as n:
                    for a in range(2):
                        multiply_unit(L, pe, n + q0, a, KD, (L.xh, L.xl))

            @block.gpsimd
            def _(pool):
                add_last_parts(L, pool, part, q0, y0, sums0)
    L.q += NP
    L.y += NP
    L.sums += 1 + KD


def mix_tile(L, k):
    return L.proj[:, T_OG + k] if k < 8 else L.proj[:, T_NQ + k - 8]


def write_outputs(L, norm):
    nc, O, bank = L.nc, L.O, L.bank
    turned, taken, y_out = L.sem("y_turned"), L.sem("y_taken"), L.sem("y_out")
    ident = L.cst[:, K_ID:K_ID + P]
    rows = [P, P, T - TP]
    with ExitStack() as scope:
        y = [L.sb(f"y{t}", [P, D], scope=scope) for t in range(3)]
        with nc.Block() as block:
            @block.tensor
            def _(pe):
                norm.tensor(pe)
                for c in range(4):
                    norm.ready(pe, 4 * c + 3)
                    for t in range(3):
                        i = 3 * c + t
                        if i >= 4:
                            pe.wait_ge(taken, i - 3)
                        for j in range(4):
                            mm = pe.transpose(bank[4 + i % 4][0:rows[t], j * P:(j + 1) * P],
                                              L.xT[:, 4 * c + j, t * P:t * P + rows[t]], ident)
                        mm.then_inc(turned, 1)

            @block.scalar
            def _(act):
                norm.scalar(act)

            @block.vector
            def _(dve):
                norm.vector(dve, None)
                for i in range(12):
                    c, t = i // 3, i % 3
                    dve.wait_ge(turned, i + 1)
                    dve.tensor_copy(y[t][0:rows[t], c * 512:(c + 1) * 512], bank[4 + i % 4][0:rows[t], :]
                                    ).then_inc(taken, 1)

            @block.sync
            def _(sp):
                for half in range(2):
                    cols = slice(half * (D // 2), (half + 1) * (D // 2))
                    for t in range(3):
                        sp.wait_ge(taken, 6 * half + 4 + t)
                        dst = O["y_p"][0, t * P:(t + 1) * P, cols] if t < 2 else \
                            O["y_s"].rearrange("b t d -> (b t) d")[:, cols]
                        sp.dma_start(dst, y[t][0:rows[t], cols]).then_inc(y_out, 16)
                sp.wait_ge(y_out, 6 * 16)
                sp.wait_ge(L.stored, 16 * L.n_stored)


_INS = ["x_prompt", "x_sample", "cache_cmp_kv", "cache_slc_kv", "cache_win_kv", "state_gla", "page_table",
        "w_ffn1_in", "w_ffn1_out", "w_in", "w_gla_gate2", "b_gla_gate2", "gla_norm_g", "cmp_pos", "cmp_w1",
        "cmp_w2", "w_out", "w_ffn2_in", "w_ffn2_out", "ln_g", "ln_b"]
_OUTS = [("y_p", (1, TP, D)), ("y_s", (NB, TS, D)),
         ("cmp_p", (1, 1, TP, 2, KV, HD)), ("slc_p", (1, 1, TP, 2, KV, HD)), ("win_p", (1, 1, PAST, 2, KV, HD)),
         ("gla_p", (1, 1, GH, P, DV)),
         ("cmp_s", (1, NB, TS, 2, KV, HD)), ("slc_s", (1, NB, TS, 2, KV, HD)), ("win_s", (1, NB, PAST, 2, KV, HD)),
         ("gla_s", (1, NB, GH, P, DV))]


def kernel(**inputs):
    import concourse.bacc as bacc
    from concourse.bass_utils import run_bass_kernel_spmd

    nc = bacc.Bacc("TRN2", target_bir_lowering=False, num_devices=1)
    arrays = {name: np.ascontiguousarray(inputs[name]) for name in _INS}
    arrays["consts"], arrays["levels"] = constants(), level_masks()
    A = {n: nc.dram_tensor("in_" + n, a.shape, mybir.dt.from_np(a.dtype), kind="ExternalInput").ap()
         for n, a in arrays.items()}
    O = {n: nc.dram_tensor("out_" + n, shape, F32, kind="ExternalOutput").ap() for n, shape in _OUTS}
    build(nc, A, O)
    r = run_bass_kernel_spmd(nc, [{"in_" + n: a for n, a in arrays.items()}], core_ids=[0])
    return tuple(r.results[0]["out_" + n] for n, _ in _OUTS)
```
